# Optimizing a Trainium2 kernel written in Bass

```python
import functools
import jax, jax.numpy as jnp
from jax import lax
import numpy as np

D_MODEL = 2048
BATCH = 1
SEQ = 256
DEPTH = 1
DEC_BATCH = 8
DEC_SEQ = 4
PAST_LEN = 256
PAGE_SIZE = 128

RW_HEADS = 16
RW_HEAD = 64
RW_WIDTH = RW_HEADS * RW_HEAD
D_DECAY_LORA = 96
D_AAA_LORA = 96
D_GATE_LORA = 128
RW_COLS = 3 * RW_WIDTH + D_DECAY_LORA + D_AAA_LORA + D_GATE_LORA
GN_EPS = 64e-5
ATT_HEADS = 8
KV_HEADS = 2
HEAD_DIM = 128
ATT_WIDTH = ATT_HEADS * HEAD_DIM
KV_WIDTH = KV_HEADS * HEAD_DIM
IDX_HEADS = 16
IDX_DIM = 64
IDX_W_SCALE = (IDX_HEADS * IDX_DIM) ** -0.5
TOPK_MAX = 256
Q_BLOCK = 128
ROPE_THETA = 10000.0
ATT_COLS = ATT_WIDTH + 2 * KV_WIDTH + IDX_HEADS * IDX_DIM + IDX_DIM + IDX_HEADS
GATE_COLS = 2 * D_MODEL
IN_COLS = RW_COLS + ATT_COLS + GATE_COLS
D_FF = 5632
CONV_W = 3
RMS_EPS = 1e-6

kernel_name = "rwkv7_dsa_gated_hybrid_step"

def _split(z, sizes):
    return jnp.split(z, [int(o) for o in np.cumsum(sizes)[:-1]], axis=-1)

def rmsnorm(x, g):
    xf = x.astype(jnp.float32)
    y = xf * lax.rsqrt(jnp.mean(xf * xf, axis=-1, keepdims=True) + RMS_EPS)
    return (y * g.astype(jnp.float32)).astype(x.dtype)

def rope(x, pos):
    half = x.shape[-1] // 2
    inv_freq = 1.0 / (ROPE_THETA ** (jnp.arange(half, dtype=jnp.float32) / half))
    ang = pos.astype(jnp.float32)[:, None] * inv_freq[None, :]
    cos = jnp.cos(ang)[:, None, :]
    sin = jnp.sin(ang)[:, None, :]
    xf = x.astype(jnp.float32)
    x1, x2 = xf[..., :half], xf[..., half:]
    return jnp.concatenate([x1 * cos - x2 * sin, x2 * cos + x1 * sin], axis=-1).astype(x.dtype)

def rwkv7_mix(cols, shift_prev, wkv_prev, mu, w0, w2, a0, a2, g2, k_k, k_a, r_k, lnx_w, lnx_b):
    f32 = jnp.float32
    B, T, _ = cols.shape
    prev = jnp.concatenate([shift_prev[:, None, :].astype(cols.dtype), cols[:, :-1]], axis=1)
    m = cols + (prev - cols) * mu
    r, k, v, wl, al, gl = _split(m, (RW_WIDTH, RW_WIDTH, RW_WIDTH, D_DECAY_LORA, D_AAA_LORA, D_GATE_LORA))
    w_log = -jax.nn.softplus(-(w0 + jnp.tanh(wl) @ w2).astype(f32)) - 0.5
    decay = jnp.exp(-jnp.exp(w_log))
    a = jax.nn.sigmoid((a0 + al @ a2).astype(f32))
    g = jax.nn.sigmoid(gl) @ g2

    def heads(z):
        return z.astype(f32).reshape(B, T, RW_HEADS, RW_HEAD)

    kk = heads(k * k_k)
    kk = kk * lax.rsqrt(jnp.maximum(jnp.sum(kk * kk, axis=-1, keepdims=True), 1e-24))
    k = k.astype(f32) * (1.0 + (a - 1.0) * k_a.astype(f32))
    r_h, k_h, v_h, a_h, w_h = heads(r), heads(k), heads(v), heads(a), heads(decay)
    vec_a = -kk
    vec_b = kk * a_h

    def step(S, inp):
        r_t, w_t, k_t, v_t, a_t, b_t = inp
        sa = jnp.einsum('bhij,bhj->bhi', S, a_t)
        S = S * w_t[:, :, None, :] + sa[..., None] * b_t[:, :, None, :] + v_t[..., None] * k_t[:, :, None, :]
        return S, jnp.einsum('bhij,bhj->bhi', S, r_t)

    seq = tuple(jnp.moveaxis(z, 1, 0) for z in (r_h, w_h, k_h, v_h, vec_a, vec_b))
    S_fin, ys = lax.scan(step, wkv_prev.astype(f32), seq)
    y = jnp.moveaxis(ys, 0, 1)
    mean = jnp.mean(y, axis=-1, keepdims=True)
    var = jnp.mean(jnp.square(y - mean), axis=-1, keepdims=True)
    y = ((y - mean) * lax.rsqrt(var + GN_EPS)).reshape(B, T, RW_WIDTH) * lnx_w + lnx_b
    bonus = jnp.sum(r_h * k_h * r_k.astype(f32).reshape(RW_HEADS, RW_HEAD), axis=-1, keepdims=True) * v_h
    out = (y + bonus.reshape(B, T, RW_WIDTH)) * g
    return out.astype(cols.dtype), S_fin.astype(wkv_prev.dtype), cols[:, -1]

def index_select(qi, wi, ki_all, qpos, topk):
    f32 = jnp.float32
    dots = jnp.einsum('bqhd,bld->bqhl', qi.astype(f32), ki_all.astype(f32))
    score = jnp.einsum('bqh,bqhl->bql', wi.astype(f32), jax.nn.relu(dots))
    kpos = jnp.arange(ki_all.shape[1])
    causal = kpos[None, :] <= qpos[:, None]
    score = jnp.where(causal[None], score, -jnp.inf)
    _, idx = lax.top_k(score, topk)
    valid = idx <= qpos[None, :, None]
    return idx, valid

def sparse_attend(q, kg, vg, valid):
    f32 = jnp.float32
    B, Q = q.shape[:2]
    qg = q.reshape(B, Q, KV_HEADS, ATT_HEADS // KV_HEADS, HEAD_DIM).astype(f32)
    s = jnp.einsum('bqgrd,bqkgd->bqgrk', qg, kg.astype(f32)) * (HEAD_DIM ** -0.5)
    s = jnp.where(valid[:, :, None, None, :], s, -jnp.inf)
    p = jax.nn.softmax(s, axis=-1)
    o = jnp.einsum('bqgrk,bqkgd->bqgrd', p, vg.astype(f32))
    return o.reshape(B, Q, ATT_WIDTH).astype(q.dtype)

def dsa_prompt(q, k, v, qi, ki, wi):
    B, S = q.shape[:2]
    topk = min(TOPK_MAX, S // 4)
    nb = S // Q_BLOCK

    def blk(z):
        return jnp.moveaxis(z.reshape((B, nb, Q_BLOCK) + z.shape[2:]), 1, 0)

    def one(args):
        qb, qib, wb, t0 = args
        qpos = t0 + jnp.arange(Q_BLOCK)
        idx, valid = index_select(qib, wb, ki, qpos, topk)
        kg = jax.vmap(lambda f, i: f[i])(k, idx)
        vg = jax.vmap(lambda f, i: f[i])(v, idx)
        return sparse_attend(qb, kg, vg, valid)

    out = lax.map(one, (blk(q), blk(qi), blk(wi), jnp.arange(nb) * Q_BLOCK))
    return jnp.moveaxis(out, 0, 1).reshape(B, S, ATT_WIDTH)

def dsa_sample(q, k, v, qi, ki, wi, pos, cache_k, cache_v, cache_kidx, page_table):
    B, T = q.shape[:2]
    page = cache_k.shape[1]
    past_len = page_table.shape[1] * page
    topk = min(TOPK_MAX, (past_len + T) // 4)
    ki_past = cache_kidx[page_table].reshape(B, past_len, IDX_DIM).astype(ki.dtype)
    ki_all = jnp.concatenate([ki_past, ki], axis=1)
    idx, valid = index_select(qi, wi, ki_all, pos, topk)
    in_past = idx < past_len
    pidx = jnp.minimum(idx, past_len - 1)
    phys = jax.vmap(lambda pt, i: pt[i])(page_table, pidx // page) * page + pidx % page
    nidx = jnp.clip(idx - past_len, 0, T - 1)

    def gather(pool, new):
        g_past = pool.reshape(-1, KV_HEADS, HEAD_DIM)[phys].astype(new.dtype)
        g_new = jax.vmap(lambda n, i: n[i])(new, nidx)
        return jnp.where(in_past[..., None, None], g_past, g_new)

    return sparse_attend(q, gather(cache_k, k), gather(cache_v, v), valid)

def conv_glu(n, conv_prev, w_up, conv_w, conv_b, w_down):
    T = n.shape[1]
    gate, up = _split(n @ w_up, (D_FF, D_FF))
    ext = jnp.concatenate([conv_prev.astype(gate.dtype), gate], axis=1)
    c = conv_b + ext[:, 0:T] * conv_w[0]
    for j in range(1, CONV_W):
        c = c + ext[:, j:j + T] * conv_w[j]
    return (jax.nn.silu(c) * up) @ w_down, ext[:, T:]

def decoder_layer(x, pos, shift_prev, wkv_prev, conv_prev, attend, lw):
    (norm1, w_in, rw_mu, rw_w0, rw_w2, rw_a0, rw_a2, rw_g2, rw_k_k, rw_k_a, rw_r_k,
     rw_lnx_w, rw_lnx_b, p_rw, p_att, w_o, norm2, w_up, conv_w, conv_b, w_down) = lw
    B, T, _ = x.shape
    n = rmsnorm(x, norm1)
    c_rw, c_att, c_gate = _split(n @ w_in, (RW_COLS, ATT_COLS, GATE_COLS))
    o_rw, wkv_new, shift_new = rwkv7_mix(c_rw, shift_prev, wkv_prev, rw_mu, rw_w0, rw_w2, rw_a0, rw_a2,
                                         rw_g2, rw_k_k, rw_k_a, rw_r_k, rw_lnx_w, rw_lnx_b)
    q, k, v, qi, ki, wi = _split(c_att, (ATT_WIDTH, KV_WIDTH, KV_WIDTH, IDX_HEADS * IDX_DIM, IDX_DIM, IDX_HEADS))
    q = rope(q.reshape(B, T, ATT_HEADS, HEAD_DIM), pos)
    k = rope(k.reshape(B, T, KV_HEADS, HEAD_DIM), pos)
    v = v.reshape(B, T, KV_HEADS, HEAD_DIM)
    qi = rope(qi.reshape(B, T, IDX_HEADS, IDX_DIM), pos)
    ki = rope(ki[:, :, None, :], pos)[:, :, 0, :]
    o_att = attend(q, k, v, qi, ki, wi * IDX_W_SCALE)
    g_rw, g_att = _split(c_gate, (D_MODEL, D_MODEL))
    merged = jax.nn.sigmoid(g_rw) * (o_rw @ p_rw) + jax.nn.sigmoid(g_att) * (o_att @ p_att)
    h = x + merged @ w_o
    f, conv_new = conv_glu(rmsnorm(h, norm2), conv_prev, w_up, conv_w, conv_b, w_down)
    return h + f, (k, v, ki), wkv_new, shift_new, conv_new

def setup_inputs(seed: int = 0) -> dict:
    key = jax.random.key(seed)
    keys = jax.random.split(key, 64)
    counter = iter(range(64))
    f32 = jnp.float32

    def nk():
        return keys[next(counter)]

    def nrm(shape, scale):
        return scale * jax.random.normal(nk(), shape, f32)

    def unif(shape, lo, hi):
        return jax.random.uniform(nk(), shape, f32, lo, hi)

    n_pages = PAST_LEN // PAGE_SIZE
    n_used = DEC_BATCH * n_pages
    n_pool = n_used + max(1, n_used // 4)
    L = DEPTH
    inputs = {}
    inputs["x_prompt"] = nrm((BATCH, SEQ, D_MODEL), 1.0)
    inputs["x_sample"] = nrm((DEC_BATCH, DEC_SEQ, D_MODEL), 1.0)
    inputs["cache_k"] = nrm((L, n_pool, PAGE_SIZE, KV_HEADS, HEAD_DIM), 1.0)
    inputs["cache_v"] = nrm((L, n_pool, PAGE_SIZE, KV_HEADS, HEAD_DIM), 1.0)
    inputs["cache_kidx"] = nrm((L, n_pool, PAGE_SIZE, IDX_DIM), 1.0)
    inputs["state_wkv"] = nrm((L, DEC_BATCH, RW_HEADS, RW_HEAD, RW_HEAD), 0.5)
    inputs["state_shift"] = nrm((L, DEC_BATCH, RW_COLS), 1.0)
    inputs["state_conv"] = nrm((L, DEC_BATCH, CONV_W - 1, D_FF), 1.0)
    perm = jax.random.permutation(nk(), n_pool)
    inputs["page_table"] = perm[:n_used].reshape(DEC_BATCH, n_pages).astype(jnp.int32)
    inputs["norm1"] = 1.0 + nrm((L, D_MODEL), 0.05)
    inputs["w_in"] = nrm((L, D_MODEL, IN_COLS), D_MODEL ** -0.5)
    inputs["rw_mu"] = unif((L, RW_COLS), 0.0, 1.0)
    inputs["rw_w0"] = unif((L, RW_WIDTH), -3.0, 1.0)
    inputs["rw_w2"] = nrm((L, D_DECAY_LORA, RW_WIDTH), 0.1 * D_DECAY_LORA ** -0.5)
    inputs["rw_a0"] = nrm((L, RW_WIDTH), 0.1)
    inputs["rw_a2"] = nrm((L, D_AAA_LORA, RW_WIDTH), 0.5 * D_AAA_LORA ** -0.5)
    inputs["rw_g2"] = nrm((L, D_GATE_LORA, RW_WIDTH), D_GATE_LORA ** -0.5)
    inputs["rw_k_k"] = 0.85 + nrm((L, RW_WIDTH), 0.05)
    inputs["rw_k_a"] = 1.0 + nrm((L, RW_WIDTH), 0.05)
    inputs["rw_r_k"] = nrm((L, RW_WIDTH), 0.1)
    inputs["rw_lnx_w"] = 1.0 + nrm((L, RW_WIDTH), 0.05)
    inputs["rw_lnx_b"] = nrm((L, RW_WIDTH), 0.01)
    inputs["p_rw"] = nrm((L, RW_WIDTH, D_MODEL), RW_WIDTH ** -0.5)
    inputs["p_att"] = nrm((L, ATT_WIDTH, D_MODEL), ATT_WIDTH ** -0.5)
    inputs["w_o"] = nrm((L, D_MODEL, D_MODEL), D_MODEL ** -0.5)
    inputs["norm2"] = 1.0 + nrm((L, D_MODEL), 0.05)
    inputs["w_up"] = nrm((L, D_MODEL, 2 * D_FF), D_MODEL ** -0.5)
    inputs["conv_w"] = nrm((L, CONV_W, D_FF), CONV_W ** -0.5)
    inputs["conv_b"] = nrm((L, D_FF), 0.01)
    inputs["w_down"] = nrm((L, D_FF, D_MODEL), D_FF ** -0.5)
    inputs["norm_f"] = 1.0 + nrm((D_MODEL,), 0.05)
    return inputs

def reference(x_prompt, x_sample, cache_k, cache_v, cache_kidx, state_wkv, state_shift, state_conv,
              page_table, norm1, w_in, rw_mu, rw_w0, rw_w2, rw_a0, rw_a2, rw_g2, rw_k_k, rw_k_a,
              rw_r_k, rw_lnx_w, rw_lnx_b, p_rw, p_att, w_o, norm2, w_up, conv_w, conv_b, w_down, norm_f):
    B, S, _ = x_prompt.shape
    DB, DS, _ = x_sample.shape
    page = cache_k.shape[2]
    past_len = page_table.shape[1] * page
    pos_p = jnp.arange(S)
    pos_s = past_len + jnp.arange(DS)
    dt = x_prompt.dtype
    hp, hs = x_prompt, x_sample
    kp_l, vp_l, kip_l, ks_l, vs_l, kis_l = [], [], [], [], [], []
    wkvp_l, wkvs_l, shp_l, shs_l, cvp_l, cvs_l = [], [], [], [], [], []
    for l in range(DEPTH):
        lw = (norm1[l], w_in[l], rw_mu[l], rw_w0[l], rw_w2[l], rw_a0[l], rw_a2[l], rw_g2[l], rw_k_k[l],
              rw_k_a[l], rw_r_k[l], rw_lnx_w[l], rw_lnx_b[l], p_rw[l], p_att[l], w_o[l], norm2[l],
              w_up[l], conv_w[l], conv_b[l], w_down[l])
        hp, (kp, vp, kip), wkvp, shp, cvp = decoder_layer(
            hp, pos_p, jnp.zeros((B, RW_COLS), dt), jnp.zeros((B, RW_HEADS, RW_HEAD, RW_HEAD), dt),
            jnp.zeros((B, CONV_W - 1, D_FF), dt), dsa_prompt, lw)
        attend_s = functools.partial(dsa_sample, pos=pos_s, cache_k=cache_k[l], cache_v=cache_v[l],
                                     cache_kidx=cache_kidx[l], page_table=page_table)
        hs, (ksn, vsn, kisn), wkvs, shs, cvs = decoder_layer(
            hs, pos_s, state_shift[l], state_wkv[l], state_conv[l], attend_s, lw)
        kp_l.append(kp.reshape(B, S // page, page, KV_HEADS, HEAD_DIM))
        vp_l.append(vp.reshape(B, S // page, page, KV_HEADS, HEAD_DIM))
        kip_l.append(kip.reshape(B, S // page, page, IDX_DIM))
        ks_l.append(ksn)
        vs_l.append(vsn)
        kis_l.append(kisn)
        wkvp_l.append(wkvp)
        wkvs_l.append(wkvs)
        shp_l.append(shp)
        shs_l.append(shs)
        cvp_l.append(cvp)
        cvs_l.append(cvs)
    y_prompt = rmsnorm(hp, norm_f)
    y_sample = rmsnorm(hs, norm_f)
    return (y_prompt, y_sample, jnp.stack(kp_l), jnp.stack(vp_l), jnp.stack(kip_l), jnp.stack(ks_l),
            jnp.stack(vs_l), jnp.stack(kis_l), jnp.stack(wkvp_l), jnp.stack(wkvs_l), jnp.stack(shp_l),
            jnp.stack(shs_l), jnp.stack(cvp_l), jnp.stack(cvs_l))


_drawn_inputs = setup_inputs


def setup_inputs(seed=0):
    import zlib

    import numpy as np

    out = dict(_drawn_inputs(seed))
    spreads = {}
    factors = {'rw_w2': 5.568, 'rw_k_k': 12.338, 'rw_lnx_w': 4.263, 'rw_lnx_b': 30.533, 'conv_b': 8.0}
    for name, (base, spread) in spreads.items():
        noise = np.random.default_rng([zlib.crc32(name.encode()), seed]).standard_normal(out[name].shape)
        drawn = base * np.exp(spread * noise) if base else spread * noise
        out[name] = __import__('jax').numpy.asarray(drawn.astype(out[name].dtype))
    for name, factor in factors.items():
        out[name] = (out[name] * factor).astype(out[name].dtype)
    return out
```

```python
from contextlib import ExitStack

import numpy as np
import concourse.bass as bass
from concourse import mybir

F32 = mybir.dt.float32
F32R = mybir.dt.float32r
I32 = mybir.dt.int32
ALU = mybir.AluOpType
ACT = mybir.ActivationFunctionType
AX = mybir.AxisListType

P = 128
D_MODEL = 2048
SEQ = 256
DB, DS = 8, 4
NS = DB * DS
N = SEQ + NS
PAST = 256
PAGE = 128
HEADS_RW, HD = 16, 64
RW_WIDTH = HEADS_RW * HD
LORA_W, LORA_A, LORA_G = 96, 96, 128
RW_COLS = 3 * RW_WIDTH + LORA_W + LORA_A + LORA_G
GN_EPS = 64e-5
AH, KVH, HDIM = 8, 2, 128
IH, ID = 16, 64
IDX_SCALE = (IH * ID) ** -0.5
TOPK_P = min(256, SEQ // 4)
TOPK_S = min(256, (PAST + DS) // 4)
ROPE_THETA = 10000.0
D_FF = 5632
RMS_EPS = 1e-6
DECAY_SCALE = -float(np.exp(-0.5))

KT = D_MODEL // P
FT = D_FF // P
RW_T = 27
ATT_T = 21
PAIRS = RW_WIDTH // P
E = 1 + SEQ + DB * (1 + DS)
TE = E - 1
T_LW, T_LA, T_LG = 24, 25, 26
T_Q, T_K, T_V, T_QI, T_KI = 27, 35, 37, 39, 47
WI_ROW = 96
CH = 64
NCH = SEQ // CH
KEYS_S = PAST + DS
N_POOL = 20
BIGNEG = -1e30
MARK = -3e38
DK = 11
DU = FT // DK
GE = 2 + SEQ + DB * (2 + DS)
CE = GE - 2

U_IN = 0
U_GATE = U_IN + RW_T + ATT_T
U_P = U_GATE + 2 * KT
U_O = U_P + KT
U_UP = U_O + KT
U_DOWN = U_UP + 2 * FT


def constants():
    c = {}
    i = np.arange(P)
    eye = np.eye(P, dtype=np.float32)

    def blk(n):
        return (i[:, None] // n == i[None, :] // n)

    up, upi, low = i[:, None] < i[None, :], i[:, None] <= i[None, :], i[:, None] > i[None, :]
    c["ident"] = eye
    c["mean_ones"] = np.full((P, P), 1.0 / D_MODEL)
    c["head_ones"] = blk(HD)
    c["tri_incl"] = (blk(CH) & upi) * (0.5 * DECAY_SCALE)
    c["tri_excl"] = (blk(CH) & up) * (0.5 * DECAY_SCALE)
    c["m_ab"] = np.concatenate([blk(CH) & up, blk(CH) & upi], 1)
    c["m16u"] = blk(16) & up
    c["m16l"] = blk(16) & low
    c["m32l"] = blk(32) & ~blk(16) & low
    c["m64l"] = blk(64) & ~blk(32) & low
    s = slice(0, NS)
    b4 = blk(DS)
    small = np.zeros((P, 4 * NS + NS + DB))
    small[s, 0:NS] = (b4 & up)[s, s]
    small[s, NS:2 * NS] = (b4 & upi)[s, s]
    small[s, 2 * NS:3 * NS] = (b4 & low)[s, s]
    small[s, 3 * NS:4 * NS] = (b4 & upi)[s, s] * (0.5 * DECAY_SCALE)
    small[s, 4 * NS:5 * NS] = (b4 & up)[s, s] * (0.5 * DECAY_SCALE)
    small[s, 5 * NS:] = np.arange(NS)[:, None] // DS == np.arange(DB)[None, :]
    c["small"] = small
    main = np.concatenate([np.asarray(v, np.float32) for v in c.values()], 1)
    at, o = {}, 0
    for k, v in c.items():
        at[k] = (o, v.shape[1])
        o += v.shape[1]

    a = {}
    rot = np.zeros((P, P))
    for m in range(P):
        rot[(m + 64) % P, m] = -1.0 if m < 64 else 1.0
    a["rot_head"] = rot
    rot = np.zeros((P, P))
    for m in range(P):
        base, r = m // 64 * 64, m % 64
        rot[base + (r + 32) % 64, m] = -1.0 if r < 32 else 1.0
    a["rot_idx"] = rot
    pos = np.zeros(TE, np.float32)
    pos[:SEQ] = np.arange(SEQ)
    for b in range(DB):
        for t in range(DS):
            pos[SEQ + 5 * b + 1 + t] = PAST + t
    for name, half in (("head", HDIM // 2), ("idx", ID // 2)):
        inv = (1.0 / (np.float32(ROPE_THETA) ** (np.arange(half, dtype=np.float32) / np.float32(half)))).astype(np.float32)
        ang = (pos[None, :] * inv[i % half][:, None]).astype(np.float32).astype(np.float64)
        a["cos_" + name] = np.cos(ang)
        a["sin_" + name] = np.sin(ang)
    row = np.arange(P)
    r_par, r_b2, r_h, r_t = row // 64, row // 32 % 2, row // 4 % 8, row % 4
    sel = np.zeros((P, P))
    sel[WI_ROW + 2 * r_h + r_par, row] = IDX_SCALE
    a["sel_head"] = sel
    q = np.arange(NS)
    a["m_query"] = np.stack([(q[None, :] == (2 * c4 + r_b2[:, None]) * DS + r_t[:, None]) for c4 in range(4)], 1).reshape(P, -1)
    selq = np.zeros((P, 2, P))
    for half in range(2):
        selq[(4 * half + row // 32) * DS + row % 4, half, row] = 1.0
    a["sel_query"] = selq.reshape(P, -1)
    k = np.arange(SEQ)
    a["causal"] = np.stack([np.where(k[None, :] <= (qt * P + i)[:, None], 0.0, BIGNEG) for qt in range(2)], 1).reshape(P, -1)
    ks = np.arange(KEYS_S)
    a["causal_s"] = np.where(ks[None, :] <= PAST + (i % DS)[:, None], 0.0, BIGNEG)
    att = np.concatenate([np.asarray(v, np.float32) for v in a.values()], 1)
    ata, o = {}, 0
    for kx, v in a.items():
        ata[kx] = (o, v.shape[1])
        o += v.shape[1]
    return main, at, att, ata


MAIN_C, MAIN_AT, ATT_C, ATT_AT = constants()

ROPE_TILES = [T_KI] + [T_QI + i for i in range(8)] + [T_K, T_K + 1] + [T_Q + i for i in range(8)]
PROMPT_STEPS = [(0, 0), (0, 1), (1, 0), (1, 1)]
PAIR_STEPS = 20
UP_STEPS = 6

(PR_MUR, PR_MUK, PR_MUV, PR_A0H, PR_KK, PR_KA, PR_RK, PR_LW, PR_LB, NPRM) = range(10)



class Steps:

    def __init__(self, eng, sem):
        self.eng, self.sem, self.n, self.base = eng, sem, 0, 0

    def mark(self, ins):
        ins.then_inc(self.sem, 1)
        self.n += 1

    def sync(self):
        self.eng.wait_ge(self.sem, self.base + self.n)

    def done(self, ins):
        self.mark(ins)
        self.sync()

    def repeat(self, count, per, body, first=0):
        start = self.base + self.n
        with self.eng.Fori(first, count) as i:
            self.base, self.n = i * per + (start - first * per), 0
            body(i)
            assert self.n == per, (self.n, per)
        self.base, self.n = start + (count - first) * per, 0


def rows_of(x):
    return x.rearrange("o p f -> (o p) f")


def step(x):
    return x.rearrange("p o f -> p (o f)")


def samples(x, width):
    return x.rearrange("p (b f) -> p b f", f=width)[:, :, width - DS:width]


def by_request(x):
    return x.rearrange("p (b t) -> p b t", t=DS)


def spread(x, axis, shape):
    return x.unsqueeze(axis).broadcast_to(shape)


def build(nc, a, o):
    start = (nc.sbuf_base + 31) // 32 * 32
    end = nc.sbuf_usable_end // 32 * 32

    def size_of(shape):
        return (4 * int(np.prod(shape[1:])) + 31) // 32 * 32

    def region(offset):
        def take(name, shape, dt=F32):
            t = nc.alloc_sbuf_tensor_at(name, shape, dt, offset=take.at)
            take.at += size_of(shape)
            assert take.at <= end, (name, take.at - end)
            return t
        take.at = offset
        return take

    m = region(start)
    MC = m("main_consts", [P, MAIN_C.shape[1]])
    PRM_ALL = m("pair_params_all", [P, PAIRS, NPRM])
    LMU = m("lora_mu", [P, 3])
    NORMS = m("norm_gains", [P, 3, KT])
    CONVP = m("conv_params", [P, FT, 4])
    PTAB = m("page_table", [1, 2 * DB], I32)
    WRAW = m("w_raw", [P, 2, KT, P])
    WHI = m("w_hi", [P, 2, KT, P], F32R)
    WLO = m("w_lo", [P, 2, KT, P], F32R)
    xn_at = m.at
    XN = m("x_split", [P, 2, KT, N], F32R)
    big = m.at

    m = region(big)
    XRAW = m("x_raw", [P, KT, N])
    SQ = m("squares", [P, 2, N])
    RSTD = m("rstd", [P, N])
    m = region(big)
    COLS = m("cols", [P, RW_T + ATT_T, E])
    AC = m("att_consts", [P, ATT_C.shape[1]])
    SHP = m("shift_prev", [P, RW_T, DB])
    SHO = m("shift_out", [P, RW_T, 1 + DB])
    RT = m("rope_tmp", [P, 2, TE])
    KC = m("k_cache", [P, 4, KVH, PAST])
    VC = m("v_cache", [P, 4, 2, KVH * HDIM])
    KIC = m("ki_cache", [P, DB, PAST])
    BIASP = m("bias_prompt", [P, 2, SEQ])
    BIASS = m("bias_sample", [NS, KEYS_S])
    VNEW = m("v_new", [DS, 4, KVH * HDIM])
    QIS = m("qi_sample", [P, DB, 8, DS])
    WM = m("w_mix", [P, 4, NS])
    WI = m("w_idx", [P, 2, IH])
    M8 = m("max8", [P, 8])
    ST8 = m("softmax_stats", [P, 16])
    QZ = m("q_grouped", [P, KVH, 4, AH, DS])
    sel_at = m.at
    ACC = m("scores", [P, 2, SEQ])
    ACS = m("scores_s", [NS, KEYS_S])
    RELU = m("relu", [P, 2, 2 * SEQ + 16])
    m = region(sel_at)
    PROB = m("prob", [P, 4 * SEQ])
    PRT = m("prob_t", [P, 2 * 4 * P])
    VTOK = m("v_tok", [P, 2, KVH * HDIM])
    m = region(big + (4 * (RW_T + 8) * E + 31) // 32 * 32)
    GATES = m("gates", [P, 2 * KT, N])
    r0 = m.at
    m = region(r0)
    DIFF = m("diff", [P, 3, TE])
    RKV = m("rkv", [P, 3, N])
    KKN = m("kk_unit", [P, N])
    AG = m("a_gate", [P, N])
    KP = m("k_mixed", [P, N])
    SQK = m("squares_k", [P, N])
    LDT = m("decay_tok", [P, 3, P])
    r_end = m.at
    m = region(r0)
    PEXP = m("decay_exp", [P, 3, N])
    m = region(r0)
    U1 = m("u1", [P, 4, P])
    L1 = m("l1", [P, 4, P])
    U2 = m("u2", [P, 4, P])
    L2 = m("l2", [P, 4, P])
    ML = m("m_low", [P, 4, P])
    TT = m("t_inv", [P, 4, P])
    m = region(r0)
    UM = m("u_by_request", [NS, 2, DB * HD])
    VM = m("v_by_request", [NS, 2, DB * HD])
    YS = m("y", [P, N])
    YQ = m("y_sq", [P, N])
    m = region(r_end)
    AR = m("ar", [P, 2, 2, P])
    ARS = m("ar_s", [P, 2, NS])
    BT = m("b_t", [P, N])
    KTL = m("k_t", [P, N])
    TOK = m("tok", [P, 2, 3 * P])
    TOKS = m("tok_s", [NS, 3 * P])
    MB = m("mat_b", [P, 2, 2, 2 * P])
    MK = m("mat_k", [P, 2, 2, 2 * P])
    LORA = m("lora", [P, 3, P])
    SIN = m("state_s", [P, DB, HD])
    STT = m("state", [P, P])
    STP = m("state_decayed", [P, P])
    RR = m("rhs", [P, P])
    UU = m("u", [P, P])
    MBS = m("mat_b_s", [NS, 2, 2 * NS])
    MKS = m("mat_k_s", [NS, 2, 2 * NS])
    MLS = m("m_low_s", [NS, 2, NS])
    TS = m("t_inv_s", [NS, 2, NS])
    L2S = m("l2_s", [NS, 2, NS])
    SPR = m("state_prod", [P, 2, NS])
    RS = m("rhs_s", [NS, P])
    US = m("u_s", [NS, P])
    PRM = m("pair_params", [P, NPRM])
    PC = m("chunk_decay", [P, NCH + DB])
    m = region(big)
    XM = m("merged_split", [P, 2, KT, N], F32R)
    m = region(r0)
    H = m("h", [P, KT, N])
    MG = m("merge_tmp", [P, 4, N])
    HSQ = m("h_squares", [P, 2, N])
    HRSTD = m("h_rstd", [P, N])
    m = region(big)
    XF = m("act_split", [P, 2, FT, N], F32R)
    CPREV = m("conv_prev", [P, FT, 2 * DB])
    COUT = m("conv_out", [P, FT, 2 + 2 * DB])
    GX = m("gate_ext", [P, 2, GE])
    CV = m("conv", [P, 2, 2, CE])
    m = region(xn_at)
    H2 = m("h2", [P, KT, N])
    YO = m("y_out", [P, KT, N])
    m = region(big + size_of([P, 2 * FT, N]))
    FSQ = m("f_squares", [P, 2, N])
    FRSTD = m("f_rstd", [P, N])

    def cst(name, rows=P):
        off, w = MAIN_AT[name]
        return MC[0:rows, off:off + w]

    def acst(name, rows=P):
        off, w = ATT_AT[name]
        return AC[0:rows, off:off + w]

    ident, mean_ones, head_ones = cst("ident"), cst("mean_ones"), cst("head_ones")
    tri_incl, tri_excl = cst("tri_incl"), cst("tri_excl")
    m_ab, m16u, m16l, m32l, m64l = (cst(x) for x in ("m_ab", "m16u", "m16l", "m32l", "m64l"))
    small = cst("small", NS)
    ms_ab, ms_l = small[:, 0:2 * NS], small[:, 2 * NS:3 * NS]
    tris_incl, tris_excl = small[:, 3 * NS:4 * NS], small[:, 4 * NS:5 * NS]
    ms_req = small[:, 5 * NS:5 * NS + DB]

    h_spill = nc.dram_tensor("h_spill", [P, KT * N], F32, kind="Internal").ap()

    with ExitStack() as ctx:
        BK = [ctx.enter_context(nc.psum_tensor(f"bank{i}", [P, 512], F32)) for i in range(8)]
        sems = {}

        def sem(name):
            if name not in sems:
                sems[name] = ctx.enter_context(nc.semaphore(name))
            return sems[name]

        block = ctx.enter_context(nc.Block())
        mm, tr = nc.tensor.matmul, nc.tensor.transpose
        actv = nc.scalar.activation
        V = nc.vector
        FORI_IN, FORI_UP, FORI_P = (RW_T + ATT_T) // 4, FT // 2, KT // 4
        N_UNITS = U_DOWN + KT * DU
        OUT_DMAS = [0]

        colsv = COLS[:].rearrange("p (g j) e -> p g j e", j=4)
        rwv = COLS[:, 0:24, :].rearrange("p (j h) e -> p j h e", j=3)
        gatesv = GATES[:].rearrange("p (g j) n -> p g j n", j=4)

        @block.sync
        def _(sp):
            sp.dma_start(XRAW[:], a["x"]).then_inc(sem("x_in"), 16)
            sp.dma_start(MC[:], a["main_c"]).then_inc(sem("main_c_in"), 16)
            sp.dma_start(NORMS[:], a["norms"]).then_inc(sem("norms_in"), 16)

            def load(n, slot, src, kt=KT):
                if not isinstance(n, int) or n >= 2:
                    sp.wait_ge(sem("w_split"), n - 1)
                dst = WRAW[:, slot, 0:kt, :].rearrange("p k c -> p (k c)")
                sp.dma_start(dst, src).then_inc(sem(f"w_in{slot}"), 16)

            def section(name, u0, count, per, kt=KT):
                src = a[name].rearrange("(g j) p f -> g j p f", j=per)
                def body(g):
                    for j in range(per):
                        one = src[g, j] if isinstance(g, int) else rows_of(src[bass.ds(g, 1), j])
                        load(g * per + (u0 + j), j % 2, one, kt)
                if u0 == 0:
                    body(0)
                with sp.Fori(1 if u0 == 0 else 0, count // per) as g:
                    body(g)

            section("w_in", U_IN, RW_T + ATT_T, 4)
            section("w_gate", U_GATE, 2 * KT, 4)
            section("w_p", U_P, KT, 4)
            section("w_o", U_O, KT, 4)
            section("w_up", U_UP, 2 * FT, 4)
            section("w_down", U_DOWN, KT * DU, 8, DK)
            sp.wait_ge(sem("att_out"), 16 * 3)
            sp.wait_ge(sem("sout_done"), 16 * PAIRS)
            sp.wait_ge(sem("stout_done"), 32 * PAIRS)
            sp.wait_ge(sem("out_done"), 16 * 6)
        def settle(eng):
            eng.wait_ge(sem("x_split"), 4)

        def mix_scores(pe, c):
            pe.wait_ge(sem("relu"), 16 + c + 1)
            mm(BK[6][0:NS, 0:KEYS_S], WM[:, c, :], RELU[:, c % 2, 0:KEYS_S], start=c == 0,
               stop=c == 3).then_inc(sem("mixed"), 1)

        def n_ge2(n):
            return not isinstance(n, int) or n >= 2

        def split_lo(eng, n, slot, kt=KT):
            eng.wait_ge(sem("w_hi"), n + 1)
            eng.tensor_tensor(WLO[:, slot, 0:kt], WRAW[:, slot, 0:kt], WHI[:, slot, 0:kt].bitcast(F32),
                             ALU.subtract).then_inc(sem("w_split"), 1)

        def split_hi(act, n, slot, kt=KT):
            act.wait_ge(sem(f"w_in{slot}"), unit_landed(n, slot))
            if n_ge2(n):
                act.wait_ge(sem("unit_done"), n - 1)
            actv(WHI[:, slot, 0:kt], WRAW[:, slot, 0:kt], ACT.Copy).then_inc(sem("w_hi"), 1)

        def unit_landed(n, slot):
            return (n - slot) * 8 + 16

        @block.tensor
        def _(pe):
            def norm_sum(k, squares):
                for t in range(KT):
                    pe.wait_ge(sem("norm_sq"), KT * k + t + 1)
                    mm(BK[2][:, 0:N], mean_ones, squares[:, t % 2, :], start=t == 0,
                       stop=t == KT - 1).then_inc(sem("norm_sq_used"), 1)

            def blocks(n, slot, ks, out, rhs, first=True, last=True, kt=KT):
                for k in ks:
                    hi, lo, w, wl = rhs[:, 0, k0(k, rhs)], rhs[:, 1, k0(k, rhs)], WHI[:, slot, k], WLO[:, slot, k]
                    mm(out, wl, hi, start=first and k == ks[0], stop=False, skip_group_check=True)
                    mm(out, w, lo, start=False, stop=False, skip_group_check=True)
                    ins = mm(out, w, hi, start=False, stop=last and k == ks[-1], skip_group_check=True)
                return ins

            koff = [0]

            def k0(k, rhs):
                return k + koff[0]

            pe.wait_ge(sem("main_c_in"), 16)
            norm_sum(0, SQ)
            pe.wait_ge(sem("x_split"), 4)

            def in_units(g):
                for j in range(4):
                    n = g * 4 + j
                    pe.wait_ge(sem("w_split"), n + 1)
                    if n_ge2(n):
                        pe.wait_ge(sem("unit_out"), n - 1)
                    blocks(n, j % 2, range(KT), BK[j % 2][:, 0:N], XN).then_inc(sem("unit_done"), 1)
            in_units(0)
            with pe.Fori(1, FORI_IN) as g:
                in_units(g)

            pe.wait_ge(sem("att_c_in"), 16)
            pe.wait_ge(sem("unit_out"), U_GATE)
            pe.wait_ge(sem("slots"), 1)
            for i, t in enumerate(ROPE_TILES):
                if i >= 2:
                    pe.wait_ge(sem("rot_used"), i - 1)
                rot = acst("rot_head") if t < T_V else acst("rot_idx")
                mm(BK[2 + i % 2][:, 0:TE], rot, COLS[:, t, 1:E], start=True, stop=True).then_inc(sem("rot"), 1)
            for qt in range(2):
                ins = tr(BK[4][:, qt * P:(qt + 1) * P], COLS[:, T_LW, 1 + qt * P:1 + (qt + 1) * P], ident)
            ins.then_inc(sem("wi_t"), 1)
            mm(BK[5][:, 0:NS], acst("sel_head"), samples(COLS[:, T_LW, 1 + SEQ:E], 5), start=True,
               stop=True).then_inc(sem("wi_rows"), 1)
            pe.wait_ge(sem("roped"), len(ROPE_TILES))
            for qt in range(2):
                for i in range(8):
                    n = qt * 8 + i
                    if n == 1:
                        pe.wait_ge(sem("wi_sb"), 1)
                        pe.wait_ge(sem("w_mix"), 1)
                    if n >= 2:
                        pe.wait_ge(sem("relu"), n - 1)
                    for par in range(2):
                        r = slice(64 * par, 64 * par + 64)
                        ins = mm(BK[2 + n % 2 * 2 + par][:, 0:SEQ], COLS[r, T_QI + i, qt * P:(qt + 1) * P],
                                 COLS[r, T_KI, 0:SEQ], start=True, stop=True)
                    ins.then_inc(sem("dots"), 1)
            pe.wait_ge(sem("ki_in"), 16 * 2 * 2 * DB)
            for c in range(4):
                n = 16 + c
                pe.wait_ge(sem("relu"), n - 1)
                for b2 in range(2):
                    b = 2 * c + b2
                    for par in range(2):
                        r = slice(64 * par, 64 * par + 64)
                        out = BK[2 + n % 2 * 2][64 * par + 32 * b2:64 * par + 32 * b2 + 32]
                        q = QIS[r, b].rearrange("p h t -> p (h t)")
                        mm(out[:, 0:PAST], q, KIC[r, b, :], start=True, stop=True)
                        ins = mm(out[:, PAST:KEYS_S], q, COLS[r, T_KI, SEQ + DS * b:SEQ + DS * b + DS],
                                 start=True, stop=True)
                ins.then_inc(sem("dots"), 1)
                if c >= 1:
                    mix_scores(pe, c - 1)
            mix_scores(pe, 3)
            pe.wait_ge(sem("v_compact"), 1)
            pe.wait_ge(sem("relu"), 20)
            for kc in range(2):
                for g in range(KVH):
                    ins = tr(BK[4][:, (kc * KVH + g) * P:(kc * KVH + g + 1) * P], RT[:, g, kc * P:(kc + 1) * P], ident)
            ins.then_inc(sem("v_t"), 1)
            for n, (qt, g) in enumerate(PROMPT_STEPS):
                pe.wait_ge(sem("bias_ready"), 1)
                if n >= 1:
                    pe.wait_ge(sem("s_used"), n)
                for r in range(4):
                    ins = mm(BK[2 + r // 2][:, r % 2 * SEQ:(r % 2 + 1) * SEQ],
                             COLS[:, T_Q + 4 * g + r, qt * P:(qt + 1) * P], COLS[:, T_K + g, 0:SEQ],
                             start=True, stop=True)
                ins.then_inc(sem("s_mm"), 1)
                pe.wait_ge(sem("prob"), n + 1)
                pe.wait_ge(sem("v_tok"), 1)
                for kc in range(2):
                    for r in range(4):
                        ins = tr(BK[4 + kc][:, r * P:(r + 1) * P], PROB[:, r * SEQ + kc * P:r * SEQ + (kc + 1) * P], ident)
                ins.then_inc(sem("p_t"), 1)
                pe.wait_ge(sem("p_sb"), n + 1)
                pe.wait_ge(sem("p_sb2"), n + 1)
                for kc in range(2):
                    ins = mm(BK[6][:], VTOK[:, kc, g * P:(g + 1) * P], PRT[:, kc * 512:(kc + 1) * 512],
                             start=kc == 0, stop=kc == 1)
                ins.then_inc(sem("pv"), 1)
            for half in range(2):
                n = 4 + half
                pe.wait_ge(sem("q_grouped"), half + 1)
                pe.wait_ge(sem("kv_in"), 16 * 32 * (half + 1))
                if half:
                    pe.wait_ge(sem("exp"), 5)
                mm(BK[7][:, 0:KEYS_S], acst("sel_query", NS)[:, half * P:(half + 1) * P], BIASS[:], start=True, stop=False,
                   skip_group_check=True)
                for b in range(4):
                    out = BK[7][32 * b:32 * b + 32]
                    for g in range(KVH):
                        q = QZ[:, g, b].rearrange("p h t -> p (h t)")
                        c0 = SEQ + DS * (4 * half + b)
                        mm(out[:, 0:PAST], q, KC[:, b, g, :], start=False, stop=False, skip_group_check=True)
                        ins = mm(out[:, PAST:KEYS_S], q, COLS[:, T_K + g, c0:c0 + DS], start=False, stop=g == 1,
                                 skip_group_check=True)
                ins.then_inc(sem("s_mm"), 1)
                if half == 0:
                    pe.wait_ge(sem("s_used"), 4)
                for b in range(4):
                    for g in range(KVH):
                        c0 = SEQ + DS * (4 * half + b)
                        i = b * KVH + g
                        ins = tr(BK[2 + i // 4][0:DS, i % 4 * P:(i % 4 + 1) * P], RT[:, g, c0:c0 + DS], ident)
                ins.then_inc(sem("v_new_t"), 1)
                pe.wait_ge(sem("prob"), n + 1)
                pe.wait_ge(sem("p_sb"), n)
                tr(BK[4][:, 0:P], PROB[:, 0:P], ident)
                tr(BK[4][:, P:2 * P], PROB[:, P:2 * P], ident)
                tr(BK[4][0:DS, 2 * P:3 * P], PROB[:, 2 * P:KEYS_S], ident).then_inc(sem("p_t"), 1)
                pe.wait_ge(sem("p_sb"), n + 1)
                pe.wait_ge(sem("v_new"), half + 1)
                pe.wait_ge(sem("o_sb"), n)
                for b in range(4):
                    for g in range(KVH):
                        out = BK[6][:, (b * KVH + g) * 16:(b * KVH + g + 1) * 16]
                        c0 = b * 32 + g * 16
                        for kc in range(2):
                            mm(out, VC[:, b, kc, g * P:(g + 1) * P], PRT[:, kc * P + c0:kc * P + c0 + 16],
                               start=kc == 0, stop=False)
                        ins = mm(out, VNEW[:, b, g * P:(g + 1) * P], PRT[0:DS, 2 * P + c0:2 * P + c0 + 16],
                                 start=False, stop=True)
                ins.then_inc(sem("pv"), 1)

            def pair(it):
                pos = [0]

                def fill(count):
                    while count:
                        j, k = divmod(pos[0], KT)
                        todo = min(count, KT - k)
                        n = it * 4 + (U_GATE + j)
                        if k == 0:
                            pe.wait_ge(sem("w_split"), n + 1)
                            pe.wait_ge(sem("unit_out"), n - 1)
                        ins = blocks(n, j % 2, range(k, k + todo), BK[j % 2][:, 0:N], XN, k == 0, k + todo == KT)
                        if k + todo == KT:
                            ins.then_inc(sem("unit_done"), 1)
                        pos[0] += todo
                        count -= todo

                v = it + 1
                halves = [slice(0, 64), slice(64, 128)]
                pe.wait_ge(sem("pair_done"), v)
                pe.wait_ge(sem("lora_in"), v * 16)
                lw = COLS[:, T_LW]
                for tt in range(2):
                    mm(BK[2][:, tt * P:(tt + 1) * P], lw[0:97, tt * P:(tt + 1) * P], LORA[0:97, 0, :], start=True, stop=True)
                mm(BK[2][0:NS, 2 * P:3 * P], lw[0:97, SEQ:N], LORA[0:97, 0, :], start=True,
                   stop=True).then_inc(sem("z_mm"), 1)
                mm(BK[3][:, 0:N], LORA[0:LORA_A, 1, :], COLS[0:LORA_A, T_LA, 0:N], start=True,
                   stop=True).then_inc(sem("a_mm"), 1)
                mm(BK[6][:, 0:N], LORA[:, 2, :], COLS[:, T_LG, 0:N], start=True, stop=True).then_inc(sem("g_mm"), 1)
                pe.wait_ge(sem("kk_sq"), v)
                mm(BK[4][:, 0:N], head_ones, SQK[:], start=True, stop=True).then_inc(sem("kk_sum"), 1)
                fill(6)
                pe.wait_ge(sem("decay_tok"), v)
                pe.wait_ge(sem("g_sb"), v)
                for bank, tri, tris in ((5, tri_incl, tris_incl), (6, tri_excl, tris_excl)):
                    for tt in range(2):
                        mm(BK[bank][:, tt * P:(tt + 1) * P], LDT[:, tt, :], tri, start=True, stop=True)
                    ins = mm(BK[bank][:, SEQ:N], LDT[0:NS, 2, :], tris, start=True, stop=True)
                ins.then_inc(sem("log_decay"), 1)
                fill(6)
                pe.wait_ge(sem("rkr"), v)
                mm(BK[4][:, 0:N], head_ones, SQK[:], start=True, stop=True).then_inc(sem("bonus_mm"), 1)
                pe.wait_ge(sem("ar_ready"), v)
                for w, src in enumerate((BT, KTL, RKV[:, 2, :])):
                    for tt in range(2):
                        tr(BK[2 + tt][:, w * P:(w + 1) * P], src[:, tt * P:(tt + 1) * P], ident)
                    ins = tr(BK[7][0:NS, w * P:(w + 1) * P], src[:, SEQ:N], ident)
                ins.then_inc(sem("tok_mm"), 1)
                for tt in range(2):
                    for e, h in enumerate(halves):
                        ins = mm(BK[5 + e][:, tt * SEQ:(tt + 1) * SEQ], BT[h, tt * P:(tt + 1) * P],
                                 AR[h, tt].rearrange("p x n -> p (x n)"), start=True, stop=True)
                ins.then_inc(sem("b_mm"), 1)
                fill(4)
                pe.wait_ge(sem("bonus"), v)
                pe.wait_ge(sem("tok_sb"), v)

                def half_mm(e, h):
                    for tt in range(2):
                        mm(BK[4][:, (tt * 2 + e) * P:(tt * 2 + e + 1) * P], AR[h, tt, 0, :], BT[h, tt * P:(tt + 1) * P],
                           start=True, stop=True)
                    ars = ARS[h].rearrange("p x n -> p (x n)")
                    mm(BK[7][0:NS, e * 64:e * 64 + 64], BT[h, SEQ:N], ars, start=True, stop=True)
                    mm(BK[7][0:NS, 128 + e * 64:192 + e * 64], KTL[h, SEQ:N], ars, start=True, stop=True)
                    return mm(BK[7][0:NS, 256 + e * 32:288 + e * 32], ARS[h, 0, :], BT[h, SEQ:N], start=True, stop=True)
                half_mm(0, halves[0]).then_inc(sem("head0_mm"), 1)
                for tt in range(2):
                    for e, h in enumerate(halves):
                        mm(BK[2 + e][:, tt * SEQ:(tt + 1) * SEQ], KTL[h, tt * P:(tt + 1) * P],
                           AR[h, tt].rearrange("p x n -> p (x n)"), start=True, stop=True)
                pe.wait_ge(sem("head0_mm"), v)
                ins = half_mm(1, halves[1])
                ins.then_inc(sem("k_mm"), 1)
                fill(4)

                def four(bank, lhs, rhs):
                    for u in range(4):
                        ins = mm(BK[bank][:, u * P:(u + 1) * P], lhs[:, u], rhs[:, u], start=True, stop=True)
                    return ins

                settle(pe)
                pe.wait_ge(sem("mats"), v)
                four(5, L1, U1)
                four(6, U1, L1).then_inc(sem("inv_mm"), 1)
                for e in range(2):
                    ins = mm(BK[7][0:NS, e * 32:e * 32 + 32], MBS[:, e, 0:NS], MLS[:, e, :], start=True, stop=True)
                ins.then_inc(sem("l2s_mm"), 1)
                fill(4)
                pe.wait_ge(sem("inv_u"), v * 5 - 4)
                pe.wait_ge(sem("inv_l"), v * 8 - 7)
                four(4, L2, U2)
                four(2, U2, L2)
                four(3, L2, TT).then_inc(sem("inv_mm"), 1)
                settle(pe)
                pe.wait_ge(sem("l2s"), v)
                for e in range(2):
                    ins = mm(BK[7][0:NS, 64 + e * 32:96 + e * 32], L2S[:, e, :], TS[:, e, :], start=True, stop=True)
                ins.then_inc(sem("ts_mm"), 1)
                fill(4)
                pe.wait_ge(sem("inv_u"), v * 5 - 3)
                pe.wait_ge(sem("inv_l"), v * 8 - 6)
                four(5, U1, L1)
                four(6, L1, TT).then_inc(sem("inv_mm"), 1)
                fill(4)
                pe.wait_ge(sem("inv_u"), v * 5 - 2)
                pe.wait_ge(sem("inv_l"), v * 8 - 5)
                four(4, L2, TT).then_inc(sem("inv_mm"), 1)
                fill(3)
                for merge in range(2):
                    pe.wait_ge(sem("inv_l"), v * 8 - 4 + merge * 2)
                    if merge == 0:
                        b0 = 2, 3, 5
                    else:
                        b0 = 6, 4, 2
                    for u in range(4):
                        tr(BK[b0[0]][:, u * P:(u + 1) * P], TT[:, u], ident)
                    four(b0[1], U1, TT).then_inc(sem("inv_mm"), 1)
                    fill(3)
                    pe.wait_ge(sem("inv_u"), v * 5 - 1 + merge)
                    pe.wait_ge(sem("inv_l"), v * 8 - 3 + merge * 2)
                    four(b0[2], L1, L2).then_inc(sem("inv_mm"), 1)
                    fill(3)
                pe.wait_ge(sem("inv_l"), v * 8)

                def rhs_mm(c):
                    tt, r = c // 2, halves[c % 2]
                    if c:
                        pe.wait_ge(sem("state"), v * 5 - 4 + c)
                    mm(BK[5][r, 0:P], AR[:, tt, 0, r], STT[:], start=True, stop=False, skip_group_check=True)
                    for e in range(2):
                        ins = mm(BK[5][r, e * 64:e * 64 + 64], MK[:, tt, e, r], TOK[:, tt, 2 * P + e * 64:2 * P + e * 64 + 64],
                                 start=False, stop=True, skip_group_check=True)
                    ins.then_inc(sem("rhs_mm"), 1)
                    mm(BK[7][:, c * CH:(c + 1) * CH], STT[:], AR[:, tt, 1, r], start=True, stop=False, skip_group_check=True)
                    for e, h in enumerate(halves):
                        mm(BK[7][h, c * CH:(c + 1) * CH], TOK[:, tt, 2 * P + e * 64:2 * P + e * 64 + 64],
                           MK[:, tt, e, P + 64 * (c % 2):P + 64 * (c % 2) + 64], start=False, stop=False,
                           skip_group_check=True)

                def u_mm(c):
                    tt, r = c // 2, halves[c % 2]
                    settle(pe)
                    pe.wait_ge(sem(f"rhs{c}"), v)
                    for e in range(2):
                        ins = mm(BK[6][r, e * 64:e * 64 + 64], TT[r, tt * 2 + e, r], RR[r, e * 64:e * 64 + 64],
                                 start=True, stop=True)
                    ins.then_inc(sem("u_mm"), 1)

                def state_mm(c):
                    tt, r = c // 2, halves[c % 2]
                    pe.wait_ge(sem("u"), v * 4 - 3 + c)
                    mm(BK[4][:, 0:P], TOK[r, tt, 0:P], UU[r, :], start=True, stop=False)
                    mm(BK[4][:, 0:P], TOK[r, tt, P:2 * P], TOK[r, tt, 2 * P:3 * P], start=False, stop=True)
                    for e, h in enumerate(halves):
                        ins = mm(BK[7][h, c * CH:(c + 1) * CH], UU[r, e * 64:e * 64 + 64],
                                 MB[r, tt, e, P + 64 * (c % 2):P + 64 * (c % 2) + 64], start=False, stop=True,
                                 skip_group_check=True)
                    ins.then_inc(sem("state_mm"), 1)

                pe.wait_ge(sem("state"), v * 5 - 4)
                pe.wait_ge(sem("ts"), v)
                rhs_mm(0)
                settle(pe)
                pe.wait_ge(sem("sin_in"), v * 16)
                for b in range(DB):
                    for e, h in enumerate(halves):
                        ins = mm(BK[3][h, b * 8:b * 8 + 8], SIN[h, b, :], ARS[h, :, b * DS:(b + 1) * DS], start=True, stop=True)
                ins.then_inc(sem("s0_mm"), 1)
                u_mm(0)
                fill(1)
                pe.wait_ge(sem("s0"), v)
                mm(BK[2][0:NS, 0:P], SPR[:, 0, :], ident, start=True, stop=False, skip_group_check=True)
                for e in range(2):
                    ins = mm(BK[2][0:NS, e * 64:e * 64 + 64], MKS[:, e, 0:NS], TOKS[:, 2 * P + e * 64:2 * P + e * 64 + 64],
                             start=False, stop=True, skip_group_check=True)
                ins.then_inc(sem("rhs_s_mm"), 1)
                state_mm(0)
                fill(1)
                rhs_mm(1)
                settle(pe)
                pe.wait_ge(sem("rhs_s"), v)
                for e in range(2):
                    ins = mm(BK[3][0:NS, e * 64:e * 64 + 64], TS[:, e, :], RS[:, e * 64:e * 64 + 64], start=True, stop=True)
                ins.then_inc(sem("u_s_mm"), 1)
                fill(1)
                u_mm(1)
                fill(1)
                state_mm(1)
                fill(1)
                rhs_mm(2)
                pe.wait_ge(sem("u_s"), v)
                for e, h in enumerate(halves):
                    mm(BK[2][h, :], TOKS[:, e * 64:e * 64 + 64], UM[:, e, :], start=True, stop=False)
                    ins = mm(BK[2][h, :], TOKS[:, P + e * 64:P + e * 64 + 64], VM[:, e, :], start=False, stop=True)
                ins.then_inc(sem("state_s_mm"), 1)
                u_mm(2)
                fill(1)
                state_mm(2)
                for e, h in enumerate(halves):
                    mm(BK[7][h, SEQ:N], US[:, e * 64:e * 64 + 64], MBS[:, e, NS:2 * NS], start=True, stop=False,
                       skip_group_check=True)
                    mm(BK[7][h, SEQ:N], TOKS[:, 2 * P + e * 64:2 * P + e * 64 + 64], MKS[:, e, NS:2 * NS], start=False,
                       stop=True, skip_group_check=True)
                fill(1)
                rhs_mm(3)
                fill(1)
                u_mm(3)
                fill(1)
                state_mm(3)
                fill(3)
                pe.wait_ge(sem("y"), v)
                mm(BK[3][:, 0:N], head_ones, YS[:], start=True, stop=True).then_inc(sem("y_mean"), 1)
                fill(4)
                pe.wait_ge(sem("y_sq"), v)
                mm(BK[5][:, 0:N], head_ones, YQ[:], start=True, stop=True).then_inc(sem("y_var"), 1)
                fill(KT * 4 - pos[0])

            with pe.Fori(0, PAIRS) as it:
                pair(it)

            def p_units(g):
                for j in range(4):
                    n = g * 4 + (U_P + j)
                    pe.wait_ge(sem("w_split"), n + 1)
                    if not (isinstance(g, int) and j < 2):
                        pe.wait_ge(sem("p_out"), g * 4 + (j - 1))
                    b = 2 * (j % 2)
                    blocks(n, j % 2, range(0, 8), BK[b][:, 0:N], XN)
                    blocks(n, j % 2, range(8, 16), BK[b + 1][:, 0:N], XN).then_inc(sem("unit_done"), 1)
            pe.wait_ge(sem("unit_out"), U_P)
            pe.wait_ge(sem("o_split"), 4)
            p_units(0)
            with pe.Fori(1, FORI_P) as g:
                p_units(g)
            def o_units(g):
                for j in range(4):
                    n = g * 4 + (U_O + j)
                    pe.wait_ge(sem("w_split"), n + 1)
                    if not (isinstance(g, int) and j < 2):
                        pe.wait_ge(sem("h_sum"), g * 4 + (j - 1))
                    blocks(n, j % 2, range(KT), BK[j % 2][:, 0:N], XM).then_inc(sem("unit_done"), 1)
            pe.wait_ge(sem("merged"), KT)
            o_units(0)
            with pe.Fori(1, FORI_P) as g:
                o_units(g)
            norm_sum(1, HSQ)
            pe.wait_ge(sem("x_split"), 8)

            def up_units(g):
                for j in range(4):
                    n = g * 4 + (U_UP + j)
                    pe.wait_ge(sem("w_split"), n + 1)
                    if not (isinstance(g, int) and j < 2):
                        pe.wait_ge(sem("up_out" if j % 2 else "gate_out"), g * 2 + (j // 2))
                    blocks(n, j % 2, range(KT), BK[j % 2][:, 0:N], XN).then_inc(sem("unit_done"), 1)
            up_units(0)
            with pe.Fori(1, FORI_UP) as g:
                up_units(g)
            pe.wait_ge(sem("act_split"), FT)
            pe.wait_ge(sem("up_out"), FT)

            def down_units(g):
                for j in range(2 * DU):
                    n = g * (2 * DU) + (U_DOWN + j)
                    tile, q = divmod(j, DU)
                    pe.wait_ge(sem("w_split"), n + 1)
                    if q == 0 and not isinstance(g, int):
                        pe.wait_ge(sem("down_out"), g * 2 + (tile - 1))
                    koff[0] = q * DK
                    blocks(n, j % 2, range(DK), BK[tile][:, 0:N], XF, q == 0, q == DU - 1).then_inc(sem("unit_done"), 1)
                koff[0] = 0
            down_units(0)
            with pe.Fori(1, KT // 2) as g:
                down_units(g)
            norm_sum(2, FSQ)

        @block.scalar
        def _(act):
            for dst, src, name in ((SHP, "shift_prev", "shp_in"), (PRM_ALL, "pair_params", "prm_in"),
                                   (LMU, "lora_mu", "lmu_in"), (AC, "att_c", "att_c_in"),
                                   (CONVP, "conv_params", "convp_in")):
                if dst is not SHP and dst is not AC:
                    act.dma_start(dst[:], a[src]).then_inc(sem(name), 16)
            for t in range(KT):
                act.wait_ge(sem("x_in"), 16)
                if t >= 2:
                    act.wait_ge(sem("norm_sq_used"), t - 1)
                actv(SQ[:, t % 2, :], XRAW[:, t, :], ACT.Square).then_inc(sem("norm_sq"), 1)

            def norm_tail(k, rstd, tiles, split):
                act.wait_ge(sem("norm_ms"), k + 1)
                actv(rstd[:], rstd[:], ACT.Sqrt).then_inc(sem("norm_rms"), 1)
                if split:
                    for i in range(4):
                        act.wait_ge(sem("normed"), 4 * k + i + 1)
                        actv(XN[:, 0, 4 * i:4 * i + 4, :], tiles[:, 4 * i:4 * i + 4, :], ACT.Copy).then_inc(sem("x_hi"), 1)

            split_hi(act, 0, 0)
            split_hi(act, 1, 1)
            norm_tail(0, RSTD, XRAW, True)
            act.wait_ge(sem("x_split"), 4)
            act.dma_start(SHP[:], a["shift_prev"]).then_inc(sem("shp_in"), 16)
            act.dma_start(AC[:], a["att_c"]).then_inc(sem("att_c_in"), 16)

            def in_units(g):
                for j in range(4):
                    n = g * 4 + j
                    act.wait_ge(sem("unit_done"), n + 1)
                    if isinstance(g, int):
                        tile = COLS[:, n, :]
                    else:
                        tile = step(colsv[:, bass.ds(g, 1), j, :])
                    actv(tile[:, 1:1 + SEQ], BK[j % 2][:, 0:SEQ], ACT.Copy)
                    actv(samples(tile[:, 1 + SEQ:E], 5), by_request(BK[j % 2][:, SEQ:N]), ACT.Copy).then_inc(sem("unit_out"), 1)
                    split_hi(act, n + 2, j % 2)
            in_units(0)
            with act.Fori(1, FORI_IN) as g:
                in_units(g)

            act.wait_ge(sem("shift_out"), 1)
            act.dma_start(o["shift"], SHO[:]).then_inc(sem("out_done"), 16)
            act.wait_ge(sem("roped"), len(ROPE_TILES))
            for g in range(KVH):
                actv(RT[:, g, 0:SEQ], COLS[:, T_V + g, 1:1 + SEQ], ACT.Copy)
                ins = actv(by_request(RT[:, g, SEQ:N]), samples(COLS[:, T_V + g, 1 + SEQ:E], 5), ACT.Copy)
            ins.then_inc(sem("v_compact"), 1)
            act.wait_ge(sem("v_compact"), 1)
            act.dma_start(o["v"], RT[:, :, 0:N]).then_inc(sem("att_out"), 16)
            act.dma_start(o["k"], COLS[:, T_K:T_K + KVH, 0:N]).then_inc(sem("att_out"), 16)
            act.dma_start(o["ki"], COLS[0:ID, T_KI, 0:N]).then_inc(sem("att_out"), 16)
            for n in range(16):
                act.wait_ge(sem("dots"), n + 1)
                if n >= 2:
                    act.wait_ge(sem("relu_used"), n - 1)
                for par in range(2):
                    ins = actv(RELU[:, n % 2, par * SEQ:(par + 1) * SEQ], BK[2 + n % 2 * 2 + par][:, 0:SEQ], ACT.Relu)
                ins.then_inc(sem("relu"), 1)
            for c in range(4):
                act.wait_ge(sem("dots"), 16 + c + 1)
                if c < 2:
                    act.wait_ge(sem("relu_used"), 15 + c)
                else:
                    act.wait_ge(sem("mixed"), c - 1)
                actv(RELU[:, c % 2, 0:KEYS_S], BK[2 + c % 2 * 2][:, 0:KEYS_S], ACT.Relu).then_inc(sem("relu"), 1)
            act.wait_ge(sem("v_t"), 1)
            act.wait_ge(sem("bias_ready"), 1)
            actv(VTOK[:].rearrange("p k f -> p (k f)"), BK[4][:], ACT.Copy).then_inc(sem("v_tok"), 1)
            for n, (qt, g) in enumerate(PROMPT_STEPS):
                act.wait_ge(sem("s_max"), n + 1)
                for r in range(4):
                    ins = actv(PROB[:, r * SEQ:(r + 1) * SEQ], PROB[:, r * SEQ:(r + 1) * SEQ], ACT.Exp,
                               bias=ST8[:, r:r + 1], accum_out=ST8[:, 4 + r:5 + r])
                ins.then_inc(sem("exp"), 1)
                act.wait_ge(sem("p_t"), n + 1)
                if n:
                    act.wait_ge(sem("pv"), n)
                actv(PRT[:, 0:512], BK[4][:], ACT.Copy).then_inc(sem("p_sb"), 1)
                act.wait_ge(sem("pv"), n + 1)
                actv(COLS[:, T_Q + 4 * g:T_Q + 4 * g + 4, qt * P:(qt + 1) * P],
                     BK[6][:].rearrange("p (r q) -> p r q", r=4), ACT.Copy).then_inc(sem("o_sb"), 1)
            for half in range(2):
                n = 4 + half
                act.wait_ge(sem("s_max"), n + 1)
                actv(PROB[:, 0:KEYS_S], BK[7][:, 0:KEYS_S], ACT.Exp, bias=ST8[:, 0:1], scale=HDIM ** -0.5,
                     accum_out=ST8[:, 4:5]).then_inc(sem("exp"), 1)
                act.wait_ge(sem("p_t"), n + 1)
                act.wait_ge(sem("pv"), n)
                actv(PRT[:, 0:2 * P], BK[4][:, 0:2 * P], ACT.Copy)
                actv(PRT[0:DS, 2 * P:3 * P], BK[4][0:DS, 2 * P:3 * P], ACT.Copy).then_inc(sem("p_sb"), 1)
                act.wait_ge(sem("v_new_t"), half + 1)
                for x in range(2):
                    ins = actv(VNEW[:, 2 * x:2 * x + 2, :].rearrange("t b f -> t (b f)"), BK[2 + x][0:DS, :], ACT.Copy)
                ins.then_inc(sem("v_new"), 1)
                act.wait_ge(sem("pv"), n + 1)
                c0 = SEQ + 16 * half
                for b in range(4):
                    ins = actv(COLS[:, T_Q:T_Q + AH, c0 + DS * b:c0 + DS * b + DS],
                               BK[6][:, b * 32:b * 32 + 32].rearrange("p (h t) -> p h t", t=DS), ACT.Copy)
                ins.then_inc(sem("o_sb"), 1)
            act.wait_ge(sem("lora_mix"), 1)
            actv(COLS[0:LORA_W, T_LW, 0:N], RKV[0:LORA_W, 0, :], ACT.Tanh)
            actv(COLS[0:LORA_A, T_LA, 0:N], RKV[0:LORA_A, 1, :], ACT.Copy)
            actv(COLS[:, T_LG, 0:N], RKV[:, 2, :], ACT.Tanh, scale=0.5).then_inc(sem("lora_act"), 1)
            act.wait_ge(sem("att_out"), 3 * 16)

            def pair(it):
                v = it + 1
                halves = [slice(0, 64), slice(64, 128)]

                def stream(j):
                    n = it * 4 + (U_GATE + j)
                    act.wait_ge(sem("unit_done"), n + 1)
                    actv(step(gatesv[:, bass.ds(it, 1), j, :]), BK[j % 2][:, 0:N], ACT.Tanh,
                         scale=0.5).then_inc(sem("unit_out"), 1)
                    split_hi(act, n + 2, j % 2)

                act.wait_ge(sem("rkv"), v)
                actv(SQK[:], RKV[:, 1, :], ACT.Square, scale=PRM[:, PR_KK:PR_KK + 1]).then_inc(sem("kk_sq"), 1)
                act.wait_ge(sem("z_mm"), v)
                actv(LDT[:, 0:2, :].rearrange("p t f -> p (t f)"), BK[2][:, 0:2 * P], ACT.Tanh, scale=0.5)
                actv(LDT[0:NS, 2, :], BK[2][0:NS, 2 * P:3 * P], ACT.Tanh, scale=0.5).then_inc(sem("z_tanh"), 1)
                act.wait_ge(sem("a_mm"), v)
                actv(AG[:], BK[3][:, 0:N], ACT.Tanh, bias=PRM[:, PR_A0H:PR_A0H + 1], scale=0.5).then_inc(sem("a_tanh"), 1)
                act.wait_ge(sem("g_mm"), v)
                actv(step(rwv[:, 2, bass.ds(it, 1), 0:N]), BK[6][:, 0:N], ACT.Copy).then_inc(sem("g_sb"), 1)
                act.wait_ge(sem("kk_max"), v)
                actv(SQK[:], KP[:], ACT.Sqrt).then_inc(sem("kk_norm"), 1)
                act.wait_ge(sem("log_decay"), v)
                actv(PEXP[:, 0, :], BK[5][:, 0:N], ACT.Exp)
                actv(PEXP[:, 1, :], BK[5][:, 0:N], ACT.Exp, scale=-1.0)
                actv(PEXP[:, 2, :], BK[6][:, 0:N], ACT.Exp).then_inc(sem("decay"), 1)
                act.wait_ge(sem("tok_mm"), v)
                actv(TOK[:, 0, :], BK[2][:, 0:3 * P], ACT.Copy)
                actv(TOK[:, 1, :], BK[3][:, 0:3 * P], ACT.Copy)
                actv(TOKS[:], BK[7][0:NS, 0:3 * P], ACT.Copy).then_inc(sem("tok_sb"), 1)
                stream(0)

                def evac(dst, bank, k):
                    act.wait_ge(sem("inv_mm"), v * 8 - 8 + k)
                    actv(dst[:].rearrange("p u f -> p (u f)"), BK[bank][:], ACT.Copy).then_inc(sem("inv_u"), 1)
                evac(U2, 5, 1)
                evac(U1, 4, 2)
                evac(L2, 5, 3)
                stream(1)
                evac(L1, 2, 5)
                evac(L1, 6, 7)
                stream(2)
                act.wait_ge(sem("s0_mm"), v)
                for x in range(2):
                    src = BK[3][:, 0:DB * 2 * DS].rearrange("p (b x t) -> p x b t", b=DB, x=2)[:, x]
                    ins = actv(by_request(SPR[:, x, :]), src, ACT.Copy)
                ins.then_inc(sem("s0"), 1)
                act.wait_ge(sem("y_centred"), v)
                actv(YQ[:], YS[:], ACT.Square).then_inc(sem("y_sq"), 1)
                act.wait_ge(sem("y_var_sb"), v)
                actv(YQ[:], YQ[:], ACT.Sqrt).then_inc(sem("y_std"), 1)
                stream(3)
            with act.Fori(0, PAIRS) as it:
                pair(it)

            act.wait_ge(sem("pair_done"), 1 + PAIRS)
            act.wait_ge(sem("sout_done"), 16 * PAIRS)
            act.wait_ge(sem("stout_done"), 32 * PAIRS)
            act.dma_start(H[:], a["x"]).then_inc(sem("h_in"), 16)
            act.wait_ge(sem("pair_done"), 1 + PAIRS)
            actv(XN[:, 0, 0:8, :], COLS[:, 0:8, 0:N], ACT.Copy).then_inc(sem("o_hi"), 1)
            actv(XN[:, 0, 8:16, :], COLS[:, T_Q:T_Q + 8, 0:N], ACT.Copy).then_inc(sem("o_hi"), 1)
            act.wait_ge(sem("o_split"), 4)

            xmv = XM[:].rearrange("p x (g j) n -> p x g j n", j=4)
            hv = H[:].rearrange("p (g j) n -> p g j n", j=4)

            def p_units(g):
                for j in range(4):
                    n = g * 4 + (U_P + j)
                    if isinstance(g, int):
                        dst = XM[:, 0, j, :]
                    else:
                        dst = step(xmv[:, 0, bass.ds(g, 1), j, :])
                    act.wait_ge(sem("unit_done"), n + 1)
                    split_hi(act, n + 2, j % 2)
                    act.wait_ge(sem("merge_sum"), g * 4 + (j + 1))
                    actv(dst, MG[:, 2 * (j % 2), :], ACT.Copy, scale=0.5).then_inc(sem("merge_hi"), 1)
            p_units(0)
            with act.Fori(1, FORI_P) as g:
                p_units(g)

            def o_units(g):
                for j in range(4):
                    split_hi(act, g * 4 + (U_O + j + 2), j % 2)
            o_units(0)
            with act.Fori(1, FORI_P) as g:
                o_units(g)
            act.wait_ge(sem("h_sum"), KT)
            act.dma_start(h_spill, H[:].rearrange("p k n -> p (k n)")).then_inc(sem("h_spilled"), 16)
            for t in range(KT):
                if t >= 2:
                    act.wait_ge(sem("norm_sq_used"), KT + t - 1)
                actv(HSQ[:, t % 2, :], H[:, t, :], ACT.Square).then_inc(sem("norm_sq"), 1)
            norm_tail(1, HRSTD, H, True)
            act.wait_ge(sem("x_split"), 8)
            act.dma_start(CPREV[:], a["conv_prev"]).then_inc(sem("cprev_in"), 16)

            xfv = XF[:].rearrange("p x (g j) n -> p x g j n", j=2)

            def up_units(g):
                for j in range(2):
                    n = g * 4 + (U_UP + 2 * j)
                    act.wait_ge(sem("unit_done"), n + 1)
                    if not (isinstance(g, int)):
                        act.wait_ge(sem("conv_used"), g * 2 + (j - 1))
                    actv(GX[:, j, 2:2 + SEQ], BK[0][:, 0:SEQ], ACT.Copy)
                    actv(samples(GX[:, j, 2 + SEQ:GE], 6), by_request(BK[0][:, SEQ:N]), ACT.Copy).then_inc(sem("gate_out"), 1)
                    split_hi(act, n + 2, 0)
                    act.wait_ge(sem("conv_done"), g * 2 + (j + 1))
                    actv(CV[:, j, 1, :], CV[:, j, 0, :], ACT.Silu).then_inc(sem("silu"), 1)
                    split_hi(act, n + 3, 1)
                    act.wait_ge(sem("up_out"), g * 2 + (j + 1))
                    dst = XF[:, 0, j, :] if isinstance(g, int) else step(xfv[:, 0, bass.ds(g, 1), j, :])
                    actv(dst, CV[:, j, 0, 0:N], ACT.Copy).then_inc(sem("glu_hi"), 1)
            up_units(0)
            with act.Fori(1, FORI_UP) as g:
                up_units(g)
            act.wait_ge(sem("conv_done"), FT)
            act.dma_start(o["conv"], COUT[:]).then_inc(sem("out_done"), 16)
            act.wait_ge(sem("h_spilled"), 16)
            act.wait_ge(sem("unit_done"), U_DOWN)
            act.dma_start(H2[:].rearrange("p k n -> p (k n)"), h_spill).then_inc(sem("h_back"), 16)

            def down_units(g, count=2 * DU):
                for j in range(count):
                    split_hi(act, g * (2 * DU) + (U_DOWN + j + 2), j % 2, DK)
            with act.Fori(0, KT // 2 - 1) as g:
                down_units(g)
            down_units(KT // 2 - 1, 2 * DU - 2)
            act.wait_ge(sem("down_out"), KT)
            for t in range(KT):
                if t >= 2:
                    act.wait_ge(sem("norm_sq_used"), 2 * KT + t - 1)
                actv(FSQ[:, t % 2, :], H2[:, t, :], ACT.Square).then_inc(sem("norm_sq"), 1)
            norm_tail(2, FRSTD, None, False)
            for i in range(4):
                act.wait_ge(sem("normed"), 8 + i + 1)
                act.dma_start(o["y"][:, 4 * i:4 * i + 4, :], YO[:, 4 * i:4 * i + 4, :]).then_inc(sem("out_done"), 16)

        @block.gpsimd
        def _(pool):
            pool.dma_start(PTAB[:], a["page_table"]).then_inc(sem("ptab_in"), 16)
            pool.wait_ge(sem("ptab_in"), 16)
            pool.wait_ge(sem("x_split"), 4)
            for b in range(DB):
                if b == 4:
                    pool.wait_ge(sem("pv"), 5)
                for j in range(2):
                    i = 2 * b + j
                    page = pool.value_load(PTAB[0:1, i:i + 1], min_val=0, max_val=N_POOL - 1)
                    keys = slice(j * PAGE, (j + 1) * PAGE)
                    for g in range(KVH):
                        pool.dma_start(KC[:, b % 4, g, keys], rows_of(a["cache_k"][bass.ds(page, 1), g])).then_inc(sem("kv_in"), 16)
                        pool.dma_start(VC[:, b % 4, j, g * P:(g + 1) * P],
                                       rows_of(a["cache_v"][bass.ds(page, 1), g])).then_inc(sem("kv_in"), 16)
                    if b < 4:
                        for b2 in (b, b + 4):
                            page = pool.value_load(PTAB[0:1, 2 * b2 + j:2 * b2 + j + 1], min_val=0, max_val=N_POOL - 1)
                            for par in range(2):
                                pool.dma_start(KIC[64 * par:64 * par + 64, b2, keys],
                                               rows_of(a["cache_kidx"][bass.ds(page, 1)])).then_inc(sem("ki_in"), 16)
            pool.wait_ge(sem("pair_done"), 1)
            pool.memset(STT[:], 0.0).then_inc(sem("state"), 1)
            pool.dma_start(LORA[:], a["lora"][0]).then_inc(sem("lora_in"), 16)
            pool.dma_start(SIN[:], a["state_s"][0]).then_inc(sem("sin_in"), 16)
            pool.wait_ge(sem("w_split"), U_GATE + 2)

            def pair(it, last):
                v = it + 1
                n = it * 4 + U_GATE
                split_lo(pool, n + 2, 0)
                if not last:
                    pool.wait_ge(sem("g_mm"), v)
                    pool.dma_start(LORA[:], rows3(a["lora"][bass.ds(it + 1, 1)])).then_inc(sem("lora_in"), 16)
                split_lo(pool, n + 3, 1)
                split_lo(pool, n + 4, 0)
                pool.wait_ge(sem("state_s_done"), v)
                dst = a_or(o["wkv_s"], it)
                pool.dma_start(dst, SIN[:]).then_inc(sem("sout_done"), 16)
                pool.wait_ge(sem("state"), v * 5)
                for e, h in enumerate((slice(0, 64), slice(64, 128))):
                    pool.dma_start(a_or(o["wkv_p"], it)[h, :], STT[h, h]).then_inc(sem("stout_done"), 16)
                split_lo(pool, n + 5, 1)
                pool.wait_ge(sem("sout_done"), v * 16)
                if not last:
                    pool.dma_start(SIN[:], rows3(a["state_s"][bass.ds(it + 1, 1)])).then_inc(sem("sin_in"), 16)
                pool.wait_ge(sem("stout_done"), v * 32)
                if not last:
                    pool.tensor_tensor(STT[:], ident, ident, ALU.subtract).then_inc(sem("state"), 1)

            def rows3(x):
                return x.rearrange("o p a b -> (o p) a b")

            def a_or(x, it):
                if isinstance(it, int):
                    return x[it]
                x = x[bass.ds(it, 1)]
                return rows3(x) if len(x.shape) == 4 else rows_of(x)

            with pool.Fori(0, PAIRS - 1) as it:
                pair(it, False)
            pair(PAIRS - 1, True)

        @block.vector
        def _(dve):
            st = Steps(dve, sem("dve_step"))
            dve.wait_ge(sem("norms_in"), 16)

            def norm(k, rstd, src, dst, gain, split):
                dve.wait_ge(sem("norm_sq_used"), KT * (k + 1))
                V.tensor_scalar(rstd[:], BK[2][:, 0:N], RMS_EPS, None, ALU.add).then_inc(sem("norm_ms"), 1)
                dve.wait_ge(sem("norm_rms"), k + 1)
                st.done(V.reciprocal(rstd[:], rstd[:]))
                for t in range(KT):
                    ins = V.scalar_tensor_tensor(dst[:, t, :], src[:, t, :], NORMS[:, k, t:t + 1], rstd[:], ALU.mult, ALU.mult)
                    if t % 4 == 3:
                        ins.then_inc(sem("normed"), 1)
                if split:
                    for i in range(4):
                        q = slice(4 * i, 4 * i + 4)
                        dve.wait_ge(sem("x_hi"), 4 * k + i + 1)
                        V.tensor_tensor(XN[:, 1, q, :], dst[:, q, :], XN[:, 0, q, :].bitcast(F32),
                                        ALU.subtract).then_inc(sem("x_split"), 1)

            split_lo(dve, 0, 0)
            split_lo(dve, 1, 1)
            norm(0, RSTD, XRAW, XRAW, 0, True)
            dve.wait_ge(sem("x_split"), 4)
            V.memset(COLS[:, :, 0:1], 0.0)
            V.memset(COLS[:, RW_T:, 1 + SEQ:E:5], 0.0)
            dve.wait_ge(sem("shp_in"), 16)
            V.tensor_copy(COLS[:, 0:RW_T, 1 + SEQ:E:5], SHP[:]).then_inc(sem("slots"), 1)
            V.memset(QZ[:].rearrange("p g b h t -> p (g b h t)"), 0.0)

            def in_units(g):
                for j in range(4):
                    split_lo(dve, g * 4 + (j + 2), j % 2)
            in_units(0)
            with dve.Fori(1, FORI_IN) as g:
                in_units(g)

            dve.wait_ge(sem("unit_out"), U_GATE)
            dve.wait_ge(sem("slots"), 1)
            V.tensor_copy(SHO[:, :, 0:1], COLS[:, 0:RW_T, SEQ:SEQ + 1])
            V.tensor_copy(SHO[:, :, 1:1 + DB], COLS[:, 0:RW_T, SEQ + 5:E:5]).then_inc(sem("shift_out"), 1)
            dve.wait_ge(sem("att_c_in"), 16)
            for i, t in enumerate(ROPE_TILES):
                kind = "head" if t < T_V else "idx"
                dve.wait_ge(sem("rot"), i + 1)
                V.tensor_tensor(RT[:, 0, :], BK[2 + i % 2][:, 0:TE], acst("sin_" + kind), ALU.mult).then_inc(sem("rot_used"), 1)
                st.done(V.tensor_tensor(RT[:, 1, :], COLS[:, t, 1:E], acst("cos_" + kind), ALU.mult))
                dve.wait_ge(sem("rot_used"), i + 1)
                st.mark(V.tensor_tensor(COLS[:, t, 0:SEQ], RT[:, 0, 0:SEQ], RT[:, 1, 0:SEQ], ALU.add))
                if T_QI <= t < T_KI:
                    dst = QIS[:, :, t - T_QI, :]
                else:
                    dst = by_request(COLS[:, t, SEQ:N])
                V.tensor_tensor(dst, samples(RT[:, 0, SEQ:TE], 5), samples(RT[:, 1, SEQ:TE], 5),
                                ALU.add).then_inc(sem("roped"), 1)
                dve.wait_ge(sem("roped"), i + 1)
                st.sync()
            dve.wait_ge(sem("wi_t"), 1)
            V.tensor_scalar(WI[:], BK[4][:, 0:2 * P].rearrange("p (q f) -> p q f", q=2)[:, :, WI_ROW:WI_ROW + IH],
                            IDX_SCALE, None, ALU.mult).then_inc(sem("wi_sb"), 1)
            dve.wait_ge(sem("wi_rows"), 1)
            for c in range(4):
                ins = V.tensor_tensor(WM[:, c, :], BK[5][:, 0:NS], acst("m_query")[:, c * NS:(c + 1) * NS], ALU.mult)
            ins.then_inc(sem("w_mix"), 1)
            dve.wait_ge(sem("wi_sb"), 1)
            for qt in range(2):
                for i in range(8):
                    n = qt * 8 + i
                    dve.wait_ge(sem("relu"), n + 1)
                    for par in range(2):
                        src = RELU[:, n % 2, par * SEQ:(par + 1) * SEQ]
                        w = WI[:, qt, 2 * i + par:2 * i + par + 1]
                        base = ACC[:, qt, :] if i or par else acst("causal")[:, qt * SEQ:(qt + 1) * SEQ]
                        ins = V.scalar_tensor_tensor(ACC[:, qt, :], src, w, base, ALU.mult, ALU.add)
                        st.done(ins) if par == 0 else None
                    ins.then_inc(sem("relu_used"), 1)
                    dve.wait_ge(sem("relu_used"), n + 1)
            dve.wait_ge(sem("mixed"), 4)
            st.done(V.tensor_tensor(ACS[:], BK[6][0:NS, 0:KEYS_S], acst("causal_s", NS), ALU.add))
            for scores, topk, bias, causal in (
                    (ACC[:, 0, :], TOPK_P, BIASP[:, 0, :], acst("causal")[:, 0:SEQ]),
                    (ACC[:, 1, :], TOPK_P, BIASP[:, 1, :], acst("causal")[:, SEQ:2 * SEQ]),
                    (ACS[:], TOPK_S, BIASS[:], acst("causal_s", NS))):
                m8 = M8[0:scores.shape[0], :]
                while topk > 0:
                    st.done(V.max(m8, scores))
                    if topk < 8:
                        st.done(V.memset(m8[:, topk:8], MARK))
                    st.done(V.match_replace(scores, m8, scores, MARK))
                    topk -= 8
                st.done(V.tensor_scalar(scores, scores, MARK / 2, -BIGNEG, ALU.is_lt, ALU.mult))
                ins = V.scalar_tensor_tensor(bias, scores, BIGNEG, causal, ALU.add, ALU.add)
                if bias.shape[0] == P:
                    st.done(ins)
            ins.then_inc(sem("bias_ready"), 1)
            dve.wait_ge(sem("bias_ready"), 1)
            for n, (qt, g) in enumerate(PROMPT_STEPS):
                dve.wait_ge(sem("s_mm"), n + 1)
                if n:
                    dve.wait_ge(sem("p_t"), n)
                else:
                    dve.wait_ge(sem("mixed"), 4)
                for r in range(4):
                    ins = V.scalar_tensor_tensor(PROB[:, r * SEQ:(r + 1) * SEQ], BK[2 + r // 2][:, r % 2 * SEQ:(r % 2 + 1) * SEQ],
                                                 HDIM ** -0.5, BIASP[:, qt, :], ALU.mult, ALU.add)
                ins.then_inc(sem("s_used"), 1)
                dve.wait_ge(sem("s_used"), n + 1)
                V.tensor_reduce(ST8[:, 0:4], PROB[:].rearrange("p (r k) -> p r k", r=4), AX.X, ALU.max,
                                negate=True).then_inc(sem("s_max"), 1)
                dve.wait_ge(sem("exp"), n + 1)
                st.done(V.reciprocal(ST8[:, 8:12], ST8[:, 4:8]))
                for r in range(4):
                    ins = V.tensor_scalar(PROB[:, r * SEQ:(r + 1) * SEQ], PROB[:, r * SEQ:(r + 1) * SEQ],
                                          ST8[:, 8 + r:9 + r], None, ALU.mult)
                ins.then_inc(sem("prob"), 1)
                dve.wait_ge(sem("p_t"), n + 1)
                if n:
                    dve.wait_ge(sem("pv"), n)
                V.tensor_copy(PRT[:, 512:1024], BK[5][:]).then_inc(sem("p_sb2"), 1)
            for half in range(2):
                n = 4 + half
                if half:
                    dve.wait_ge(sem("s_mm"), 5)
                for g in range(KVH):
                    for b in range(4):
                        c0 = SEQ + DS * (4 * half + b)
                        ins = V.tensor_copy(QZ[:, g, b, 4 * g:4 * g + 4, :], COLS[:, T_Q + 4 * g:T_Q + 4 * g + 4, c0:c0 + DS])
                ins.then_inc(sem("q_grouped"), 1)
                dve.wait_ge(sem("s_mm"), n + 1)
                st.done(V.tensor_reduce(ST8[:, 1:2], BK[7][:, 0:KEYS_S], AX.X, ALU.max, negate=True))
                V.tensor_scalar(ST8[:, 0:1], ST8[:, 1:2], HDIM ** -0.5, None, ALU.mult).then_inc(sem("s_max"), 1)
                dve.wait_ge(sem("p_t"), n)
                dve.wait_ge(sem("exp"), n + 1)
                st.done(V.reciprocal(ST8[:, 8:9], ST8[:, 4:5]))
                V.tensor_scalar(PROB[:, 0:KEYS_S], PROB[:, 0:KEYS_S], ST8[:, 8:9], None, ALU.mult).then_inc(sem("prob"), 1)

            dve.wait_ge(sem("o_sb"), 6)
            dve.wait_ge(sem("pv"), 6)
            dve.wait_ge(sem("prm_in"), 16)
            dve.wait_ge(sem("lmu_in"), 16)

            def mix(src, dst, mu):
                st.done(V.tensor_tensor(DIFF[:], src[:, :, 0:TE], src[:, :, 1:E], ALU.subtract))
                for j in range(3):
                    V.scalar_tensor_tensor(dst[:, j, 0:SEQ], DIFF[:, j, 0:SEQ], mu[:, j:j + 1], src[:, j, 1:1 + SEQ],
                                           ALU.mult, ALU.add)
                    ins = V.scalar_tensor_tensor(by_request(dst[:, j, SEQ:N]), samples(DIFF[:, j, SEQ:TE], 5), mu[:, j:j + 1],
                                                 samples(src[:, j, 1 + SEQ:E], 5), ALU.mult, ALU.add)
                return ins
            mix(COLS[:, T_LW:T_LG + 1, :], RKV, LMU).then_inc(sem("lora_mix"), 1)
            dve.wait_ge(sem("lora_act"), 1)
            st.done(V.memset(COLS[LORA_W:LORA_W + 1, T_LW, 0:N], 1.0))
            st.done(V.tensor_scalar(COLS[:, T_LG, 0:N], COLS[:, T_LG, 0:N], 0.5, 0.5, ALU.mult, ALU.add))
            V.tensor_scalar(PRM_ALL[:, :, PR_A0H], PRM_ALL[:, :, PR_A0H], 0.5, None, ALU.mult).then_inc(sem("pair_done"), 1)
            dve.wait_ge(sem("pair_done"), 1)

            def pair(it):
                v = it + 1
                halves = [slice(0, 64), slice(64, 128)]
                r_, k_, v_ = RKV[:, 0, :], RKV[:, 1, :], RKV[:, 2, :]

                def prm(i):
                    return PRM[:, i:i + 1]

                st.done(V.tensor_copy(PRM[:], step(PRM_ALL[:, bass.ds(it, 1), :])))
                src = rwv[:, :, bass.ds(it, 1), :].rearrange("p j o e -> p (j o) e")
                mix(src, RKV, PRM).then_inc(sem("rkv"), 1)
                dve.wait_ge(sem("rkv"), v)
                dve.wait_ge(sem("kk_sum"), v)
                V.tensor_scalar(KP[:], BK[4][:, 0:N], 1e-24, None, ALU.max).then_inc(sem("kk_max"), 1)
                dve.wait_ge(sem("a_tanh"), v)
                st.done(V.tensor_scalar(AG[:], AG[:], 0.5, 0.5, ALU.mult, ALU.add))
                dve.wait_ge(sem("z_tanh"), v)
                V.tensor_scalar(LDT[:, 0:2, :], LDT[:, 0:2, :], 1.0, None, ALU.add)
                V.tensor_scalar(LDT[0:NS, 2, :], LDT[0:NS, 2, :], 1.0, None, ALU.add).then_inc(sem("decay_tok"), 1)
                dve.wait_ge(sem("kk_norm"), v)
                st.done(V.reciprocal(SQK[:], SQK[:]))
                st.mark(V.scalar_tensor_tensor(KKN[:], k_, prm(PR_KK), SQK[:], ALU.mult, ALU.mult))
                st.done(V.tensor_scalar(KP[:], AG[:], 1.0, prm(PR_KA), ALU.subtract, ALU.mult))
                st.done(V.scalar_tensor_tensor(KP[:], KP[:], 1.0, k_, ALU.add, ALU.mult))
                V.scalar_tensor_tensor(SQK[:], r_, prm(PR_RK), KP[:], ALU.mult, ALU.mult).then_inc(sem("rkr"), 1)
                st.done(V.tensor_tensor(AG[:], KKN[:], AG[:], ALU.mult))
                dve.wait_ge(sem("decay"), v)

                def two(x):
                    return x[:, 0:SEQ].rearrange("p (t n) -> p t n", t=2)
                p, pi, px = PEXP[:, 0, :], PEXP[:, 1, :], PEXP[:, 2, :]
                V.scalar_tensor_tensor(AR[:, :, 0, :], two(KKN), -1.0, two(px), ALU.mult, ALU.mult)
                V.scalar_tensor_tensor(ARS[:, 0, :], KKN[:, SEQ:N], -1.0, px[:, SEQ:N], ALU.mult, ALU.mult)
                V.tensor_tensor(AR[:, :, 1, :], two(r_), two(p), ALU.mult)
                V.tensor_tensor(ARS[:, 1, :], r_[:, SEQ:N], p[:, SEQ:N], ALU.mult)
                V.tensor_tensor(BT[:], AG[:], pi, ALU.mult)
                V.tensor_copy(PC[:, 0:NCH], p[:, CH - 1:SEQ:CH])
                V.tensor_copy(PC[:, NCH:], p[:, SEQ + DS - 1:N:DS])
                V.tensor_tensor(KTL[:], KP[:], pi, ALU.mult).then_inc(sem("ar_ready"), 1)
                dve.wait_ge(sem("bonus_mm"), v)
                V.tensor_tensor(step(rwv[:, 1, bass.ds(it, 1), 0:N]), BK[4][:, 0:N], v_, ALU.mult).then_inc(sem("bonus"), 1)
                dve.wait_ge(sem("tok_mm"), v)
                dve.wait_ge(sem("ar_ready"), v)
                dve.wait_ge(sem("bonus"), v)
                dve.wait_ge(sem("b_mm"), v)
                for e in range(2):
                    bank = BK[5 + e][:].rearrange("p (t f) -> p t f", t=2)
                    V.tensor_tensor(MB[:, :, e, :], bank, spread(m_ab, 1, [P, 2, 2 * P]), ALU.mult)
                    ins = V.tensor_tensor(U1[:, e::2, :], bank[:, :, 0:P], spread(m16u, 1, [P, 2, P]), ALU.mult)
                st.done(ins)
                V.tensor_tensor(TT[:], U1[:], spread(ident, 1, [P, 4, P]), ALU.add)
                dve.wait_ge(sem("k_mm"), v)
                bank = BK[4][:].rearrange("p (u f) -> p u f", u=4)
                V.tensor_tensor(L1[:], bank, spread(m16l, 1, [P, 4, P]), ALU.mult)
                V.tensor_copy(ML[:], bank)
                for e in range(2):
                    bank = BK[2 + e][:].rearrange("p (t f) -> p t f", t=2)
                    V.tensor_tensor(MK[:, :, e, :], bank, spread(m_ab, 1, [P, 2, 2 * P]), ALU.mult)
                bank = BK[7][0:NS]
                st.mark(V.tensor_tensor(MBS[:], bank[:, 0:128].rearrange("p (e f) -> p e f", e=2), spread(ms_ab, 1, [NS, 2, 2 * NS]), ALU.mult))
                V.tensor_tensor(MKS[:], bank[:, 128:256].rearrange("p (e f) -> p e f", e=2), spread(ms_ab, 1, [NS, 2, 2 * NS]), ALU.mult)
                st.sync()
                V.tensor_tensor(TS[:], MBS[:, :, 0:NS], spread(ident[0:NS, 0:NS], 1, [NS, 2, NS]), ALU.add)
                V.tensor_tensor(MLS[:], bank[:, 256:320].rearrange("p (e f) -> p e f", e=2), spread(ms_l, 1, [NS, 2, NS]),
                                ALU.mult).then_inc(sem("mats"), 1)
                dve.wait_ge(sem("mats"), v)

                def grid(bank):
                    return BK[bank][:].rearrange("p (u f) -> p u f", u=4)

                def inv(k):
                    dve.wait_ge(sem("inv_mm"), v * 8 - 8 + k)

                def add_t(bank, k):
                    V.tensor_tensor(TT[:], TT[:], grid(bank), ALU.add).then_inc(sem("inv_l"), 1)
                    dve.wait_ge(sem("inv_l"), v * 8 - 8 + k)
                inv(1)
                V.tensor_copy(L2[:], grid(6)).then_inc(sem("inv_l"), 1)
                dve.wait_ge(sem("l2s_mm"), v)
                V.tensor_copy(L2S[:], BK[7][0:NS, 0:2 * NS].rearrange("p (e f) -> p e f", e=2)).then_inc(sem("l2s"), 1)
                inv(2)
                V.tensor_copy(L1[:], grid(2))
                add_t(3, 2)
                dve.wait_ge(sem("ts_mm"), v)
                V.tensor_tensor(TS[:], TS[:], BK[7][0:NS, 2 * NS:4 * NS].rearrange("p (e f) -> p e f", e=2),
                                ALU.add).then_inc(sem("ts"), 1)
                inv(3)
                V.tensor_tensor(U1[:], ML[:], spread(m32l, 1, [P, 4, P]), ALU.mult)
                add_t(6, 3)
                inv(4)
                add_t(4, 4)
                for merge in range(2):
                    inv(5 + 2 * merge)
                    V.tensor_copy(L2[:], grid((3, 4)[merge])).then_inc(sem("inv_l"), 1)
                    if merge == 0:
                        V.tensor_tensor(U1[:], ML[:], spread(m64l, 1, [P, 4, P]), ALU.mult)
                    inv(6 + 2 * merge)
                    add_t((5, 2)[merge], 6 + 2 * merge)

                def rhs(c):
                    r = halves[c % 2]
                    dve.wait_ge(sem("rhs_mm"), v * 4 - 3 + c)
                    V.tensor_copy(RR[r, :], BK[5][r, 0:P]).then_inc(sem(f"rhs{c}"), 1)
                    dve.wait_ge(sem("state"), v * 5 - 4 + c)
                    st.mark(V.tensor_scalar(STP[:], STT[:], PC[:, c:c + 1], None, ALU.mult))

                def u(c):
                    r = halves[c % 2]
                    dve.wait_ge(sem("u_mm"), v * 4 - 3 + c)
                    V.tensor_copy(UU[r, :], BK[6][r, 0:P]).then_inc(sem("u"), 1)

                def state(c):
                    st.sync()
                    dve.wait_ge(sem("state_mm"), v * 4 - 3 + c)
                    for h in halves:
                        ins = V.scalar_tensor_tensor(STT[h, h], BK[4][h, h], PC[h, c:c + 1], STP[h, h], ALU.mult, ALU.add)
                    ins.then_inc(sem("state"), 1)

                rhs(0)
                u(0)
                dve.wait_ge(sem("rhs_s_mm"), v)
                V.tensor_copy(RS[:], BK[2][0:NS, 0:P]).then_inc(sem("rhs_s"), 1)
                state(0)
                rhs(1)
                dve.wait_ge(sem("u_s_mm"), v)
                st.done(V.tensor_copy(US[:], BK[3][0:NS, 0:P]))
                req = spread(ms_req, 2, [NS, DB, HD])
                for e in range(2):
                    for dst, val in ((UM, US[:, e * HD:(e + 1) * HD]), (VM, TOKS[:, 2 * P + e * HD:2 * P + (e + 1) * HD])):
                        ins = V.tensor_tensor(dst[:, e, :].rearrange("p (b f) -> p b f", b=DB), spread(val, 1, [NS, DB, HD]),
                                              req, ALU.mult)
                ins.then_inc(sem("u_s"), 1)
                u(1)
                state(1)
                rhs(2)
                u(2)
                dve.wait_ge(sem("state_s_mm"), v)
                st.done(V.tensor_tensor(SIN[:], SIN[:], BK[2][:].rearrange("p (b f) -> p b f", b=DB), ALU.add))
                V.tensor_tensor(SIN[:], SIN[:], spread(PC[:, NCH:], 2, [P, DB, HD]), ALU.mult).then_inc(sem("state_s_done"), 1)
                state(2)
                rhs(3)
                u(3)
                state(3)
                V.tensor_copy(YS[:, 0:SEQ], BK[7][:, 0:SEQ])
                dve.wait_ge(sem("s0"), v)
                V.tensor_tensor(YS[:, SEQ:N], BK[7][:, SEQ:N], SPR[:, 1, :], ALU.add).then_inc(sem("y"), 1)
                dve.wait_ge(sem("y"), v)
                dve.wait_ge(sem("y_mean"), v)
                V.scalar_tensor_tensor(YS[:], BK[3][:, 0:N], -1.0 / HD, YS[:], ALU.mult, ALU.add).then_inc(sem("y_centred"), 1)
                dve.wait_ge(sem("y_var"), v)
                V.tensor_scalar(YQ[:], BK[5][:, 0:N], 1.0 / HD, GN_EPS, ALU.mult, ALU.add).then_inc(sem("y_var_sb"), 1)
                dve.wait_ge(sem("y_std"), v)
                st.done(V.reciprocal(YQ[:], YQ[:]))
                st.done(V.tensor_tensor(YS[:], YS[:], YQ[:], ALU.mult))
                st.done(V.tensor_scalar(YS[:], YS[:], prm(PR_LW), prm(PR_LB), ALU.mult, ALU.add))
                st.done(V.tensor_tensor(YS[:], YS[:], step(rwv[:, 1, bass.ds(it, 1), 0:N]), ALU.add))
                dve.wait_ge(sem("g_sb"), v)
                V.tensor_tensor(step(rwv[:, 0, bass.ds(it, 1), 0:N]), YS[:], step(rwv[:, 2, bass.ds(it, 1), 0:N]),
                                ALU.mult).then_inc(sem("pair_done"), 1)
            st.repeat(PAIRS, PAIR_STEPS, pair)

            dve.wait_ge(sem("pair_done"), 1 + PAIRS)
            for i, t in ((0, 0), (1, T_Q)):
                dve.wait_ge(sem("o_hi"), i + 1)
                V.tensor_tensor(XN[:, 1, 8 * i:8 * i + 8, :], COLS[:, t:t + 8, 0:N], XN[:, 0, 8 * i:8 * i + 8, :].bitcast(F32),
                                ALU.subtract).then_inc(sem("o_split"), 2)
            dve.wait_ge(sem("w_split"), U_P + 2)
            xmv = XM[:].rearrange("p x (g j) n -> p x g j n", j=4)
            hv = H[:].rearrange("p (g j) n -> p g j n", j=4)
            dve.wait_ge(sem("h_in"), 16)

            def p_units(g):
                for j in range(4):
                    n = g * 4 + (U_P + j)
                    m1 = g * 4 + (j + 1)
                    b, s0 = 2 * (j % 2), 2 * (j % 2)
                    if isinstance(g, int):
                        ga, gb, hi, lo = GATES[:, j, :], GATES[:, KT + j, :], XM[:, 0, j, :], XM[:, 1, j, :]
                    else:
                        ga, gb = step(gatesv[:, bass.ds(g, 1), j, :]), step(gatesv[:, bass.ds(g + KT // 4, 1), j, :])
                        hi, lo = (step(xmv[:, x, bass.ds(g, 1), j, :]) for x in range(2))
                    dve.wait_ge(sem("unit_done"), n + 1)
                    if not (isinstance(g, int) and j < 2):
                        dve.wait_ge(sem("merged"), m1 - 2)
                    V.scalar_tensor_tensor(MG[:, s0, :], ga, 1.0, BK[b][:, 0:N], ALU.add, ALU.mult)
                    V.scalar_tensor_tensor(MG[:, s0 + 1, :], gb, 1.0, BK[b + 1][:, 0:N], ALU.add, ALU.mult).then_inc(sem("p_out"), 1)
                    dve.wait_ge(sem("p_out"), m1)
                    V.tensor_tensor(MG[:, s0, :], MG[:, s0, :], MG[:, s0 + 1, :], ALU.add).then_inc(sem("merge_sum"), 1)
                    split_lo(dve, n + 2, j % 2)
                    dve.wait_ge(sem("merge_hi"), m1)
                    V.scalar_tensor_tensor(lo, MG[:, s0, :], 0.5, hi.bitcast(F32), ALU.mult, ALU.subtract).then_inc(sem("merged"), 1)
            p_units(0)
            with dve.Fori(1, FORI_P) as g:
                p_units(g)

            def o_units(g):
                for j in range(4):
                    n = g * 4 + (U_O + j)
                    t = H[:, j, :] if isinstance(g, int) else step(hv[:, bass.ds(g, 1), j, :])
                    dve.wait_ge(sem("unit_done"), n + 1)
                    V.tensor_tensor(t, t, BK[j % 2][:, 0:N], ALU.add).then_inc(sem("h_sum"), 1)
                    split_lo(dve, n + 2, j % 2)
            o_units(0)
            with dve.Fori(1, FORI_P) as g:
                o_units(g)
            dve.wait_ge(sem("h_spilled"), 16)
            norm(1, HRSTD, H, H, 1, True)
            dve.wait_ge(sem("x_split"), 8)
            V.memset(GX[:, :, 0:2], 0.0)
            dve.wait_ge(sem("cprev_in"), 16)
            dve.wait_ge(sem("convp_in"), 16)
            xfv = XF[:].rearrange("p x (g j) n -> p x g j n", j=2)
            cpv = CPREV[:].rearrange("p (g j) n -> p g j n", j=2)
            cov = COUT[:].rearrange("p (g j) n -> p g j n", j=2)
            cfv = CONVP[:].rearrange("p (g j) n -> p g j n", j=2)

            def up_pair(g, j):
                n = g * 4 + (U_UP + 2 * j)
                p1 = g * 2 + (j + 1)
                if isinstance(g, int):
                    prev, out, cf, hi, lo = CPREV[:, j, :], COUT[:, j, :], CONVP[:, j, :], XF[:, 0, j, :], XF[:, 1, j, :]
                else:
                    prev, out, cf = (step(x[:, bass.ds(g, 1), j, :]) for x in (cpv, cov, cfv))
                    hi, lo = (step(xfv[:, x, bass.ds(g, 1), j, :]) for x in range(2))
                gx = GX[:, j, :]
                hist = gx[:, 2 + SEQ:GE].rearrange("p (b f) -> p b f", f=6)
                st.done(V.tensor_copy(hist[:, :, 0:2], prev.rearrange("p (b f) -> p b f", f=2)))
                dve.wait_ge(sem("gate_out"), p1)
                c = CV[:, j, 0, :]
                st.done(V.tensor_scalar(c, gx[:, 0:CE], cf[:, 0:1], cf[:, 3:4], ALU.mult, ALU.add))
                st.done(V.scalar_tensor_tensor(c, gx[:, 1:1 + CE], cf[:, 1:2], c, ALU.mult, ALU.add))
                V.scalar_tensor_tensor(c, gx[:, 2:2 + CE], cf[:, 2:3], c, ALU.mult, ALU.add).then_inc(sem("conv_done"), 1)
                V.tensor_copy(out[:, 0:2], gx[:, SEQ:SEQ + 2])
                V.tensor_copy(out[:, 2:].rearrange("p (b f) -> p b f", f=2), hist[:, :, 4:6]).then_inc(sem("conv_used"), 1)
                split_lo(dve, n + 2, 0)
                dve.wait_ge(sem("silu"), p1)
                dve.wait_ge(sem("unit_done"), n + 2)
                s = CV[:, j, 1, :]
                V.tensor_tensor(c[:, 0:SEQ], s[:, 0:SEQ], BK[1][:, 0:SEQ], ALU.mult)
                V.tensor_tensor(by_request(c[:, SEQ:N]), samples(s[:, SEQ:CE], 6), by_request(BK[1][:, SEQ:N]),
                                ALU.mult).then_inc(sem("up_out"), 1)
                split_lo(dve, n + 3, 1)
                dve.wait_ge(sem("glu_hi"), p1)
                V.tensor_tensor(lo, c[:, 0:N], hi.bitcast(F32), ALU.subtract).then_inc(sem("act_split"), 1)
                dve.wait_ge(sem("act_split"), p1)
            up_pair(0, 0)
            up_pair(0, 1)
            st.repeat(FORI_UP, UP_STEPS, lambda g: (up_pair(g, 0), up_pair(g, 1)), first=1)

            dve.wait_ge(sem("h_back"), 16)
            h2v = H2[:].rearrange("p (g j) n -> p g j n", j=2)

            def down_units(g, count=2 * DU):
                for j in range(2 * DU):
                    n = g * (2 * DU) + (U_DOWN + j)
                    tile, q = divmod(j, DU)
                    if q == DU - 1:
                        dve.wait_ge(sem("unit_done"), n + 1)
                        t = H2[:, 2 * g + tile, :] if isinstance(g, int) else step(h2v[:, bass.ds(g, 1), tile, :])
                        V.tensor_tensor(t, t, BK[tile][:, 0:N], ALU.add).then_inc(sem("down_out"), 1)
                    if j < count:
                        split_lo(dve, n + 2, j % 2, DK)
            with dve.Fori(0, KT // 2 - 1) as g:
                down_units(g)
            down_units(KT // 2 - 1, 2 * DU - 2)
            norm(2, FRSTD, H2, YO, 2, False)


def units(w, tiles=None):
    k, n = w.shape
    return np.ascontiguousarray(w.reshape(k // P, P, n // P, P).transpose(2, 1, 0, 3)).reshape(n // P, P, k)


def tiles_of(v):
    return v.reshape(-1, P).T


def pad_cols(w, n):
    return np.concatenate([w, np.zeros((w.shape[0], n - w.shape[1]), w.dtype)], 1)


def rw_tiles(x):
    z = np.zeros(x.shape[:-1] + (32,), x.dtype)
    o = 3 * RW_WIDTH
    return np.concatenate([x[..., :o + 96], z, x[..., o + 96:o + 192], z, x[..., o + 192:]], -1)


OUTS = {"y": (P, KT, N), "k": (P, KVH, N), "v": (P, KVH, N), "ki": (ID, N), "wkv_p": (PAIRS, P, HD),
        "wkv_s": (PAIRS, P, DB, HD), "shift": (P, RW_T, 1 + DB), "conv": (P, FT, 2 + 2 * DB)}


def kernel(**inputs):
    import concourse.bacc as bacc
    from concourse.bass_utils import run_bass_kernel_spmd

    x = {k: np.asarray(v) for k, v in inputs.items()}
    w1 = {k: x[k][0] for k in x if k not in ("x_prompt", "x_sample", "page_table", "norm_f")}
    tokens = np.concatenate([x["x_prompt"][0], x["x_sample"].reshape(NS, D_MODEL)], 0)
    w_in = w1["w_in"]
    rw, att, gate = w_in[:, :RW_COLS], w_in[:, RW_COLS:-2 * D_MODEL], w_in[:, -2 * D_MODEL:]
    att_n = (AH + 2 * KVH) * HDIM
    qi = att[:, att_n:att_n + IH * ID]
    ki = att[:, att_n + IH * ID:att_n + IH * ID + ID]
    wi = att[:, att_n + IH * ID + ID:]
    rw = rw_tiles(rw)
    lw = rw[:, T_LW * P:(T_LW + 1) * P]
    rw = np.concatenate([rw[:, :T_LW * P], lw[:, :WI_ROW], wi, lw[:, WI_ROW + IH:], rw[:, (T_LW + 1) * P:]], 1)
    arr = {}
    arr["x"] = tokens.T.reshape(KT, P, N).transpose(1, 0, 2)
    arr["main_c"], arr["att_c"] = MAIN_C, ATT_C
    arr["w_in"] = units(np.concatenate([rw, att[:, :att_n], qi, ki, ki], 1))
    arr["w_gate"] = units(gate)
    arr["w_p"] = np.concatenate([units(w1["p_rw"]), units(w1["p_att"])], 2)
    arr["w_o"] = units(w1["w_o"])
    up = units(w1["w_up"])
    arr["w_up"] = np.stack([up[:FT], up[FT:]], 1).reshape(2 * FT, P, D_MODEL)
    arr["w_down"] = units(w1["w_down"]).reshape(KT, P, DU, DK * P).transpose(0, 2, 1, 3).reshape(KT * DU, P, DK * P)
    arr["norms"] = np.stack([tiles_of(w1["norm1"]), tiles_of(w1["norm2"]), tiles_of(x["norm_f"])], 1)
    mu = tiles_of(rw_tiles(w1["rw_mu"]))
    prm = [mu[:, 0:8], mu[:, 8:16], mu[:, 16:24]] + [tiles_of(w1[k]) for k in (
        "rw_a0", "rw_k_k", "rw_k_a", "rw_r_k", "rw_lnx_w", "rw_lnx_b")]
    arr["pair_params"] = np.stack(prm, 2)
    arr["lora_mu"] = mu[:, T_LW:]
    lora = np.zeros((PAIRS, P, 3, P), np.float32)
    for i, (k, rows) in enumerate((("rw_w2", LORA_W), ("rw_a2", LORA_A), ("rw_g2", LORA_G))):
        lora[:, :rows, i, :] = w1[k].reshape(rows, PAIRS, P).transpose(1, 0, 2)
    lora[:, LORA_W, 0, :] = w1["rw_w0"].reshape(PAIRS, P)
    arr["lora"] = lora
    arr["shift_prev"] = rw_tiles(w1["state_shift"]).reshape(DB, RW_T, P).transpose(2, 1, 0)
    arr["state_s"] = w1["state_wkv"].reshape(DB, PAIRS, 2, HD, HD).transpose(1, 2, 4, 0, 3).reshape(PAIRS, P, DB, HD)
    arr["cache_k"] = w1["cache_k"].transpose(0, 2, 3, 1)
    arr["cache_v"] = w1["cache_v"].transpose(0, 2, 1, 3)
    arr["cache_kidx"] = w1["cache_kidx"].transpose(0, 2, 1)
    arr["page_table"] = x["page_table"].reshape(1, -1)
    arr["conv_params"] = np.stack([tiles_of(w1["conv_w"][0]), tiles_of(w1["conv_w"][1]), tiles_of(w1["conv_w"][2]),
                                   tiles_of(w1["conv_b"])], 2)
    arr["conv_prev"] = w1["state_conv"].reshape(2 * DB, FT, P).transpose(2, 1, 0)

    nc = bacc.Bacc("TRN2", target_bir_lowering=False, num_devices=1)
    arr = {f"in_{k}": np.ascontiguousarray(v) for k, v in arr.items()}
    a = {k[3:]: nc.dram_tensor(k, v.shape, mybir.dt.from_np(v.dtype), kind="ExternalInput").ap() for k, v in arr.items()}
    o = {k: nc.dram_tensor(f"out_{k}", shape, F32, kind="ExternalOutput").ap() for k, shape in OUTS.items()}
    build(nc, a, o)
    r = run_bass_kernel_spmd(nc, [arr], core_ids=[0]).results[0]
    r = {k: np.asarray(r[f"out_{k}"]) for k in OUTS}

    def tok(z):
        return z.transpose(2, 1, 0).reshape(z.shape[2], -1)

    y, k, v = tok(r["y"]), tok(r["k"]), tok(r["v"])
    ki = r["ki"].T
    pages = SEQ // PAGE
    sh = tok(r["shift"])
    o3 = 3 * RW_WIDTH
    sh = np.concatenate([sh[:, :o3 + 96], sh[:, o3 + 128:o3 + 224], sh[:, o3 + 256:]], 1)
    cv = tok(r["conv"])
    wp = r["wkv_p"].reshape(HEADS_RW, HD, HD).transpose(0, 2, 1)
    ws = r["wkv_s"].reshape(PAIRS, 2, HD, DB, HD).transpose(3, 0, 1, 4, 2).reshape(DB, HEADS_RW, HD, HD)
    c = np.ascontiguousarray
    return (c(y[:SEQ][None]), c(y[SEQ:].reshape(DB, DS, D_MODEL)),
            c(k[:SEQ].reshape(1, 1, pages, PAGE, KVH, HDIM)), c(v[:SEQ].reshape(1, 1, pages, PAGE, KVH, HDIM)),
            c(ki[:SEQ].reshape(1, 1, pages, PAGE, ID)), c(k[SEQ:].reshape(1, DB, DS, KVH, HDIM)),
            c(v[SEQ:].reshape(1, DB, DS, KVH, HDIM)), c(ki[SEQ:].reshape(1, DB, DS, ID)),
            c(wp[None, None]), c(ws[None]), c(sh[:1][None]), c(sh[1:][None]),
            c(cv[:2].reshape(1, 1, 2, D_FF)), c(cv[2:].reshape(1, DB, 2, D_FF)))
```

```python
from contextlib import ExitStack

import numpy as np
import concourse.bass as bass
from concourse import mybir

F32 = mybir.dt.float32
F32R = mybir.dt.float32r
I32 = mybir.dt.int32
ALU = mybir.AluOpType
ACT = mybir.ActivationFunctionType
AX = mybir.AxisListType

P = 128
D_MODEL = 2048
SEQ = 256
DB, DS = 8, 4
NS = DB * DS
N = SEQ + NS
PAST = 256
PAGE = 128
HEADS_RW, HD = 16, 64
RW_WIDTH = HEADS_RW * HD
LORA_W, LORA_A, LORA_G = 96, 96, 128
RW_COLS = 3 * RW_WIDTH + LORA_W + LORA_A + LORA_G
GN_EPS = 64e-5
AH, KVH, HDIM = 8, 2, 128
IH, ID = 16, 64
IDX_SCALE = (IH * ID) ** -0.5
TOPK_P = min(256, SEQ // 4)
TOPK_S = min(256, (PAST + DS) // 4)
ROPE_THETA = 10000.0
D_FF = 5632
RMS_EPS = 1e-6
DECAY_SCALE = -float(np.exp(-0.5))

KT = D_MODEL // P
FT = D_FF // P
RW_T = 27
ATT_T = 21
PAIRS = RW_WIDTH // P
E = 1 + SEQ + DB * (1 + DS)
TE = E - 1
T_LW, T_LA, T_LG = 24, 25, 26
T_Q, T_K, T_V, T_QI, T_KI = 27, 35, 37, 39, 47
FIRST_COLS = 24
WI_ROW = 96
CH = 64
NCH = SEQ // CH
KEYS_S = PAST + DS
N_POOL = 20
BIGNEG = -1e30
MARK = -3e38
DK = 11
DU = FT // DK
GE = 2 + SEQ + DB * (2 + DS)
CE = GE - 2

U_IN = 0
U_GATE = U_IN + RW_T + ATT_T
U_P = U_GATE + 2 * KT
U_O = U_P + KT
U_UP = U_O + KT
U_DOWN = U_UP + 2 * FT


def constants():
    c = {}
    i = np.arange(P)
    eye = np.eye(P, dtype=np.float32)

    def blk(n):
        return (i[:, None] // n == i[None, :] // n)

    up, upi, low = i[:, None] < i[None, :], i[:, None] <= i[None, :], i[:, None] > i[None, :]
    c["ident"] = eye
    c["mean_ones"] = np.full((P, P), 1.0 / D_MODEL)
    c["head_ones"] = blk(HD)
    c["tri_incl"] = (blk(CH) & upi) * (0.5 * DECAY_SCALE)
    c["tri_excl"] = (blk(CH) & up) * (0.5 * DECAY_SCALE)
    c["m_ab"] = np.concatenate([blk(CH) & up, blk(CH) & upi], 1)
    c["m16u"] = blk(16) & up
    c["m16l"] = blk(16) & low
    c["m32l"] = blk(32) & ~blk(16) & low
    c["m64l"] = blk(64) & ~blk(32) & low
    s = slice(0, NS)
    b4 = blk(DS)
    small = np.zeros((P, 4 * NS + NS + DB))
    small[s, 0:NS] = (b4 & up)[s, s]
    small[s, NS:2 * NS] = (b4 & upi)[s, s]
    small[s, 2 * NS:3 * NS] = (b4 & low)[s, s]
    small[s, 3 * NS:4 * NS] = (b4 & upi)[s, s] * (0.5 * DECAY_SCALE)
    small[s, 4 * NS:5 * NS] = (b4 & up)[s, s] * (0.5 * DECAY_SCALE)
    small[s, 5 * NS:] = np.arange(NS)[:, None] // DS == np.arange(DB)[None, :]
    c["small"] = small
    main = np.concatenate([np.asarray(v, np.float32) for v in c.values()], 1)
    at, o = {}, 0
    for k, v in c.items():
        at[k] = (o, v.shape[1])
        o += v.shape[1]

    a = {}
    rot = np.zeros((P, P))
    for m in range(P):
        rot[(m + 64) % P, m] = -1.0 if m < 64 else 1.0
    a["rot_head"] = rot
    rot = np.zeros((P, P))
    for m in range(P):
        base, r = m // 64 * 64, m % 64
        rot[base + (r + 32) % 64, m] = -1.0 if r < 32 else 1.0
    a["rot_idx"] = rot
    pos = np.zeros(TE, np.float32)
    pos[:SEQ] = np.arange(SEQ)
    for b in range(DB):
        for t in range(DS):
            pos[SEQ + 5 * b + 1 + t] = PAST + t
    for name, half in (("head", HDIM // 2), ("idx", ID // 2)):
        inv = (1.0 / (np.float32(ROPE_THETA) ** (np.arange(half, dtype=np.float32) / np.float32(half)))).astype(np.float32)
        ang = (pos[None, :] * inv[i % half][:, None]).astype(np.float32).astype(np.float64)
        a["cos_" + name] = np.cos(ang)
        a["sin_" + name] = np.sin(ang)
    row = np.arange(P)
    r_par, r_b2, r_h, r_t = row // 64, row // 32 % 2, row // 4 % 8, row % 4
    sel = np.zeros((P, P))
    sel[WI_ROW + 2 * r_h + r_par, row] = IDX_SCALE
    a["sel_head"] = sel
    q = np.arange(NS)
    a["m_query"] = np.stack([(q[None, :] == (2 * c4 + r_b2[:, None]) * DS + r_t[:, None]) for c4 in range(4)], 1).reshape(P, -1)
    selq = np.zeros((P, 2, P))
    for half in range(2):
        selq[(4 * half + row // 32) * DS + row % 4, half, row] = 1.0
    a["sel_query"] = selq.reshape(P, -1)
    k = np.arange(SEQ)
    a["causal"] = np.stack([np.where(k[None, :] <= (qt * P + i)[:, None], 0.0, BIGNEG) for qt in range(2)], 1).reshape(P, -1)
    ks = np.arange(KEYS_S)
    a["causal_s"] = np.where(ks[None, :] <= PAST + (i % DS)[:, None], 0.0, BIGNEG)
    att = np.concatenate([np.asarray(v, np.float32) for v in a.values()], 1)
    ata, o = {}, 0
    for kx, v in a.items():
        ata[kx] = (o, v.shape[1])
        o += v.shape[1]
    return main, at, att, ata


MAIN_C, MAIN_AT, ATT_C, ATT_AT = constants()

ROPE_TILES = [T_KI] + [T_QI + i for i in range(8)] + [T_K, T_K + 1] + [T_Q + i for i in range(8)]
ATT_STEPS = [("sample", 0), (0, 0), (0, 1), (1, 0), (1, 1), ("sample", 1)]
PAIR_STEPS = 19
UP_STEPS = 6
POOL_LOADS_FROM = 13
FILL_FIRST = 14
FILL_ROPE, FILL_TOPK_S, FILL_DOTS, FILL_TOPK, FILL_SCORES, FILL_SOFTMAX, FILL_P_T = 4,24,2,64,8,8,10

(PR_MUR, PR_MUK, PR_MUV, PR_A0H, PR_KK, PR_KA, PR_RK, PR_LW, PR_LB, NPRM) = range(10)



class Steps:

    def __init__(self, eng, sem):
        self.eng, self.sem, self.n, self.base = eng, sem, 0, 0

    def mark(self, ins):
        ins.then_inc(self.sem, 1)
        self.n += 1

    def sync(self):
        self.eng.wait_ge(self.sem, self.base + self.n)

    def done(self, ins):
        self.mark(ins)
        self.sync()

    def repeat(self, count, per, body, first=0):
        start = self.base + self.n
        with self.eng.Fori(first, count) as i:
            self.base, self.n = i * per + (start - first * per), 0
            body(i)
            assert self.n == per, (self.n, per)
        self.base, self.n = start + (count - first) * per, 0


def rows_of(x):
    return x.rearrange("o p f -> (o p) f")


def step(x):
    return x.rearrange("p o f -> p (o f)")


def samples(x, width):
    return x.rearrange("p (b f) -> p b f", f=width)[:, :, width - DS:width]


def by_request(x):
    return x.rearrange("p (b t) -> p b t", t=DS)


def spread(x, axis, shape):
    return x.unsqueeze(axis).broadcast_to(shape)


def build(nc, a, o):
    start = (nc.sbuf_base + 31) // 32 * 32
    end = nc.sbuf_usable_end // 32 * 32

    def size_of(shape):
        return (4 * int(np.prod(shape[1:])) + 31) // 32 * 32

    def region(offset):
        def take(name, shape, dt=F32):
            t = nc.alloc_sbuf_tensor_at(name, shape, dt, offset=take.at)
            take.at += size_of(shape)
            assert take.at <= end, (name, take.at - end)
            return t
        take.at = offset
        return take

    m = region(start)
    MC = m("main_consts", [P, MAIN_C.shape[1]])
    PRM_ALL = m("pair_params_all", [P, PAIRS, NPRM])
    LMU = m("lora_mu", [P, 3])
    NORMS = m("norm_gains", [P, 3, KT])
    CONVP = m("conv_params", [P, FT, 4])
    PTAB = m("page_table", [1, 2 * DB], I32)
    WRAW = m("w_raw", [P, 2, KT, P])
    WHI = m("w_hi", [P, 2, KT, P], F32R)
    WLO = m("w_lo", [P, 2, KT, P], F32R)
    xn_at = m.at
    XN = m("x_split", [P, 2, KT, N], F32R)
    big = m.at

    m = region(big)
    XRAW = m("x_raw", [P, KT, N])
    SQ = m("squares", [P, 2, N])
    RSTD = m("rstd", [P, N])
    m = region(big)
    COLS = m("cols", [P, RW_T + ATT_T, E])
    AC = m("att_consts", [P, ATT_C.shape[1]])
    SHP = m("shift_prev", [P, RW_T, DB])
    SHO = m("shift_out", [P, RW_T, 1 + DB])
    RT = m("rope_tmp", [P, 2, TE])
    KC = m("k_cache", [P, 4, KVH, PAST])
    VC = m("v_cache", [P, 4, 2, KVH * HDIM])
    KIC = m("ki_cache", [P, DB, PAST])
    BIASP = m("bias_prompt", [P, 2, SEQ])
    BIASS = m("bias_sample", [NS, KEYS_S])
    VNEW = m("v_new", [DS, 4, KVH * HDIM])
    QIS = m("qi_sample", [P, DB, 8, DS])
    WM = m("w_mix", [P, 4, NS])
    WI = m("w_idx", [P, 2, IH])
    M8 = m("max8", [P, 8])
    ST8 = m("softmax_stats", [P, 16])
    QZ = m("q_grouped", [P, KVH, 4, AH, DS])
    sel_at = m.at
    ACC = m("scores", [P, 2, SEQ])
    ACS = m("scores_s", [NS, KEYS_S])
    RELU = m("relu", [P, 2, 2 * SEQ + 16])
    m = region(sel_at)
    PROB = m("prob", [P, 4 * SEQ])
    PRT = m("prob_t", [P, 2 * 4 * P])
    VTOK = m("v_tok", [P, 2, KVH * HDIM])
    m = region(big + (4 * (RW_T + 8) * E + 31) // 32 * 32)
    GATES = m("gates", [P, 2 * KT, N])
    r0 = m.at
    m = region(r0)
    DIFF = m("diff", [P, 3, TE])
    RKV = m("rkv", [P, 3, N])
    KKN = m("kk_unit", [P, N])
    AG = m("a_gate", [P, N])
    KP = m("k_mixed", [P, N])
    SQK = m("squares_k", [P, N])
    LDT = m("decay_tok", [P, 3, P])
    r_end = m.at
    m = region(r0)
    PEXP = m("decay_exp", [P, 3, N])
    m = region(r0)
    U1 = m("u1", [P, 4, P])
    L1 = m("l1", [P, 4, P])
    U2 = m("u2", [P, 4, P])
    L2 = m("l2", [P, 4, P])
    TT = m("t_inv", [P, 4, P])
    ML = m("m_low", [P, 4, P])
    m = region(r0)
    UM = m("u_by_request", [NS, 2, DB * HD])
    VM = m("v_by_request", [NS, 2, DB * HD])
    m = region(r_end)
    AR = m("ar", [P, 2, 2, P])
    ARS = m("ar_s", [P, 2, NS])
    BT = m("b_t", [P, N])
    KTL = m("k_t", [P, N])
    TOK = m("tok", [P, 2, 3 * P])
    TOKS = m("tok_s", [NS, 3 * P])
    MB = m("mat_b", [P, 2, 2, 2 * P])
    MK = m("mat_k", [P, 2, 2, 2 * P])
    LORA = m("lora", [P, 3, P])
    SIN = m("state_s", [P, DB, HD])
    STT = m("state", [P, P])
    YS = nc.alloc_sbuf_tensor_at("y", [P, N], F32, offset=m.at)
    STP = m("state_decayed", [P, P])
    RR = m("rhs", [P, P])
    UU = m("u", [P, P])
    MBS = m("mat_b_s", [NS, 2, 2 * NS])
    MKS = m("mat_k_s", [NS, 2, 2 * NS])
    MLS = m("m_low_s", [NS, 2, NS])
    TS = m("t_inv_s", [NS, 2, NS])
    L2S = m("l2_s", [NS, 2, NS])
    SPR = m("state_prod", [P, 2, NS])
    RS = m("rhs_s", [NS, P])
    US = m("u_s", [NS, P])
    PRM = m("pair_params", [P, NPRM])
    PRM_LN = m("pair_params_ln", [P, 2])
    ROOT = m("table_of", [P, 2])
    PC = m("chunk_decay", [P, NCH + DB])
    YQ = m("y_sq", [P, N])
    m = region(big)
    XM = m("merged_split", [P, 2, KT, N], F32R)
    m = region(big)
    HN = m("h_normed", [P, KT, N])
    m = region(r0)
    H = m("h", [P, KT, N])
    MG = m("merge_tmp", [P, 4, N])
    HSQ = m("h_squares", [P, 2, N])
    HRSTD = m("h_rstd", [P, N])
    m = region(big)
    XF = m("act_split", [P, 2, FT, N], F32R)
    CPREV = m("conv_prev", [P, FT, 2 * DB])
    COUT = m("conv_out", [P, FT, 2 + 2 * DB])
    GX = m("gate_ext", [P, 2, GE])
    CV = m("conv", [P, 2, 2, CE])
    m = region(xn_at)
    H2 = m("h2", [P, KT, N])
    YO = m("y_out", [P, KT, N])
    m = region(big + size_of([P, 2 * FT, N]))
    FSQ = m("f_squares", [P, 2, N])
    FRSTD = m("f_rstd", [P, N])

    def cst(name, rows=P):
        off, w = MAIN_AT[name]
        return MC[0:rows, off:off + w]

    def acst(name, rows=P):
        off, w = ATT_AT[name]
        return AC[0:rows, off:off + w]

    ident, mean_ones, head_ones = cst("ident"), cst("mean_ones"), cst("head_ones")
    tri_incl, tri_excl = cst("tri_incl"), cst("tri_excl")
    m_ab, m16u, m16l, m32l, m64l = (cst(x) for x in ("m_ab", "m16u", "m16l", "m32l", "m64l"))
    small = cst("small", NS)
    ms_ab, ms_l = small[:, 0:2 * NS], small[:, 2 * NS:3 * NS]
    tris_incl, tris_excl = small[:, 3 * NS:4 * NS], small[:, 4 * NS:5 * NS]
    ms_req = small[:, 5 * NS:5 * NS + DB]

    h_spill = nc.dram_tensor("h_spill", [P, KT * N], F32, kind="Internal").ap()

    with ExitStack() as ctx:
        BK = [ctx.enter_context(nc.psum_tensor(f"bank{i}", [P, 512], F32)) for i in range(8)]
        sems = {}

        def sem(name):
            if name not in sems:
                sems[name] = ctx.enter_context(nc.semaphore(name))
            return sems[name]

        block = ctx.enter_context(nc.Block())
        mm, tr = nc.tensor.matmul, nc.tensor.transpose
        actv = nc.scalar.activation
        V = nc.vector
        FORI_UP, FORI_P = FT // 2, KT // 4

        colsv = COLS[:].rearrange("p (g j) e -> p g j e", j=4)
        rwv = COLS[:, 0:24, :].rearrange("p (j h) e -> p j h e", j=3)
        gatesv = GATES[:].rearrange("p (g j) n -> p g j n", j=4)

        @block.sync
        def _(sp):
            for i in range(4):
                sp.dma_start(XRAW[:, 4 * i:4 * i + 4, :], a["x"][:, 4 * i:4 * i + 4, :]).then_inc(sem(f"x_in{i}"), 16)
                if i == 0:
                    sp.dma_start(MC[:], a["main_c"]).then_inc(sem("main_c_in"), 16)
            sp.dma_start(NORMS[:], a["norms"]).then_inc(sem("norms_in"), 16)

            def load(n, slot, src, kt=KT):
                if not isinstance(n, int) or n >= 2:
                    sp.wait_ge(sem("w_split"), n - 1)
                dst = WRAW[:, slot, 0:kt, :].rearrange("p k c -> p (k c)")
                sp.dma_start(dst, src).then_inc(sem(f"w_in{slot}"), 16)

            def section(name, u0, count, per, kt=KT):
                src = a[name].rearrange("(g j) p f -> g j p f", j=per)
                def body(g):
                    for j in range(per):
                        one = src[g, j] if isinstance(g, int) else rows_of(src[bass.ds(g, 1), j])
                        load(g * per + (u0 + j), j % 2, one, kt)
                if u0 == 0:
                    body(0)
                with sp.Fori(1 if u0 == 0 else 0, count // per) as g:
                    body(g)

            section("w_in", U_IN, RW_T + ATT_T, 4)
            section("w_gate", U_GATE, 2 * KT, 4)
            section("w_p", U_P, KT, 4)
            section("w_o", U_O, KT, 4)
            section("w_up", U_UP, 2 * FT, 4)
            section("w_down", U_DOWN, KT * DU, 8, DK)
            sp.wait_ge(sem("att_out"), 16 * 4)
            sp.wait_ge(sem("sout_done"), 16 * PAIRS)
            sp.wait_ge(sem("stout_done"), 32 * PAIRS)
            sp.wait_ge(sem("out_done"), 16 * 5)

        def settle(eng):
            eng.wait_ge(sem("x_split"), 4)

        def mix_scores(pe, c):
            pe.wait_ge(sem("relu"), c + 1)
            mm(BK[6][0:NS, 0:KEYS_S], WM[:, c, :], RELU[:, c % 2, 0:KEYS_S], start=c == 0,
               stop=c == 3).then_inc(sem("mixed"), 1)

        def n_ge2(n):
            return not isinstance(n, int) or n >= 2

        def split_lo(eng, n, slot, kt=KT):
            eng.wait_ge(sem("w_hi"), n + 1)
            eng.tensor_tensor(WLO[:, slot, 0:kt], WRAW[:, slot, 0:kt], WHI[:, slot, 0:kt].bitcast(F32),
                             ALU.subtract).then_inc(sem("w_split"), 1)

        def split_hi(act, n, slot, kt=KT):
            act.wait_ge(sem(f"w_in{slot}"), unit_landed(n, slot))
            if n_ge2(n):
                act.wait_ge(sem("unit_done"), n - 1)
            actv(WHI[:, slot, 0:kt], WRAW[:, slot, 0:kt], ACT.Copy).then_inc(sem("w_hi"), 1)

        def unit_landed(n, slot):
            return (n - slot) * 8 + 16

        @block.tensor
        def _(pe):
            def norm_sum(k, t, slot, squares):
                pe.wait_ge(sem("norm_sq"), t + (KT * k + 1))
                mm(BK[2][:, 0:N], mean_ones, squares[:, slot, :], start=isinstance(t, int) and t == 0, stop=True,
                   skip_group_check=True).then_inc(sem("norm_sq_used"), 1)

            def blocks(n, slot, ks, out, rhs, first=True, last=True, k_from=0, split_from=None):
                for k in ks:
                    if split_from is not None and k % 4 == 0:
                        pe.wait_ge(sem("x_split"), split_from + k // 4 + 1)
                    hi, lo, w, wl = rhs[:, 0, k_from + k], rhs[:, 1, k_from + k], WHI[:, slot, k], WLO[:, slot, k]
                    mm(out, wl, hi, start=first and k == ks[0], stop=False, skip_group_check=True)
                    mm(out, w, lo, start=False, stop=False, skip_group_check=True)
                    ins = mm(out, w, hi, start=False, stop=last and k == ks[-1], skip_group_check=True)
                return ins

            pe.wait_ge(sem("main_c_in"), 16)
            for t in range(KT):
                norm_sum(0, t, t % 2, SQ)

            def in_units(g):
                for j in range(4):
                    n = g * 4 + j
                    pe.wait_ge(sem("w_split"), n + 1)
                    if n_ge2(n):
                        pe.wait_ge(sem("unit_out"), n - 1)
                    blocks(n, j % 2, range(KT), BK[j % 2][:, 0:N], XN,
                           split_from=0 if isinstance(g, int) and j == 0 else None).then_inc(sem("unit_done"), 1)
            in_units(0)
            with pe.Fori(1, FIRST_COLS // 4) as g:
                in_units(g)

            made = [0]

            def fill(count):
                while count and made[0] < FIRST_COLS * KT:
                    j, k = divmod(made[0], KT)
                    todo = min(count, KT - k)
                    n = FIRST_COLS + j
                    if k == 0:
                        pe.wait_ge(sem("w_split"), n + 1)
                        pe.wait_ge(sem("unit_out"), n - 1)
                    ins = blocks(n, j % 2, range(k, k + todo), BK[j % 2][:, 0:N], XN, k == 0, k + todo == KT)
                    if k + todo == KT:
                        ins.then_inc(sem("unit_done"), 1)
                    made[0] += todo
                    count -= todo
            fill_cols = fill

            pe.wait_ge(sem("att_c_in"), 16)
            pe.wait_ge(sem("unit_out"), FIRST_COLS)
            pe.wait_ge(sem("slots"), 1)
            for i, t in enumerate(ROPE_TILES):
                if i >= 2:
                    pe.wait_ge(sem("rot_used"), i - 1)
                rot = acst("rot_head") if t < T_V else acst("rot_idx")
                mm(BK[2 + i % 2][:, 0:TE], rot, COLS[:, t, 1:E], start=True, stop=True).then_inc(sem("rot"), 1)
                fill(FILL_ROPE)
            for qt in range(2):
                ins = tr(BK[4][:, qt * P:(qt + 1) * P], COLS[:, T_LW, 1 + qt * P:1 + (qt + 1) * P], ident)
            ins.then_inc(sem("wi_t"), 1)
            mm(BK[5][:, 0:NS], acst("sel_head"), samples(COLS[:, T_LW, 1 + SEQ:E], 5), start=True,
               stop=True).then_inc(sem("wi_rows"), 1)
            pe.wait_ge(sem("roped"), len(ROPE_TILES))
            pe.wait_ge(sem("ki_in"), 16 * 2 * 2 * DB)
            for c in range(4):
                if c == 1:
                    pe.wait_ge(sem("wi_sb"), 1)
                    pe.wait_ge(sem("w_mix"), 1)
                if c >= 2:
                    pe.wait_ge(sem("relu"), c - 1)
                for b2 in range(2):
                    b = 2 * c + b2
                    for par in range(2):
                        r = slice(64 * par, 64 * par + 64)
                        out = BK[2 + c % 2 * 2][64 * par + 32 * b2:64 * par + 32 * b2 + 32]
                        q = QIS[r, b].rearrange("p h t -> p (h t)")
                        mm(out[:, 0:PAST], q, KIC[r, b, :], start=True, stop=True)
                        ins = mm(out[:, PAST:KEYS_S], q, COLS[r, T_KI, SEQ + DS * b:SEQ + DS * b + DS],
                                 start=True, stop=True)
                ins.then_inc(sem("dots"), 1)
                if c >= 1:
                    mix_scores(pe, c - 1)
            mix_scores(pe, 3)
            fill(FILL_TOPK_S)
            for n in range(4, 20):
                qt, i = divmod(n - 4, 8)
                pe.wait_ge(sem("relu"), n - 1)
                for par in range(2):
                    r = slice(64 * par, 64 * par + 64)
                    ins = mm(BK[2 + n % 2 * 2 + par][:, 0:SEQ], COLS[r, T_QI + i, qt * P:(qt + 1) * P],
                             COLS[r, T_KI, 0:SEQ], start=True, stop=True)
                ins.then_inc(sem("dots"), 1)
                fill(FILL_DOTS)
            pe.wait_ge(sem("v_compact"), 1)
            pe.wait_ge(sem("relu"), 20)
            for kc in range(2):
                for g in range(KVH):
                    ins = tr(BK[4][:, (kc * KVH + g) * P:(kc * KVH + g + 1) * P], RT[:, g, kc * P:(kc + 1) * P], ident)
            ins.then_inc(sem("v_t"), 1)
            fill(FILL_TOPK)

            def sample_scores(half):
                pe.wait_ge(sem("bias_ready"), 1)
                pe.wait_ge(sem("q_grouped"), half + 1)
                pe.wait_ge(sem("kv_in"), 16 * 32 * (half + 1))
                mm(BK[7][:, 0:KEYS_S], acst("sel_query", NS)[:, half * P:(half + 1) * P], BIASS[:], start=True, stop=False,
                   skip_group_check=True)
                for b in range(4):
                    out = BK[7][32 * b:32 * b + 32]
                    for g in range(KVH):
                        q = QZ[:, g, b].rearrange("p h t -> p (h t)")
                        c0 = SEQ + DS * (4 * half + b)
                        mm(out[:, 0:PAST], q, KC[:, b, g, :], start=False, stop=False, skip_group_check=True)
                        ins = mm(out[:, PAST:KEYS_S], q, COLS[:, T_K + g, c0:c0 + DS], start=False, stop=g == 1,
                                 skip_group_check=True)
                ins.then_inc(sem("s_mm"), 1)
                if half:
                    pe.wait_ge(sem("s_used"), 4)
                for b in range(4):
                    for g in range(KVH):
                        c0 = SEQ + DS * (4 * half + b)
                        i = b * KVH + g
                        ins = tr(BK[2 + i // 4][0:DS, i % 4 * P:(i % 4 + 1) * P], RT[:, g, c0:c0 + DS], ident)
                ins.then_inc(sem("v_new_t"), 1)

            def sample_step(n, half):
                pe.wait_ge(sem("prob"), n + 1)
                if half:
                    pe.wait_ge(sem("p_sb"), n)
                else:
                    pe.wait_ge(sem("v_tok"), 1)
                tr(BK[4][:, 0:P], PROB[:, 0:P], ident)
                tr(BK[4][:, P:2 * P], PROB[:, P:2 * P], ident)
                tr(BK[4][0:DS, 2 * P:3 * P], PROB[:, 2 * P:KEYS_S], ident).then_inc(sem("p_t"), 1)
                fill(FILL_P_T)
                pe.wait_ge(sem("p_sb"), n + 1)
                pe.wait_ge(sem("v_new"), half + 1)
                if n:
                    pe.wait_ge(sem("o_sb"), n)
                for b in range(4):
                    for g in range(KVH):
                        out = BK[6][:, (b * KVH + g) * 16:(b * KVH + g + 1) * 16]
                        c0 = b * 32 + g * 16
                        for kc in range(2):
                            mm(out, VC[:, b, kc, g * P:(g + 1) * P], PRT[:, kc * P + c0:kc * P + c0 + 16],
                               start=kc == 0, stop=False)
                        ins = mm(out, VNEW[:, b, g * P:(g + 1) * P], PRT[0:DS, 2 * P + c0:2 * P + c0 + 16],
                                 start=False, stop=True)
                ins.then_inc(sem("pv"), 1)

            def prompt_scores(p, qt, g):
                if p:
                    pe.wait_ge(sem("s_used"), p)
                else:
                    pe.wait_ge(sem("v_new"), 1)
                for r in range(4):
                    ins = mm(BK[2 + r // 2][:, r % 2 * SEQ:(r % 2 + 1) * SEQ],
                             COLS[:, T_Q + 4 * g + r, qt * P:(qt + 1) * P], COLS[:, T_K + g, 0:SEQ],
                             start=True, stop=True)
                ins.then_inc(sem("s_mm"), 1)

            def prompt_step(n, g):
                pe.wait_ge(sem("prob"), n + 1)
                for kc in range(2):
                    for r in range(4):
                        ins = tr(BK[4 + kc][:, r * P:(r + 1) * P], PROB[:, r * SEQ + kc * P:r * SEQ + (kc + 1) * P], ident)
                ins.then_inc(sem("p_t"), 1)
                fill(FILL_P_T)
                pe.wait_ge(sem("p_sb"), n + 1)
                pe.wait_ge(sem("p_sb2"), n)
                pe.wait_ge(sem("o_sb"), n)
                for kc in range(2):
                    ins = mm(BK[6][:], VTOK[:, kc, g * P:(g + 1) * P], PRT[:, kc * 512:(kc + 1) * 512],
                             start=kc == 0, stop=kc == 1)
                ins.then_inc(sem("pv"), 1)

            def scores(n):
                if ATT_STEPS[n][0] == "sample":
                    sample_scores(ATT_STEPS[n][1])
                else:
                    prompt_scores(n - 1, *ATT_STEPS[n])
            scores(0)
            for n, (kind, which) in enumerate(ATT_STEPS):
                fill(FILL_SCORES)
                if n < 4:
                    scores(n + 1)
                fill(FILL_SOFTMAX)
                if kind == "sample":
                    sample_step(n, which)
                else:
                    prompt_step(n, which)
                if n == 4:
                    scores(5)

            halves = [slice(0, 64), slice(64, 128)]

            def lora_za(v):
                pe.wait_ge(sem("lora_in"), v * 16)
                lw = COLS[:, T_LW]
                for tt in range(2):
                    mm(BK[2][:, tt * P:(tt + 1) * P], lw[0:97, tt * P:(tt + 1) * P], LORA[0:97, 0, :], start=True, stop=True)
                mm(BK[2][0:NS, 2 * P:3 * P], lw[0:97, SEQ:N], LORA[0:97, 0, :], start=True,
                   stop=True).then_inc(sem("z_mm"), 1)
                mm(BK[3][:, 0:N], LORA[0:LORA_A, 1, :], COLS[0:LORA_A, T_LA, 0:N], start=True,
                   stop=True).then_inc(sem("a_mm"), 1)

            def lora_g(v):
                mm(BK[6][:, 0:N], LORA[:, 2, :], COLS[:, T_LG, 0:N], start=True, stop=True).then_inc(sem("g_mm"), 1)

            def kk_sum(v):
                pe.wait_ge(sem("kk_sq"), v)
                mm(BK[4][:, 0:N], head_ones, SQK[:], start=True, stop=True).then_inc(sem("kk_sum"), 1)

            def log_decay(v):
                pe.wait_ge(sem("decay_tok"), v)
                pe.wait_ge(sem("g_sb"), v)
                for bank, tri, tris in ((5, tri_incl, tris_incl), (6, tri_excl, tris_excl)):
                    for tt in range(2):
                        mm(BK[bank][:, tt * P:(tt + 1) * P], LDT[:, tt, :], tri, start=True, stop=True)
                    ins = mm(BK[bank][:, SEQ:N], LDT[0:NS, 2, :], tris, start=True, stop=True)
                ins.then_inc(sem("log_decay"), 1)

            def bonus_mm(v):
                pe.wait_ge(sem("rkr"), v)
                mm(BK[4][:, 0:N], head_ones, SQK[:], start=True, stop=True).then_inc(sem("bonus_mm"), 1)

            def pair(it, last=False):
                pos = [0]

                def fill(count):
                    while count:
                        j, k = divmod(pos[0], KT)
                        todo = min(count, KT - k)
                        n = it * 4 + (U_GATE + j)
                        if k == 0:
                            pe.wait_ge(sem("w_split"), n + 1)
                            pe.wait_ge(sem("unit_out"), n - 1)
                        ins = blocks(n, j % 2, range(k, k + todo), BK[j % 2][:, 0:N], XN, k == 0, k + todo == KT)
                        if k + todo == KT:
                            ins.then_inc(sem("unit_done"), 1)
                        pos[0] += todo
                        count -= todo

                v = it + 1
                fill(4)
                pe.wait_ge(sem("ar_ready"), v)
                for w, src in enumerate((BT, KTL, RKV[:, 2, :])):
                    for tt in range(2):
                        tr(BK[2 + tt][:, w * P:(w + 1) * P], src[:, tt * P:(tt + 1) * P], ident)
                    ins = tr(BK[7][0:NS, w * P:(w + 1) * P], src[:, SEQ:N], ident)
                ins.then_inc(sem("tok_mm"), 1)
                for tt in range(2):
                    for e, h in enumerate(halves):
                        ins = mm(BK[5 + e][:, tt * SEQ:(tt + 1) * SEQ], BT[h, tt * P:(tt + 1) * P],
                                 AR[h, tt].rearrange("p x n -> p (x n)"), start=True, stop=True)
                ins.then_inc(sem("b_mm"), 1)
                fill(4)
                pe.wait_ge(sem("bonus"), v)
                pe.wait_ge(sem("tok_sb"), v)

                def half_mm(e, h):
                    for tt in range(2):
                        mm(BK[4][:, (tt * 2 + e) * P:(tt * 2 + e + 1) * P], AR[h, tt, 0, :], BT[h, tt * P:(tt + 1) * P],
                           start=True, stop=True)
                    ars = ARS[h].rearrange("p x n -> p (x n)")
                    mm(BK[7][0:NS, e * 64:e * 64 + 64], BT[h, SEQ:N], ars, start=True, stop=True)
                    mm(BK[7][0:NS, 128 + e * 64:192 + e * 64], KTL[h, SEQ:N], ars, start=True, stop=True)
                    return mm(BK[7][0:NS, 256 + e * 32:288 + e * 32], ARS[h, 0, :], BT[h, SEQ:N], start=True, stop=True)
                half_mm(0, halves[0]).then_inc(sem("head0_mm"), 1)
                for tt in range(2):
                    for e, h in enumerate(halves):
                        mm(BK[2 + e][:, tt * SEQ:(tt + 1) * SEQ], KTL[h, tt * P:(tt + 1) * P],
                           AR[h, tt].rearrange("p x n -> p (x n)"), start=True, stop=True)
                pe.wait_ge(sem("head0_mm"), v)
                ins = half_mm(1, halves[1])
                ins.then_inc(sem("k_mm"), 1)
                fill(3)

                def four(bank, lhs, rhs):
                    for u in range(4):
                        ins = mm(BK[bank][:, u * P:(u + 1) * P], lhs[:, u], rhs[:, u], start=True, stop=True)
                    return ins

                settle(pe)
                pe.wait_ge(sem("block16"), v)
                four(5, L1, U1)
                four(6, U1, L1).then_inc(sem("inv_mm"), 1)
                settle(pe)
                pe.wait_ge(sem("mats"), v)
                for e in range(2):
                    ins = mm(BK[7][0:NS, e * 32:e * 32 + 32], MBS[:, e, 0:NS], MLS[:, e, :], start=True, stop=True)
                ins.then_inc(sem("l2s_mm"), 1)
                fill(4)
                pe.wait_ge(sem("inv_u"), v * 5 - 4)
                pe.wait_ge(sem("inv_l"), v * 8 - 7)
                four(4, L2, U2)
                four(2, U2, L2)
                four(3, L2, TT).then_inc(sem("inv_mm"), 1)
                settle(pe)
                pe.wait_ge(sem("l2s"), v)
                for e in range(2):
                    ins = mm(BK[7][0:NS, 64 + e * 32:96 + e * 32], L2S[:, e, :], TS[:, e, :], start=True, stop=True)
                ins.then_inc(sem("ts_mm"), 1)
                fill(3)
                pe.wait_ge(sem("inv_u"), v * 5 - 3)
                pe.wait_ge(sem("inv_l"), v * 8 - 6)
                four(5, U1, L1)
                four(6, L1, TT).then_inc(sem("inv_mm"), 1)
                fill(4)
                pe.wait_ge(sem("inv_u"), v * 5 - 2)
                pe.wait_ge(sem("inv_l"), v * 8 - 5)
                four(4, L2, TT).then_inc(sem("inv_mm"), 1)
                fill(3)
                for merge in range(2):
                    pe.wait_ge(sem("inv_l"), v * 8 - 4 + merge * 2)
                    if merge == 0:
                        b0 = 2, 3, 5
                    else:
                        b0 = 6, 4, 2
                    for u in range(4):
                        tr(BK[b0[0]][:, u * P:(u + 1) * P], TT[:, u], ident)
                    four(b0[1], U1, TT).then_inc(sem("inv_mm"), 1)
                    fill(2)
                    pe.wait_ge(sem("inv_u"), v * 5 - 1 + merge)
                    pe.wait_ge(sem("inv_l"), v * 8 - 3 + merge * 2)
                    four(b0[2], L1, L2).then_inc(sem("inv_mm"), 1)
                    fill(3)
                pe.wait_ge(sem("inv_l"), v * 8)

                def rhs_mm(c):
                    tt, r = c // 2, halves[c % 2]
                    if c:
                        pe.wait_ge(sem("state"), v * 5 - 4 + c)
                    mm(BK[5][r, 0:P], AR[:, tt, 0, r], STT[:], start=True, stop=False, skip_group_check=True)
                    for e in range(2):
                        ins = mm(BK[5][r, e * 64:e * 64 + 64], MK[:, tt, e, r], TOK[:, tt, 2 * P + e * 64:2 * P + e * 64 + 64],
                                 start=False, stop=True, skip_group_check=True)
                    ins.then_inc(sem("rhs_mm"), 1)
                    mm(BK[7][:, c * CH:(c + 1) * CH], STT[:], AR[:, tt, 1, r], start=True, stop=False, skip_group_check=True)
                    for e, h in enumerate(halves):
                        mm(BK[7][h, c * CH:(c + 1) * CH], TOK[:, tt, 2 * P + e * 64:2 * P + e * 64 + 64],
                           MK[:, tt, e, P + 64 * (c % 2):P + 64 * (c % 2) + 64], start=False, stop=False,
                           skip_group_check=True)

                def u_mm(c):
                    tt, r = c // 2, halves[c % 2]
                    settle(pe)
                    pe.wait_ge(sem(f"rhs{c}"), v)
                    for e in range(2):
                        ins = mm(BK[6][r, e * 64:e * 64 + 64], TT[r, tt * 2 + e, r], RR[r, e * 64:e * 64 + 64],
                                 start=True, stop=True)
                    ins.then_inc(sem("u_mm"), 1)

                def state_mm(c):
                    tt, r = c // 2, halves[c % 2]
                    pe.wait_ge(sem("u"), v * 4 - 3 + c)
                    mm(BK[4][:, 0:P], TOK[r, tt, 0:P], UU[r, :], start=True, stop=False)
                    mm(BK[4][:, 0:P], TOK[r, tt, P:2 * P], TOK[r, tt, 2 * P:3 * P], start=False, stop=True)
                    for e, h in enumerate(halves):
                        ins = mm(BK[7][h, c * CH:(c + 1) * CH], UU[r, e * 64:e * 64 + 64],
                                 MB[r, tt, e, P + 64 * (c % 2):P + 64 * (c % 2) + 64], start=False, stop=True,
                                 skip_group_check=True)
                    ins.then_inc(sem("state_mm"), 1)

                pe.wait_ge(sem("state"), v * 5 - 4)
                pe.wait_ge(sem("ts"), v)
                pe.wait_ge(sem("sin_in"), v * 16)
                rhs_mm(0)
                for b in range(DB):
                    for e, h in enumerate(halves):
                        ins = mm(BK[3][h, b * 8:b * 8 + 8], SIN[h, b, :], ARS[h, :, b * DS:(b + 1) * DS], start=True, stop=True)
                ins.then_inc(sem("s0_mm"), 1)
                u_mm(0)
                fill(1)
                pe.wait_ge(sem("s0"), v)
                mm(BK[2][0:NS, 0:P], SPR[:, 0, :], ident, start=True, stop=False, skip_group_check=True)
                for e in range(2):
                    ins = mm(BK[2][0:NS, e * 64:e * 64 + 64], MKS[:, e, 0:NS], TOKS[:, 2 * P + e * 64:2 * P + e * 64 + 64],
                             start=False, stop=True, skip_group_check=True)
                ins.then_inc(sem("rhs_s_mm"), 1)
                state_mm(0)
                fill(1)
                rhs_mm(1)
                settle(pe)
                pe.wait_ge(sem("rhs_s"), v)
                for e in range(2):
                    ins = mm(BK[3][0:NS, e * 64:e * 64 + 64], TS[:, e, :], RS[:, e * 64:e * 64 + 64], start=True, stop=True)
                ins.then_inc(sem("u_s_mm"), 1)
                fill(5)
                u_mm(1)
                fill(2)
                state_mm(1)
                fill(2)
                rhs_mm(2)
                pe.wait_ge(sem("u_s"), v)
                for e, h in enumerate(halves):
                    mm(BK[2][h, :], TOKS[:, e * 64:e * 64 + 64], UM[:, e, :], start=True, stop=False)
                    ins = mm(BK[2][h, :], TOKS[:, P + e * 64:P + e * 64 + 64], VM[:, e, :], start=False, stop=True)
                ins.then_inc(sem("state_s_mm"), 1)
                u_mm(2)
                fill(1)
                state_mm(2)
                for e, h in enumerate(halves):
                    mm(BK[7][h, SEQ:N], US[:, e * 64:e * 64 + 64], MBS[:, e, NS:2 * NS], start=True, stop=False,
                       skip_group_check=True)
                    mm(BK[7][h, SEQ:N], TOKS[:, 2 * P + e * 64:2 * P + e * 64 + 64], MKS[:, e, NS:2 * NS], start=False,
                       stop=True, skip_group_check=True)
                fill(2)
                rhs_mm(3)
                if not last:
                    settle(pe)
                    pe.wait_ge(sem("state_s_done"), v)
                    lora_za(it + 2)
                u_mm(3)
                fill(1)
                state_mm(3)
                if not last:
                    lora_g(it + 2)
                fill(3)
                pe.wait_ge(sem("y"), v)
                mm(BK[5][:, 0:N], head_ones, YS[:], start=True, stop=True).then_inc(sem("y_mean"), 1)
                fill(4)
                pe.wait_ge(sem("y_sq"), v)
                mm(BK[5][:, 0:N], head_ones, YQ[:], start=True, stop=True).then_inc(sem("y_var"), 1)
                fill(1)
                if not last:
                    kk_sum(it + 2)
                fill(2)
                if not last:
                    log_decay(it + 2)
                fill(4)
                if not last:
                    bonus_mm(it + 2)
                fill(KT * 4 - pos[0])

            pe.wait_ge(sem("pair_done"), 1)
            lora_za(1)
            lora_g(1)
            fill_cols(FILL_FIRST)
            kk_sum(1)
            fill_cols(2)
            log_decay(1)
            fill_cols(6)
            bonus_mm(1)
            fill_cols(FIRST_COLS * KT)
            with pe.Fori(0, PAIRS - 1) as it:
                pair(it)
            pair(PAIRS - 1, last=True)

            def p_units(g):
                for j in range(4):
                    n = g * 4 + (U_P + j)
                    pe.wait_ge(sem("w_split"), n + 1)
                    if not (isinstance(g, int) and j < 2):
                        pe.wait_ge(sem("p_out"), g * 4 + (j - 1))
                    b = 2 * (j % 2)
                    if isinstance(g, int) and j == 0:
                        pe.wait_ge(sem("o_split"), 1)
                    blocks(n, j % 2, range(8, 16), BK[b + 1][:, 0:N], XN)
                    if isinstance(g, int) and j == 0:
                        pe.wait_ge(sem("o_split"), 2)
                    blocks(n, j % 2, range(0, 8), BK[b][:, 0:N], XN).then_inc(sem("unit_done"), 1)
            pe.wait_ge(sem("unit_out"), U_P)
            pe.wait_ge(sem("y_centred"), PAIRS)
            p_units(0)
            with pe.Fori(1, FORI_P) as g:
                p_units(g)
            def o_units(g):
                for j in range(4):
                    n = g * 4 + (U_O + j)
                    pe.wait_ge(sem("w_split"), n + 1)
                    if not (isinstance(g, int) and j < 2):
                        pe.wait_ge(sem("h_sum"), g * 4 + (j - 1))
                    blocks(n, j % 2, range(KT), BK[j % 2][:, 0:N], XM).then_inc(sem("unit_done"), 1)
                    if not (isinstance(g, int) and j == 0):
                        norm_sum(1, g * 4 + (j - 1), (j - 1) % 2, HSQ)
            pe.wait_ge(sem("merged"), KT)
            o_units(0)
            with pe.Fori(1, FORI_P) as g:
                o_units(g)
            norm_sum(1, KT - 1, (KT - 1) % 2, HSQ)

            def up_units(g):
                for j in range(4):
                    n = g * 4 + (U_UP + j)
                    pe.wait_ge(sem("w_split"), n + 1)
                    if not (isinstance(g, int) and j < 2):
                        pe.wait_ge(sem("up_out" if j % 2 else "gate_out"), g * 2 + (j // 2))
                    blocks(n, j % 2, range(KT), BK[j % 2][:, 0:N], XN,
                           split_from=4 if isinstance(g, int) and j == 0 else None).then_inc(sem("unit_done"), 1)
            up_units(0)
            with pe.Fori(1, FORI_UP) as g:
                up_units(g)
            pe.wait_ge(sem("act_split"), FT)
            pe.wait_ge(sem("up_out"), FT)

            def down_units(g):
                for j in range(2 * DU):
                    n = g * (2 * DU) + (U_DOWN + j)
                    tile, q = divmod(j, DU)
                    pe.wait_ge(sem("w_split"), n + 1)
                    if q == 0 and not isinstance(g, int):
                        pe.wait_ge(sem("down_out"), g * 2 + (tile - 1))
                    blocks(n, j % 2, range(DK), BK[tile][:, 0:N], XF, q == 0, q == DU - 1,
                           k_from=q * DK).then_inc(sem("unit_done"), 1)
                    if q == 1 and not (isinstance(g, int) and tile == 0):
                        norm_sum(2, g * 2 + (tile - 1), (tile - 1) % 2, FSQ)
            down_units(0)
            with pe.Fori(1, KT // 2) as g:
                down_units(g)
            norm_sum(2, KT - 1, (KT - 1) % 2, FSQ)

        @block.scalar
        def _(act):
            for dst, src, name in ((SHP, "shift_prev", "shp_in"), (PRM_ALL, "pair_params", "prm_in"),
                                   (LMU, "lora_mu", "lmu_in"), (AC, "att_c", "att_c_in"),
                                   (CONVP, "conv_params", "convp_in")):
                if dst is not SHP and dst is not AC:
                    act.dma_start(dst[:], a[src]).then_inc(sem(name), 16)
            for t in range(KT):
                if t % 4 == 0:
                    act.wait_ge(sem(f"x_in{t // 4}"), 16)
                if t >= 2:
                    act.wait_ge(sem("norm_sq_used"), t - 1)
                actv(SQ[:, t % 2, :], XRAW[:, t, :], ACT.Square).then_inc(sem("norm_sq"), 1)

            def norm_root(k, rstd):
                act.wait_ge(sem("norm_ms"), k + 1)
                actv(rstd[:], rstd[:], ACT.Sqrt).then_inc(sem("norm_rms"), 1)

            def norm_hi(k, tiles, i):
                act.wait_ge(sem("normed"), 4 * k + i + 1)
                actv(XN[:, 0, 4 * i:4 * i + 4, :], tiles[:, 4 * i:4 * i + 4, :], ACT.Copy).then_inc(sem("x_hi"), 1)

            norm_root(0, RSTD)
            split_hi(act, 0, 0)
            norm_hi(0, XRAW, 0)
            norm_hi(0, XRAW, 1)
            split_hi(act, 1, 1)
            norm_hi(0, XRAW, 2)
            norm_hi(0, XRAW, 3)
            act.wait_ge(sem("x_split"), 4)
            act.dma_start(SHP[:], a["shift_prev"]).then_inc(sem("shp_in"), 16)
            act.dma_start(AC[:], a["att_c"]).then_inc(sem("att_c_in"), 16)

            def in_units(g):
                for j in range(4):
                    n = g * 4 + j
                    act.wait_ge(sem("unit_done"), n + 1)
                    if isinstance(g, int):
                        tile = COLS[:, FIRST_COLS + n, :]
                    else:
                        tile = step(colsv[:, bass.ds(g + FIRST_COLS // 4, 1), j, :])
                    unit_out(tile, j)
                    split_hi(act, n + 2, j % 2)

            def unit_out(tile, j):
                actv(tile[:, 1:1 + SEQ], BK[j % 2][:, 0:SEQ], ACT.Copy)
                actv(samples(tile[:, 1 + SEQ:E], 5), by_request(BK[j % 2][:, SEQ:N]), ACT.Copy).then_inc(sem("unit_out"), 1)
            in_units(0)
            with act.Fori(1, FIRST_COLS // 4) as g:
                in_units(g)

            made = [0, 0]

            def filled(count):
                made[0] = min(made[0] + count, FIRST_COLS * KT)
                while made[1] < made[0] // KT:
                    n = FIRST_COLS + made[1]
                    act.wait_ge(sem("unit_done"), n + 1)
                    unit_out(COLS[:, made[1], :], n % 2)
                    split_hi(act, n + 2, n % 2)
                    made[1] += 1

            filled(FILL_ROPE * len(ROPE_TILES))
            act.wait_ge(sem("roped"), len(ROPE_TILES))
            for g in range(KVH):
                actv(RT[:, g, 0:SEQ], COLS[:, T_V + g, 1:1 + SEQ], ACT.Copy)
                ins = actv(by_request(RT[:, g, SEQ:N]), samples(COLS[:, T_V + g, 1 + SEQ:E], 5), ACT.Copy)
            ins.then_inc(sem("v_compact"), 1)
            act.wait_ge(sem("v_compact"), 1)
            act.dma_start(o["v"], RT[:, :, 0:N]).then_inc(sem("att_out"), 16)
            act.dma_start(o["k"], COLS[:, T_K:T_K + KVH, 0:N]).then_inc(sem("att_out"), 16)
            act.dma_start(o["ki"], COLS[0:ID, T_KI, 0:N]).then_inc(sem("att_out"), 16)
            for c in range(4):
                act.wait_ge(sem("dots"), c + 1)
                if c >= 2:
                    act.wait_ge(sem("mixed"), c - 1)
                actv(RELU[:, c % 2, 0:KEYS_S], BK[2 + c % 2 * 2][:, 0:KEYS_S], ACT.Relu).then_inc(sem("relu"), 1)
            filled(FILL_TOPK_S)
            for n in range(4, 20):
                act.wait_ge(sem("dots"), n + 1)
                if n < 6:
                    act.wait_ge(sem("mixed"), n - 1)
                else:
                    act.wait_ge(sem("relu_used"), n - 5)
                for par in range(2):
                    ins = actv(RELU[:, n % 2, par * SEQ:(par + 1) * SEQ], BK[2 + n % 2 * 2 + par][:, 0:SEQ], ACT.Relu)
                ins.then_inc(sem("relu"), 1)
                filled(FILL_DOTS)
            filled(FILL_TOPK)
            act.wait_ge(sem("v_t"), 1)
            act.wait_ge(sem("bias_ready"), 1)
            actv(VTOK[:].rearrange("p k f -> p (k f)"), BK[4][:], ACT.Copy).then_inc(sem("v_tok"), 1)

            def sample_values(n, half):
                act.wait_ge(sem("v_new_t"), half + 1)
                if half:
                    act.wait_ge(sem("pv"), 1)
                for x in range(2):
                    ins = actv(VNEW[:, 2 * x:2 * x + 2, :].rearrange("t b f -> t (b f)"), BK[2 + x][0:DS, :], ACT.Copy)
                ins.then_inc(sem("v_new"), 1)

            for n, (kind, which) in enumerate(ATT_STEPS):
                if kind == "sample":
                    sample_values(n, which)
                    act.wait_ge(sem("s_max"), n + 1)
                    actv(PROB[:, 0:KEYS_S], BK[7][:, 0:KEYS_S], ACT.Exp, bias=ST8[:, 0:1], scale=HDIM ** -0.5,
                         accum_out=ST8[:, 4:5]).then_inc(sem("exp"), 1)
                else:
                    act.wait_ge(sem("s_max"), n + 1)
                    for r in range(4):
                        ins = actv(PROB[:, r * SEQ:(r + 1) * SEQ], PROB[:, r * SEQ:(r + 1) * SEQ], ACT.Exp,
                                   bias=ST8[:, r:r + 1], accum_out=ST8[:, 4 + r:5 + r])
                    ins.then_inc(sem("exp"), 1)
                filled(FILL_SCORES + FILL_SOFTMAX)
                act.wait_ge(sem("p_t"), n + 1)
                if n:
                    act.wait_ge(sem("pv"), n)
                if kind == "sample":
                    actv(PRT[:, 0:2 * P], BK[4][:, 0:2 * P], ACT.Copy)
                    actv(PRT[0:DS, 2 * P:3 * P], BK[4][0:DS, 2 * P:3 * P], ACT.Copy).then_inc(sem("p_sb"), 1)
                else:
                    actv(PRT[:, 0:512], BK[4][:], ACT.Copy).then_inc(sem("p_sb"), 1)
                filled(FILL_P_T)
                act.wait_ge(sem("pv"), n + 1)
                if kind == "sample":
                    c0 = SEQ + 16 * which
                    for b in range(4):
                        ins = actv(COLS[:, T_Q:T_Q + AH, c0 + DS * b:c0 + DS * b + DS],
                                   BK[6][:, b * 32:b * 32 + 32].rearrange("p (h t) -> p h t", t=DS), ACT.Copy)
                    ins.then_inc(sem("o_sb"), 1)
                else:
                    actv(COLS[:, T_Q + 4 * which:T_Q + 4 * which + 4, kind * P:(kind + 1) * P],
                         BK[6][:].rearrange("p (r q) -> p r q", r=4), ACT.Copy).then_inc(sem("o_sb"), 1)
            act.wait_ge(sem("lora_mix"), 1)
            actv(COLS[0:LORA_W, T_LW, 0:N], RKV[0:LORA_W, 0, :], ACT.Tanh)
            actv(COLS[0:LORA_A, T_LA, 0:N], RKV[0:LORA_A, 1, :], ACT.Copy)
            actv(COLS[:, T_LG, 0:N], RKV[:, 2, :], ACT.Tanh, scale=0.5).then_inc(sem("lora_act"), 1)

            def lora_out(v):
                act.wait_ge(sem("z_mm"), v)
                actv(LDT[:, 0:2, :].rearrange("p t f -> p (t f)"), BK[2][:, 0:2 * P], ACT.Tanh, scale=0.5)
                actv(LDT[0:NS, 2, :], BK[2][0:NS, 2 * P:3 * P], ACT.Tanh, scale=0.5).then_inc(sem("z_tanh"), 1)
                act.wait_ge(sem("a_mm"), v)
                if not (isinstance(v, int) and v == 1):
                    act.wait_ge(sem("u"), v * 4 - 4)
                act.wait_ge(sem("prm"), v)
                actv(AG[:], BK[3][:, 0:N], ACT.Tanh, bias=PRM[:, PR_A0H:PR_A0H + 1], scale=0.5).then_inc(sem("a_tanh"), 1)

            def kk_square(it, v):
                act.wait_ge(sem("rkv"), v)
                actv(SQK[:], RKV[:, 1, :], ACT.Square, scale=PRM[:, PR_KK:PR_KK + 1]).then_inc(sem("kk_sq"), 1)
                act.wait_ge(sem("g_mm"), v)
                actv(step(rwv[:, 2, bass.ds(it, 1), 0:N]), BK[6][:, 0:N], ACT.Copy).then_inc(sem("g_sb"), 1)

            def kk_root_and_decays(v):
                act.wait_ge(sem("kk_max"), v)
                actv(SQK[:], SQK[:], ACT.Sqrt).then_inc(sem("kk_norm"), 1)
                actv(ROOT[:, 1:2], ident[:, 0:1], ACT.Exp)
                act.wait_ge(sem("log_decay"), v)
                actv(PEXP[:, 0, :], BK[5][:, 0:N], ACT.Exp)
                actv(PEXP[:, 1, :], BK[5][:, 0:N], ACT.Exp, scale=-1.0)
                actv(PEXP[:, 2, :], BK[6][:, 0:N], ACT.Exp).then_inc(sem("decay"), 1)

            def pair(it, last=False):
                v = it + 1

                def stream(j):
                    n = it * 4 + (U_GATE + j)
                    act.wait_ge(sem("unit_done"), n + 1)
                    actv(step(gatesv[:, bass.ds(it, 1), j, :]), BK[j % 2][:, 0:N], ACT.Tanh,
                         scale=0.5).then_inc(sem("unit_out"), 1)
                    split_hi(act, n + 2, j % 2)

                act.wait_ge(sem("tok_mm"), v)
                actv(TOK[:, 0, :], BK[2][:, 0:3 * P], ACT.Copy)
                actv(TOK[:, 1, :], BK[3][:, 0:3 * P], ACT.Copy)
                actv(TOKS[:], BK[7][0:NS, 0:3 * P], ACT.Copy).then_inc(sem("tok_sb"), 1)

                def evac(dst, bank, k):
                    act.wait_ge(sem("inv_mm"), v * 8 - 8 + k)
                    actv(dst[:].rearrange("p u f -> p (u f)"), BK[bank][:], ACT.Copy).then_inc(sem("inv_u"), 1)
                evac(U2, 5, 1)
                evac(U1, 4, 2)
                evac(L2, 5, 3)
                stream(0)
                evac(L1, 2, 5)
                evac(L1, 6, 7)
                stream(1)
                act.wait_ge(sem("s0_mm"), v)
                for x in range(2):
                    src = BK[3][:, 0:DB * 2 * DS].rearrange("p (b x t) -> p x b t", b=DB, x=2)[:, x]
                    ins = actv(by_request(SPR[:, x, :]), src, ACT.Copy)
                ins.then_inc(sem("s0"), 1)
                stream(2)
                if not last:
                    lora_out(it + 2)
                act.wait_ge(sem("y_centred"), v)
                actv(YQ[:], YS[:], ACT.Square).then_inc(sem("y_sq"), 1)
                if not last:
                    kk_square(it + 1, it + 2)
                actv(ROOT[:, 0:1], ident[:, 0:1], ACT.Sqrt)
                act.wait_ge(sem("y_var_sb"), v)
                actv(YQ[:], YQ[:], ACT.Sqrt).then_inc(sem("y_std"), 1)
                if not last:
                    kk_root_and_decays(it + 2)
                stream(3)
            lora_out(1)
            kk_square(0, 1)
            filled(FILL_FIRST)
            kk_root_and_decays(1)
            filled(FIRST_COLS * KT)
            act.wait_ge(sem("shift_out"), 1)
            act.dma_start(o["shift"], SHO[:]).then_inc(sem("att_out"), 16)
            act.wait_ge(sem("att_out"), 4 * 16)
            with act.Fori(0, PAIRS - 1) as it:
                pair(it)
            pair(PAIRS - 1, last=True)

            act.wait_ge(sem("unit_done"), U_P)
            actv(XN[:, 0, 8:16, :], COLS[:, T_Q:T_Q + 8, 0:N], ACT.Copy).then_inc(sem("o_hi"), 1)
            act.wait_ge(sem("pair_done"), 1 + PAIRS)
            actv(XN[:, 0, 0:8, :], COLS[:, 0:8, 0:N], ACT.Copy).then_inc(sem("o_hi"), 1)
            act.wait_ge(sem("sout_done"), 16 * PAIRS)
            act.wait_ge(sem("stout_done"), 32 * PAIRS)
            act.dma_start(H[:], a["x"]).then_inc(sem("h_in"), 16)
            act.wait_ge(sem("o_split"), 2)

            xmv = XM[:].rearrange("p x (g j) n -> p x g j n", j=4)
            hv = H[:].rearrange("p (g j) n -> p g j n", j=4)

            def p_units(g):
                for j in range(4):
                    n = g * 4 + (U_P + j)
                    if isinstance(g, int):
                        dst = XM[:, 0, j, :]
                    else:
                        dst = step(xmv[:, 0, bass.ds(g, 1), j, :])
                    act.wait_ge(sem("unit_done"), n + 1)
                    split_hi(act, n + 2, j % 2)
                    act.wait_ge(sem("merge_sum"), g * 4 + (j + 1))
                    actv(dst, MG[:, 2 * (j % 2), :], ACT.Copy, scale=0.5).then_inc(sem("merge_hi"), 1)
            p_units(0)
            with act.Fori(1, FORI_P) as g:
                p_units(g)

            def square(k, t, src, dst):
                if not (isinstance(t, int) and t < 2):
                    act.wait_ge(sem("norm_sq_used"), t + (KT * k - 1))
                actv(dst, src, ACT.Square).then_inc(sem("norm_sq"), 1)

            def o_units(g):
                for j in range(4):
                    split_hi(act, g * 4 + (U_O + j + 2), j % 2)
                    act.wait_ge(sem("h_sum"), g * 4 + (j + 1))
                    square(1, g * 4 + j, H[:, j, :] if isinstance(g, int) else step(hv[:, bass.ds(g, 1), j, :]), HSQ[:, j % 2, :])
            o_units(0)
            with act.Fori(1, FORI_P) as g:
                o_units(g)
            act.wait_ge(sem("h_sum"), KT)
            act.dma_start(h_spill, H[:].rearrange("p k n -> p (k n)")).then_inc(sem("h_spilled"), 16)
            norm_root(1, HRSTD)
            for i in range(4):
                norm_hi(1, HN, i)
            act.wait_ge(sem("x_split"), 8)
            act.dma_start(CPREV[:], a["conv_prev"]).then_inc(sem("cprev_in"), 16)

            xfv = XF[:].rearrange("p x (g j) n -> p x g j n", j=2)

            def up_units(g):
                for j in range(2):
                    n = g * 4 + (U_UP + 2 * j)
                    act.wait_ge(sem("unit_done"), n + 1)
                    if not (isinstance(g, int)):
                        act.wait_ge(sem("conv_used"), g * 2 + (j - 1))
                    actv(GX[:, j, 2:2 + SEQ], BK[0][:, 0:SEQ], ACT.Copy)
                    actv(samples(GX[:, j, 2 + SEQ:GE], 6), by_request(BK[0][:, SEQ:N]), ACT.Copy).then_inc(sem("gate_out"), 1)
                    split_hi(act, n + 2, 0)
                    act.wait_ge(sem("conv_done"), g * 2 + (j + 1))
                    actv(CV[:, j, 1, :], CV[:, j, 0, :], ACT.Silu).then_inc(sem("silu"), 1)
                    split_hi(act, n + 3, 1)
                    act.wait_ge(sem("up_out"), g * 2 + (j + 1))
                    dst = XF[:, 0, j, :] if isinstance(g, int) else step(xfv[:, 0, bass.ds(g, 1), j, :])
                    actv(dst, CV[:, j, 0, 0:N], ACT.Copy).then_inc(sem("glu_hi"), 1)
            up_units(0)
            with act.Fori(1, FORI_UP) as g:
                up_units(g)
            act.wait_ge(sem("conv_done"), FT)
            act.dma_start(o["conv"], COUT[:]).then_inc(sem("out_done"), 16)
            act.wait_ge(sem("h_spilled"), 16)
            act.wait_ge(sem("unit_done"), U_DOWN)
            act.dma_start(H2[:].rearrange("p k n -> p (k n)"), h_spill).then_inc(sem("h_back"), 16)

            h2v = H2[:].rearrange("p (g j) n -> p g j n", j=2)

            def down_units(g, count=2 * DU):
                for j in range(2 * DU):
                    tile, q = divmod(j, DU)
                    if j < count:
                        split_hi(act, g * (2 * DU) + (U_DOWN + j + 2), j % 2, DK)
                    if q == DU - 1:
                        act.wait_ge(sem("down_out"), g * 2 + (tile + 1))
                        t = H2[:, 2 * g + tile, :] if isinstance(g, int) else step(h2v[:, bass.ds(g, 1), tile, :])
                        square(2, g * 2 + tile, t, FSQ[:, tile, :])
            down_units(0)
            with act.Fori(1, KT // 2 - 1) as g:
                down_units(g)
            down_units(KT // 2 - 1, 2 * DU - 2)
            norm_root(2, FRSTD)
            for i in range(4):
                act.wait_ge(sem("normed"), 8 + i + 1)
                act.dma_start(o["y"][:, 4 * i:4 * i + 4, :], YO[:, 4 * i:4 * i + 4, :]).then_inc(sem("out_done"), 16)

        @block.gpsimd
        def _(pool):
            pool.dma_start(PTAB[:], a["page_table"]).then_inc(sem("ptab_in"), 16)
            split_lo(pool, 0, 0)
            split_lo(pool, 1, 1)
            pool.wait_ge(sem("ptab_in"), 16)
            pool.wait_ge(sem("x_split"), 4)

            def load_kv(b, j):
                i = 2 * b + j
                page = pool.value_load(PTAB[0:1, i:i + 1], min_val=0, max_val=N_POOL - 1)
                keys = slice(j * PAGE, (j + 1) * PAGE)
                for g in range(KVH):
                    pool.dma_start(KC[:, b % 4, g, keys], rows_of(a["cache_k"][bass.ds(page, 1), g])).then_inc(sem("kv_in"), 16)
                    pool.dma_start(VC[:, b % 4, j, g * P:(g + 1) * P],
                                   rows_of(a["cache_v"][bass.ds(page, 1), g])).then_inc(sem("kv_in"), 16)
            for b in range(DB):
                for j in range(2):
                    page = pool.value_load(PTAB[0:1, 2 * b + j:2 * b + j + 1], min_val=0, max_val=N_POOL - 1)
                    for par in range(2):
                        pool.dma_start(KIC[64 * par:64 * par + 64, b, j * PAGE:(j + 1) * PAGE],
                                       rows_of(a["cache_kidx"][bass.ds(page, 1)])).then_inc(sem("ki_in"), 16)
            for i in range(8):
                load_kv(i // 2, i % 2)
            pool.wait_ge(sem("w_split"), FIRST_COLS + 2)
            for n in range(FIRST_COLS + 2, U_GATE + 2):
                split_lo(pool, n, n % 2)
                if n == U_GATE - 1:
                    pool.wait_ge(sem("pair_done"), 1)
                    pool.dma_start(LORA[:], a["lora"][0]).then_inc(sem("lora_in"), 16)
                    pool.dma_start(SIN[:], a["state_s"][0]).then_inc(sem("sin_in"), 16)
                    pool.memset(STT[:], 0.0).then_inc(sem("state"), 1)
                late = n - FIRST_COLS - POOL_LOADS_FROM
                if late >= 0 and late < 8:
                    if late == 0:
                        pool.wait_ge(sem("pv"), 1)
                    load_kv(4 + late // 2, late % 2)
            def pair(it, last):
                v = it + 1
                n = it * 4 + U_GATE
                split_lo(pool, n + 2, 0)
                if not last:
                    pool.wait_ge(sem("g_mm"), v)
                    pool.dma_start(LORA[:], rows3(a["lora"][bass.ds(it + 1, 1)])).then_inc(sem("lora_in"), 16)
                split_lo(pool, n + 3, 1)
                split_lo(pool, n + 4, 0)
                pool.wait_ge(sem("state_s_done"), v)
                dst = a_or(o["wkv_s"], it)
                pool.dma_start(dst, SIN[:]).then_inc(sem("sout_done"), 16)
                pool.wait_ge(sem("state"), v * 5)
                for e, h in enumerate((slice(0, 64), slice(64, 128))):
                    pool.dma_start(a_or(o["wkv_p"], it)[h, :], STT[h, h]).then_inc(sem("stout_done"), 16)
                split_lo(pool, n + 5, 1)
                pool.wait_ge(sem("sout_done"), v * 16)
                if not last:
                    pool.dma_start(SIN[:], rows3(a["state_s"][bass.ds(it + 1, 1)])).then_inc(sem("sin_in"), 16)
                pool.wait_ge(sem("stout_done"), v * 32)
                if not last:
                    pool.tensor_tensor(STT[:], ident, ident, ALU.subtract).then_inc(sem("state"), 1)

            def rows3(x):
                return x.rearrange("o p a b -> (o p) a b")

            def a_or(x, it):
                if isinstance(it, int):
                    return x[it]
                x = x[bass.ds(it, 1)]
                return rows3(x) if len(x.shape) == 4 else rows_of(x)

            with pool.Fori(0, PAIRS - 1) as it:
                pair(it, False)
            pair(PAIRS - 1, True)

        @block.vector
        def _(dve):
            st = Steps(dve, sem("dve_step"))
            dve.wait_ge(sem("norms_in"), 16)

            def norm(k, rstd, src, dst, gain, split):
                dve.wait_ge(sem("norm_sq_used"), KT * (k + 1))
                V.tensor_scalar(rstd[:], BK[2][:, 0:N], RMS_EPS, None, ALU.add).then_inc(sem("norm_ms"), 1)
                dve.wait_ge(sem("norm_rms"), k + 1)
                st.done(V.reciprocal(rstd[:], rstd[:]))
                for i in range(5):
                    if i < 4:
                        for t in range(4 * i, 4 * i + 4):
                            ins = V.scalar_tensor_tensor(dst[:, t, :], src[:, t, :], NORMS[:, k, t:t + 1], rstd[:],
                                                         ALU.mult, ALU.mult)
                        ins.then_inc(sem("normed"), 1)
                    if split and i:
                        q = slice(4 * i - 4, 4 * i)
                        dve.wait_ge(sem("x_hi"), 4 * k + i)
                        V.tensor_tensor(XN[:, 1, q, :], dst[:, q, :], XN[:, 0, q, :].bitcast(F32),
                                        ALU.subtract).then_inc(sem("x_split"), 1)

            norm(0, RSTD, XRAW, XRAW, 0, True)
            dve.wait_ge(sem("x_split"), 4)
            V.memset(COLS[:, :, 0:1], 0.0)
            V.memset(COLS[:, RW_T:, 1 + SEQ:E:5], 0.0)
            dve.wait_ge(sem("shp_in"), 16)
            V.tensor_copy(COLS[:, 0:RW_T, 1 + SEQ:E:5], SHP[:]).then_inc(sem("slots"), 1)
            V.memset(QZ[:].rearrange("p g b h t -> p (g b h t)"), 0.0)

            dve.wait_ge(sem("w_split"), 2)
            def in_units(g):
                for j in range(4):
                    split_lo(dve, g * 4 + (j + 2), j % 2)
            in_units(0)
            with dve.Fori(1, FIRST_COLS // 4) as g:
                in_units(g)

            dve.wait_ge(sem("att_c_in"), 16)
            for i, t in enumerate(ROPE_TILES):
                kind = "head" if t < T_V else "idx"
                dve.wait_ge(sem("rot"), i + 1)
                V.tensor_tensor(RT[:, 0, :], BK[2 + i % 2][:, 0:TE], acst("sin_" + kind), ALU.mult).then_inc(sem("rot_used"), 1)
                st.done(V.tensor_tensor(RT[:, 1, :], COLS[:, t, 1:E], acst("cos_" + kind), ALU.mult))
                dve.wait_ge(sem("rot_used"), i + 1)
                st.mark(V.tensor_tensor(COLS[:, t, 0:SEQ], RT[:, 0, 0:SEQ], RT[:, 1, 0:SEQ], ALU.add))
                if T_QI <= t < T_KI:
                    dst = QIS[:, :, t - T_QI, :]
                else:
                    dst = by_request(COLS[:, t, SEQ:N])
                V.tensor_tensor(dst, samples(RT[:, 0, SEQ:TE], 5), samples(RT[:, 1, SEQ:TE], 5),
                                ALU.add).then_inc(sem("roped"), 1)
                dve.wait_ge(sem("roped"), i + 1)
                st.sync()
            dve.wait_ge(sem("wi_t"), 1)
            V.tensor_scalar(WI[:], BK[4][:, 0:2 * P].rearrange("p (q f) -> p q f", q=2)[:, :, WI_ROW:WI_ROW + IH],
                            IDX_SCALE, None, ALU.mult).then_inc(sem("wi_sb"), 1)
            dve.wait_ge(sem("wi_rows"), 1)
            for c in range(4):
                ins = V.tensor_tensor(WM[:, c, :], BK[5][:, 0:NS], acst("m_query")[:, c * NS:(c + 1) * NS], ALU.mult)
            ins.then_inc(sem("w_mix"), 1)
            def select(scores, topk, bias, causal):
                m8 = M8[0:scores.shape[0], :]
                while topk > 0:
                    st.done(V.max(m8, scores))
                    if topk < 8:
                        st.done(V.memset(m8[:, topk:8], MARK))
                    st.done(V.match_replace(scores, m8, scores, MARK))
                    topk -= 8
                st.done(V.tensor_scalar(scores, scores, MARK / 2, -BIGNEG, ALU.is_lt, ALU.mult))
                return V.scalar_tensor_tensor(bias, scores, BIGNEG, causal, ALU.add, ALU.add)

            dve.wait_ge(sem("mixed"), 4)
            st.done(V.tensor_tensor(ACS[:], BK[6][0:NS, 0:KEYS_S], acst("causal_s", NS), ALU.add))
            st.done(select(ACS[:], TOPK_S, BIASS[:], acst("causal_s", NS)))
            dve.wait_ge(sem("wi_sb"), 1)
            for n in range(4, 20):
                qt, i = divmod(n - 4, 8)
                dve.wait_ge(sem("relu"), n + 1)
                for par in range(2):
                    src = RELU[:, n % 2, par * SEQ:(par + 1) * SEQ]
                    w = WI[:, qt, 2 * i + par:2 * i + par + 1]
                    base = ACC[:, qt, :] if i or par else acst("causal")[:, qt * SEQ:(qt + 1) * SEQ]
                    ins = V.scalar_tensor_tensor(ACC[:, qt, :], src, w, base, ALU.mult, ALU.add)
                    st.done(ins) if par == 0 else None
                ins.then_inc(sem("relu_used"), 1)
                dve.wait_ge(sem("relu_used"), n - 3)
            for qt in range(2):
                ins = select(ACC[:, qt, :], TOPK_P, BIASP[:, qt, :], acst("causal")[:, qt * SEQ:(qt + 1) * SEQ])
                if qt == 0:
                    st.done(ins)
            ins.then_inc(sem("bias_ready"), 1)
            dve.wait_ge(sem("bias_ready"), 1)

            def group_queries(half):
                for g in range(KVH):
                    for b in range(4):
                        c0 = SEQ + DS * (4 * half + b)
                        ins = V.tensor_copy(QZ[:, g, b, 4 * g:4 * g + 4, :], COLS[:, T_Q + 4 * g:T_Q + 4 * g + 4, c0:c0 + DS])
                ins.then_inc(sem("q_grouped"), 1)

            group_queries(0)
            for n, (kind, which) in enumerate(ATT_STEPS):
                dve.wait_ge(sem("s_mm"), n + 1)
                if n:
                    dve.wait_ge(sem("p_t"), n)
                if kind == "sample":
                    st.done(V.tensor_reduce(ST8[:, 1:2], BK[7][:, 0:KEYS_S], AX.X, ALU.max, negate=True))
                    V.tensor_scalar(ST8[:, 0:1], ST8[:, 1:2], HDIM ** -0.5, None, ALU.mult).then_inc(sem("s_max"), 1)
                    if which == 0:
                        group_queries(1)
                    dve.wait_ge(sem("exp"), n + 1)
                    st.done(V.reciprocal(ST8[:, 8:9], ST8[:, 4:5]))
                    V.tensor_scalar(PROB[:, 0:KEYS_S], PROB[:, 0:KEYS_S], ST8[:, 8:9], None, ALU.mult).then_inc(sem("prob"), 1)
                    continue
                for r in range(4):
                    ins = V.scalar_tensor_tensor(PROB[:, r * SEQ:(r + 1) * SEQ], BK[2 + r // 2][:, r % 2 * SEQ:(r % 2 + 1) * SEQ],
                                                 HDIM ** -0.5, BIASP[:, kind, :], ALU.mult, ALU.add)
                ins.then_inc(sem("s_used"), 1)
                dve.wait_ge(sem("s_used"), n)
                V.tensor_reduce(ST8[:, 0:4], PROB[:].rearrange("p (r k) -> p r k", r=4), AX.X, ALU.max,
                                negate=True).then_inc(sem("s_max"), 1)
                dve.wait_ge(sem("exp"), n + 1)
                st.done(V.reciprocal(ST8[:, 8:12], ST8[:, 4:8]))
                for r in range(4):
                    ins = V.tensor_scalar(PROB[:, r * SEQ:(r + 1) * SEQ], PROB[:, r * SEQ:(r + 1) * SEQ],
                                          ST8[:, 8 + r:9 + r], None, ALU.mult)
                ins.then_inc(sem("prob"), 1)
                dve.wait_ge(sem("p_t"), n + 1)
                dve.wait_ge(sem("pv"), n)
                V.tensor_copy(PRT[:, 512:1024], BK[5][:]).then_inc(sem("p_sb2"), 1)

            def last_tokens(t0, t1):
                V.tensor_copy(SHO[:, t0:t1, 0:1], COLS[:, t0:t1, SEQ:SEQ + 1])
                return V.tensor_copy(SHO[:, t0:t1, 1:1 + DB], COLS[:, t0:t1, SEQ + 5:E:5])
            dve.wait_ge(sem("unit_out"), FIRST_COLS + 17)
            dve.wait_ge(sem("slots"), 1)
            last_tokens(24, RW_T)
            last_tokens(0, 17)
            dve.wait_ge(sem("o_sb"), 6)
            dve.wait_ge(sem("pv"), 6)
            dve.wait_ge(sem("prm_in"), 16)
            dve.wait_ge(sem("lmu_in"), 16)

            def mix(src, dst, mu):
                st.done(mix_diff(src))
                return mix_add(src, dst, mu)

            def mix_diff(src):
                return V.tensor_tensor(DIFF[:], src[:, :, 0:TE], src[:, :, 1:E], ALU.subtract)

            def mix_add(src, dst, mu):
                for j in range(3):
                    V.scalar_tensor_tensor(dst[:, j, 0:SEQ], DIFF[:, j, 0:SEQ], mu[:, j:j + 1], src[:, j, 1:1 + SEQ],
                                           ALU.mult, ALU.add)
                    ins = V.scalar_tensor_tensor(by_request(dst[:, j, SEQ:N]), samples(DIFF[:, j, SEQ:TE], 5), mu[:, j:j + 1],
                                                 samples(src[:, j, 1 + SEQ:E], 5), ALU.mult, ALU.add)
                return ins
            mix(COLS[:, T_LW:T_LG + 1, :], RKV, LMU).then_inc(sem("lora_mix"), 1)
            dve.wait_ge(sem("lora_act"), 1)
            st.done(V.memset(COLS[LORA_W:LORA_W + 1, T_LW, 0:N], 1.0))
            st.done(V.tensor_scalar(COLS[:, T_LG, 0:N], COLS[:, T_LG, 0:N], 0.5, 0.5, ALU.mult, ALU.add))
            V.tensor_scalar(PRM_ALL[:, :, PR_A0H], PRM_ALL[:, :, PR_A0H], 0.5, None, ALU.mult).then_inc(sem("pair_done"), 1)
            dve.wait_ge(sem("pair_done"), 1)

            def params(it):
                V.tensor_copy(PRM[:], step(PRM_ALL[:, bass.ds(it, 1), :])).then_inc(sem("prm"), 1)

            def columns(it):
                return rwv[:, :, bass.ds(it, 1), :].rearrange("p j o e -> p (j o) e")

            def kk_max(v):
                dve.wait_ge(sem("kk_sum"), v)
                V.tensor_scalar(SQK[:], BK[4][:, 0:N], 1e-24, None, ALU.max).then_inc(sem("kk_max"), 1)

            def decay_and_a(v):
                dve.wait_ge(sem("z_tanh"), v)
                V.tensor_scalar(LDT[:, 0:2, :], LDT[:, 0:2, :], 1.0, None, ALU.add)
                V.tensor_scalar(LDT[0:NS, 2, :], LDT[0:NS, 2, :], 1.0, None, ALU.add).then_inc(sem("decay_tok"), 1)
                dve.wait_ge(sem("a_tanh"), v)
                V.tensor_scalar(AG[:], AG[:], 0.5, 0.5, ALU.mult, ALU.add).then_inc(sem("a_sb"), 1)

            halves = [slice(0, 64), slice(64, 128)]

            def head(it, v):
                r_, k_, v_ = RKV[:, 0, :], RKV[:, 1, :], RKV[:, 2, :]

                def prm(i):
                    return PRM[:, i:i + 1]

                dve.wait_ge(sem("rkv"), v)
                dve.wait_ge(sem("a_sb"), v)
                dve.wait_ge(sem("kk_norm"), v)
                st.done(V.reciprocal(SQK[:], SQK[:]))
                st.mark(V.scalar_tensor_tensor(KKN[:], k_, prm(PR_KK), SQK[:], ALU.mult, ALU.mult))
                st.done(V.tensor_scalar(KP[:], AG[:], 1.0, prm(PR_KA), ALU.subtract, ALU.mult))
                st.done(V.scalar_tensor_tensor(KP[:], KP[:], 1.0, k_, ALU.add, ALU.mult))
                V.scalar_tensor_tensor(SQK[:], r_, prm(PR_RK), KP[:], ALU.mult, ALU.mult).then_inc(sem("rkr"), 1)
                st.done(V.tensor_tensor(AG[:], KKN[:], AG[:], ALU.mult))
                dve.wait_ge(sem("decay"), v)

                def two(x):
                    return x[:, 0:SEQ].rearrange("p (t n) -> p t n", t=2)
                p, pi, px = PEXP[:, 0, :], PEXP[:, 1, :], PEXP[:, 2, :]
                V.scalar_tensor_tensor(AR[:, :, 0, :], two(KKN), -1.0, two(px), ALU.mult, ALU.mult)
                V.scalar_tensor_tensor(ARS[:, 0, :], KKN[:, SEQ:N], -1.0, px[:, SEQ:N], ALU.mult, ALU.mult)
                V.tensor_tensor(AR[:, :, 1, :], two(r_), two(p), ALU.mult)
                V.tensor_tensor(ARS[:, 1, :], r_[:, SEQ:N], p[:, SEQ:N], ALU.mult)
                V.tensor_tensor(BT[:], AG[:], pi, ALU.mult)
                V.tensor_copy(PC[:, 0:NCH], p[:, CH - 1:SEQ:CH])
                V.tensor_copy(PC[:, NCH:], p[:, SEQ + DS - 1:N:DS])
                V.tensor_tensor(KTL[:], KP[:], pi, ALU.mult).then_inc(sem("ar_ready"), 1)
                dve.wait_ge(sem("bonus_mm"), v)
                V.tensor_tensor(step(rwv[:, 1, bass.ds(it, 1), 0:N]), BK[4][:, 0:N], v_, ALU.mult).then_inc(sem("bonus"), 1)

            def pair(it, last=False):
                v = it + 1
                dve.wait_ge(sem("tok_mm"), v)
                dve.wait_ge(sem("ar_ready"), v)
                dve.wait_ge(sem("bonus"), v)
                dve.wait_ge(sem("b_mm"), v)
                for e in range(2):
                    bank = BK[5 + e][:].rearrange("p (t f) -> p t f", t=2)
                    V.tensor_tensor(MB[:, :, e, :], bank, spread(m_ab, 1, [P, 2, 2 * P]), ALU.mult)
                    ins = V.tensor_tensor(U1[:, e::2, :], bank[:, :, 0:P], spread(m16u, 1, [P, 2, P]), ALU.mult)
                st.done(ins)
                V.tensor_tensor(TT[:], U1[:], spread(ident, 1, [P, 4, P]), ALU.add)
                dve.wait_ge(sem("k_mm"), v)
                bank = BK[4][:].rearrange("p (u f) -> p u f", u=4)
                V.tensor_tensor(L1[:], bank, spread(m16l, 1, [P, 4, P]), ALU.mult).then_inc(sem("block16"), 1)
                V.tensor_copy(ML[:], bank)
                for e in range(2):
                    bank = BK[2 + e][:].rearrange("p (t f) -> p t f", t=2)
                    V.tensor_tensor(MK[:, :, e, :], bank, spread(m_ab, 1, [P, 2, 2 * P]), ALU.mult)
                bank = BK[7][0:NS]
                st.mark(V.tensor_tensor(MBS[:], bank[:, 0:128].rearrange("p (e f) -> p e f", e=2), spread(ms_ab, 1, [NS, 2, 2 * NS]), ALU.mult))
                V.tensor_tensor(MKS[:], bank[:, 128:256].rearrange("p (e f) -> p e f", e=2), spread(ms_ab, 1, [NS, 2, 2 * NS]), ALU.mult)
                st.sync()
                V.tensor_tensor(TS[:], MBS[:, :, 0:NS], spread(ident[0:NS, 0:NS], 1, [NS, 2, NS]), ALU.add)
                V.tensor_tensor(MLS[:], bank[:, 256:320].rearrange("p (e f) -> p e f", e=2), spread(ms_l, 1, [NS, 2, NS]),
                                ALU.mult).then_inc(sem("mats"), 1)
                dve.wait_ge(sem("mats"), v)

                def grid(bank):
                    return BK[bank][:].rearrange("p (u f) -> p u f", u=4)

                def inv(k):
                    dve.wait_ge(sem("inv_mm"), v * 8 - 8 + k)

                def add_t(bank, k):
                    V.tensor_tensor(TT[:], TT[:], grid(bank), ALU.add).then_inc(sem("inv_l"), 1)
                    dve.wait_ge(sem("inv_l"), v * 8 - 8 + k)
                inv(1)
                V.tensor_copy(L2[:], grid(6)).then_inc(sem("inv_l"), 1)
                dve.wait_ge(sem("l2s_mm"), v)
                V.tensor_copy(L2S[:], BK[7][0:NS, 0:2 * NS].rearrange("p (e f) -> p e f", e=2)).then_inc(sem("l2s"), 1)
                inv(2)
                V.tensor_copy(L1[:], grid(2))
                add_t(3, 2)
                dve.wait_ge(sem("ts_mm"), v)
                V.tensor_tensor(TS[:], TS[:], BK[7][0:NS, 2 * NS:4 * NS].rearrange("p (e f) -> p e f", e=2),
                                ALU.add).then_inc(sem("ts"), 1)
                inv(3)
                V.tensor_tensor(U1[:], ML[:], spread(m32l, 1, [P, 4, P]), ALU.mult)
                add_t(6, 3)
                inv(4)
                add_t(4, 4)
                for merge in range(2):
                    inv(5 + 2 * merge)
                    V.tensor_copy(L2[:], grid((3, 4)[merge])).then_inc(sem("inv_l"), 1)
                    if merge == 0:
                        V.tensor_tensor(U1[:], ML[:], spread(m64l, 1, [P, 4, P]), ALU.mult)
                    inv(6 + 2 * merge)
                    add_t((5, 2)[merge], 6 + 2 * merge)
                st.done(V.tensor_copy(PRM_LN[:], PRM[:, PR_LW:PR_LB + 1]))
                if not last:
                    params(it + 1)

                def rhs(c):
                    r = halves[c % 2]
                    dve.wait_ge(sem("rhs_mm"), v * 4 - 3 + c)
                    V.tensor_copy(RR[r, :], BK[5][r, 0:P]).then_inc(sem(f"rhs{c}"), 1)
                    dve.wait_ge(sem("state"), v * 5 - 4 + c)
                    st.mark(V.tensor_scalar(STP[:], STT[:], PC[:, c:c + 1], None, ALU.mult))

                def u(c):
                    r = halves[c % 2]
                    dve.wait_ge(sem("u_mm"), v * 4 - 3 + c)
                    V.tensor_copy(UU[r, :], BK[6][r, 0:P]).then_inc(sem("u"), 1)

                def state(c):
                    st.sync()
                    dve.wait_ge(sem("state_mm"), v * 4 - 3 + c)
                    for h in halves:
                        ins = V.scalar_tensor_tensor(STT[h, h], BK[4][h, h], PC[h, c:c + 1], STP[h, h], ALU.mult, ALU.add)
                    ins.then_inc(sem("state"), 1)

                rhs(0)
                u(0)
                dve.wait_ge(sem("rhs_s_mm"), v)
                V.tensor_copy(RS[:], BK[2][0:NS, 0:P]).then_inc(sem("rhs_s"), 1)
                state(0)
                rhs(1)
                dve.wait_ge(sem("u_s_mm"), v)
                st.done(V.tensor_copy(US[:], BK[3][0:NS, 0:P]))
                req = spread(ms_req, 2, [NS, DB, HD])
                for e in range(2):
                    for dst, val in ((UM, US[:, e * HD:(e + 1) * HD]), (VM, TOKS[:, 2 * P + e * HD:2 * P + (e + 1) * HD])):
                        ins = V.tensor_tensor(dst[:, e, :].rearrange("p (b f) -> p b f", b=DB), spread(val, 1, [NS, DB, HD]),
                                              req, ALU.mult)
                ins.then_inc(sem("u_s"), 1)
                u(1)
                state(1)
                rhs(2)
                u(2)
                dve.wait_ge(sem("state_s_mm"), v)
                st.done(V.tensor_tensor(SIN[:], SIN[:], BK[2][:].rearrange("p (b f) -> p b f", b=DB), ALU.add))
                V.tensor_tensor(SIN[:], SIN[:], spread(PC[:, NCH:], 2, [P, DB, HD]), ALU.mult).then_inc(sem("state_s_done"), 1)
                state(2)
                rhs(3)
                u(3)
                state(3)
                dve.wait_ge(sem("state"), v * 5)
                V.tensor_copy(YS[:, 0:SEQ], BK[7][:, 0:SEQ])
                dve.wait_ge(sem("s0"), v)
                V.tensor_tensor(YS[:, SEQ:N], BK[7][:, SEQ:N], SPR[:, 1, :], ALU.add).then_inc(sem("y"), 1)
                if not last:
                    st.mark(mix_diff(columns(it + 1)))
                dve.wait_ge(sem("y"), v)
                dve.wait_ge(sem("y_mean"), v)
                V.scalar_tensor_tensor(YS[:], BK[5][:, 0:N], -1.0 / HD, YS[:], ALU.mult, ALU.add).then_inc(sem("y_centred"), 1)
                if not last:
                    st.sync()
                    dve.wait_ge(sem("prm"), it + 2)
                    mix_add(columns(it + 1), RKV, PRM).then_inc(sem("rkv"), 1)
                dve.wait_ge(sem("y_var"), v)
                V.tensor_scalar(YQ[:], BK[5][:, 0:N], 1.0 / HD, GN_EPS, ALU.mult, ALU.add).then_inc(sem("y_var_sb"), 1)
                if not last:
                    kk_max(it + 2)
                    decay_and_a(it + 2)
                    head(it + 1, it + 2)
                dve.wait_ge(sem("y_std"), v)
                st.done(V.reciprocal(YQ[:], YQ[:]))
                st.done(V.tensor_tensor(YS[:], YS[:], YQ[:], ALU.mult))
                st.done(V.tensor_scalar(YS[:], YS[:], PRM_LN[:, 0:1], PRM_LN[:, 1:2], ALU.mult, ALU.add))
                st.done(V.tensor_tensor(YS[:], YS[:], step(rwv[:, 1, bass.ds(it, 1), 0:N]), ALU.add))
                dve.wait_ge(sem("g_sb"), v)
                V.tensor_tensor(step(rwv[:, 0, bass.ds(it, 1), 0:N]), YS[:], step(rwv[:, 2, bass.ds(it, 1), 0:N]),
                                ALU.mult).then_inc(sem("pair_done"), 1)
            params(0)
            dve.wait_ge(sem("prm"), 1)
            mix(columns(0), RKV, PRM).then_inc(sem("rkv"), 1)
            kk_max(1)
            decay_and_a(1)
            head(0, 1)
            dve.wait_ge(sem("unit_out"), U_GATE)
            last_tokens(17, 24).then_inc(sem("shift_out"), 1)
            st.repeat(PAIRS - 1, PAIR_STEPS, pair)
            pair(PAIRS - 1, last=True)

            dve.wait_ge(sem("pair_done"), 1 + PAIRS)
            for i, (x, t) in enumerate(((8, T_Q), (0, 0))):
                dve.wait_ge(sem("o_hi"), i + 1)
                V.tensor_tensor(XN[:, 1, x:x + 8, :], COLS[:, t:t + 8, 0:N], XN[:, 0, x:x + 8, :].bitcast(F32),
                                ALU.subtract).then_inc(sem("o_split"), 1)
            dve.wait_ge(sem("w_split"), U_P + 2)
            xmv = XM[:].rearrange("p x (g j) n -> p x g j n", j=4)
            hv = H[:].rearrange("p (g j) n -> p g j n", j=4)
            def p_units(g):
                for j in range(4):
                    n = g * 4 + (U_P + j)
                    m1 = g * 4 + (j + 1)
                    b, s0 = 2 * (j % 2), 2 * (j % 2)
                    if isinstance(g, int):
                        ga, gb, hi, lo = GATES[:, j, :], GATES[:, KT + j, :], XM[:, 0, j, :], XM[:, 1, j, :]
                    else:
                        ga, gb = step(gatesv[:, bass.ds(g, 1), j, :]), step(gatesv[:, bass.ds(g + KT // 4, 1), j, :])
                        hi, lo = (step(xmv[:, x, bass.ds(g, 1), j, :]) for x in range(2))
                    dve.wait_ge(sem("unit_done"), n + 1)
                    if not (isinstance(g, int) and j < 2):
                        dve.wait_ge(sem("merged"), m1 - 2)
                    V.scalar_tensor_tensor(MG[:, s0, :], ga, 1.0, BK[b][:, 0:N], ALU.add, ALU.mult)
                    V.scalar_tensor_tensor(MG[:, s0 + 1, :], gb, 1.0, BK[b + 1][:, 0:N], ALU.add, ALU.mult).then_inc(sem("p_out"), 1)
                    dve.wait_ge(sem("p_out"), m1)
                    V.tensor_tensor(MG[:, s0, :], MG[:, s0, :], MG[:, s0 + 1, :], ALU.add).then_inc(sem("merge_sum"), 1)
                    split_lo(dve, n + 2, j % 2)
                    dve.wait_ge(sem("merge_hi"), m1)
                    V.scalar_tensor_tensor(lo, MG[:, s0, :], 0.5, hi.bitcast(F32), ALU.mult, ALU.subtract).then_inc(sem("merged"), 1)
            p_units(0)
            with dve.Fori(1, FORI_P) as g:
                p_units(g)

            def o_units(g):
                for j in range(4):
                    n = g * 4 + (U_O + j)
                    t = H[:, j, :] if isinstance(g, int) else step(hv[:, bass.ds(g, 1), j, :])
                    dve.wait_ge(sem("unit_done"), n + 1)
                    V.tensor_tensor(t, t, BK[j % 2][:, 0:N], ALU.add).then_inc(sem("h_sum"), 1)
                    split_lo(dve, n + 2, j % 2)
            dve.wait_ge(sem("h_in"), 16)
            o_units(0)
            with dve.Fori(1, FORI_P) as g:
                o_units(g)
            norm(1, HRSTD, H, HN, 1, True)
            dve.wait_ge(sem("h_spilled"), 16)
            dve.wait_ge(sem("x_split"), 8)
            V.memset(GX[:, :, 0:2], 0.0)
            dve.wait_ge(sem("cprev_in"), 16)
            dve.wait_ge(sem("convp_in"), 16)
            xfv = XF[:].rearrange("p x (g j) n -> p x g j n", j=2)
            cpv = CPREV[:].rearrange("p (g j) n -> p g j n", j=2)
            cov = COUT[:].rearrange("p (g j) n -> p g j n", j=2)
            cfv = CONVP[:].rearrange("p (g j) n -> p g j n", j=2)

            def up_pair(g, j):
                n = g * 4 + (U_UP + 2 * j)
                p1 = g * 2 + (j + 1)
                if isinstance(g, int):
                    prev, out, cf, hi, lo = CPREV[:, j, :], COUT[:, j, :], CONVP[:, j, :], XF[:, 0, j, :], XF[:, 1, j, :]
                else:
                    prev, out, cf = (step(x[:, bass.ds(g, 1), j, :]) for x in (cpv, cov, cfv))
                    hi, lo = (step(xfv[:, x, bass.ds(g, 1), j, :]) for x in range(2))
                gx = GX[:, j, :]
                hist = gx[:, 2 + SEQ:GE].rearrange("p (b f) -> p b f", f=6)
                st.done(V.tensor_copy(hist[:, :, 0:2], prev.rearrange("p (b f) -> p b f", f=2)))
                dve.wait_ge(sem("gate_out"), p1)
                c = CV[:, j, 0, :]
                st.done(V.tensor_scalar(c, gx[:, 0:CE], cf[:, 0:1], cf[:, 3:4], ALU.mult, ALU.add))
                st.done(V.scalar_tensor_tensor(c, gx[:, 1:1 + CE], cf[:, 1:2], c, ALU.mult, ALU.add))
                V.scalar_tensor_tensor(c, gx[:, 2:2 + CE], cf[:, 2:3], c, ALU.mult, ALU.add).then_inc(sem("conv_done"), 1)
                V.tensor_copy(out[:, 0:2], gx[:, SEQ:SEQ + 2])
                V.tensor_copy(out[:, 2:].rearrange("p (b f) -> p b f", f=2), hist[:, :, 4:6]).then_inc(sem("conv_used"), 1)
                split_lo(dve, n + 2, 0)
                dve.wait_ge(sem("silu"), p1)
                dve.wait_ge(sem("unit_done"), n + 2)
                s = CV[:, j, 1, :]
                V.tensor_tensor(c[:, 0:SEQ], s[:, 0:SEQ], BK[1][:, 0:SEQ], ALU.mult)
                V.tensor_tensor(by_request(c[:, SEQ:N]), samples(s[:, SEQ:CE], 6), by_request(BK[1][:, SEQ:N]),
                                ALU.mult).then_inc(sem("up_out"), 1)
                split_lo(dve, n + 3, 1)
                dve.wait_ge(sem("glu_hi"), p1)
                V.tensor_tensor(lo, c[:, 0:N], hi.bitcast(F32), ALU.subtract).then_inc(sem("act_split"), 1)
                dve.wait_ge(sem("act_split"), p1)
            up_pair(0, 0)
            up_pair(0, 1)
            st.repeat(FORI_UP, UP_STEPS, lambda g: (up_pair(g, 0), up_pair(g, 1)), first=1)

            dve.wait_ge(sem("h_back"), 16)
            h2v = H2[:].rearrange("p (g j) n -> p g j n", j=2)

            def down_units(g, count=2 * DU):
                for j in range(2 * DU):
                    n = g * (2 * DU) + (U_DOWN + j)
                    tile, q = divmod(j, DU)
                    if q == DU - 1:
                        dve.wait_ge(sem("unit_done"), n + 1)
                        t = H2[:, 2 * g + tile, :] if isinstance(g, int) else step(h2v[:, bass.ds(g, 1), tile, :])
                        V.tensor_tensor(t, t, BK[tile][:, 0:N], ALU.add).then_inc(sem("down_out"), 1)
                    if j < count:
                        split_lo(dve, n + 2, j % 2, DK)
            with dve.Fori(0, KT // 2 - 1) as g:
                down_units(g)
            down_units(KT // 2 - 1, 2 * DU - 2)
            norm(2, FRSTD, H2, YO, 2, False)


def units(w, tiles=None):
    k, n = w.shape
    return np.ascontiguousarray(w.reshape(k // P, P, n // P, P).transpose(2, 1, 0, 3)).reshape(n // P, P, k)


def tiles_of(v):
    return v.reshape(-1, P).T


def pad_cols(w, n):
    return np.concatenate([w, np.zeros((w.shape[0], n - w.shape[1]), w.dtype)], 1)


def rw_tiles(x):
    z = np.zeros(x.shape[:-1] + (32,), x.dtype)
    o = 3 * RW_WIDTH
    return np.concatenate([x[..., :o + 96], z, x[..., o + 96:o + 192], z, x[..., o + 192:]], -1)


OUTS = {"y": (P, KT, N), "k": (P, KVH, N), "v": (P, KVH, N), "ki": (ID, N), "wkv_p": (PAIRS, P, HD),
        "wkv_s": (PAIRS, P, DB, HD), "shift": (P, RW_T, 1 + DB), "conv": (P, FT, 2 + 2 * DB)}


def kernel(**inputs):
    import concourse.bacc as bacc
    from concourse.bass_utils import run_bass_kernel_spmd

    x = {k: np.asarray(v) for k, v in inputs.items()}
    w1 = {k: x[k][0] for k in x if k not in ("x_prompt", "x_sample", "page_table", "norm_f")}
    tokens = np.concatenate([x["x_prompt"][0], x["x_sample"].reshape(NS, D_MODEL)], 0)
    w_in = w1["w_in"]
    rw, att, gate = w_in[:, :RW_COLS], w_in[:, RW_COLS:-2 * D_MODEL], w_in[:, -2 * D_MODEL:]
    att_n = (AH + 2 * KVH) * HDIM
    qi = att[:, att_n:att_n + IH * ID]
    ki = att[:, att_n + IH * ID:att_n + IH * ID + ID]
    wi = att[:, att_n + IH * ID + ID:]
    rw = rw_tiles(rw)
    lw = rw[:, T_LW * P:(T_LW + 1) * P]
    rw = np.concatenate([rw[:, :T_LW * P], lw[:, :WI_ROW], wi, lw[:, WI_ROW + IH:], rw[:, (T_LW + 1) * P:]], 1)
    arr = {}
    arr["x"] = tokens.T.reshape(KT, P, N).transpose(1, 0, 2)
    arr["main_c"], arr["att_c"] = MAIN_C, ATT_C
    arr["w_in"] = np.roll(units(np.concatenate([rw, att[:, :att_n], qi, ki, ki], 1)), -FIRST_COLS, 0)
    arr["w_gate"] = units(gate)
    arr["w_p"] = np.concatenate([units(w1["p_rw"]), units(w1["p_att"])], 2)
    arr["w_o"] = units(w1["w_o"])
    up = units(w1["w_up"])
    arr["w_up"] = np.stack([up[:FT], up[FT:]], 1).reshape(2 * FT, P, D_MODEL)
    arr["w_down"] = units(w1["w_down"]).reshape(KT, P, DU, DK * P).transpose(0, 2, 1, 3).reshape(KT * DU, P, DK * P)
    arr["norms"] = np.stack([tiles_of(w1["norm1"]), tiles_of(w1["norm2"]), tiles_of(x["norm_f"])], 1)
    mu = tiles_of(rw_tiles(w1["rw_mu"]))
    prm = [mu[:, 0:8], mu[:, 8:16], mu[:, 16:24]] + [tiles_of(w1[k]) for k in (
        "rw_a0", "rw_k_k", "rw_k_a", "rw_r_k", "rw_lnx_w", "rw_lnx_b")]
    arr["pair_params"] = np.stack(prm, 2)
    arr["lora_mu"] = mu[:, T_LW:]
    lora = np.zeros((PAIRS, P, 3, P), np.float32)
    for i, (k, rows) in enumerate((("rw_w2", LORA_W), ("rw_a2", LORA_A), ("rw_g2", LORA_G))):
        lora[:, :rows, i, :] = w1[k].reshape(rows, PAIRS, P).transpose(1, 0, 2)
    lora[:, LORA_W, 0, :] = w1["rw_w0"].reshape(PAIRS, P)
    arr["lora"] = lora
    arr["shift_prev"] = rw_tiles(w1["state_shift"]).reshape(DB, RW_T, P).transpose(2, 1, 0)
    arr["state_s"] = w1["state_wkv"].reshape(DB, PAIRS, 2, HD, HD).transpose(1, 2, 4, 0, 3).reshape(PAIRS, P, DB, HD)
    arr["cache_k"] = w1["cache_k"].transpose(0, 2, 3, 1)
    arr["cache_v"] = w1["cache_v"].transpose(0, 2, 1, 3)
    arr["cache_kidx"] = w1["cache_kidx"].transpose(0, 2, 1)
    arr["page_table"] = x["page_table"].reshape(1, -1)
    arr["conv_params"] = np.stack([tiles_of(w1["conv_w"][0]), tiles_of(w1["conv_w"][1]), tiles_of(w1["conv_w"][2]),
                                   tiles_of(w1["conv_b"])], 2)
    arr["conv_prev"] = w1["state_conv"].reshape(2 * DB, FT, P).transpose(2, 1, 0)

    nc = bacc.Bacc("TRN2", target_bir_lowering=False, num_devices=1)
    arr = {f"in_{k}": np.ascontiguousarray(v) for k, v in arr.items()}
    a = {k[3:]: nc.dram_tensor(k, v.shape, mybir.dt.from_np(v.dtype), kind="ExternalInput").ap() for k, v in arr.items()}
    o = {k: nc.dram_tensor(f"out_{k}", shape, F32, kind="ExternalOutput").ap() for k, shape in OUTS.items()}
    build(nc, a, o)
    r = run_bass_kernel_spmd(nc, [arr], core_ids=[0]).results[0]
    r = {k: np.asarray(r[f"out_{k}"]) for k in OUTS}

    def tok(z):
        return z.transpose(2, 1, 0).reshape(z.shape[2], -1)

    y, k, v = tok(r["y"]), tok(r["k"]), tok(r["v"])
    ki = r["ki"].T
    pages = SEQ // PAGE
    sh = tok(r["shift"])
    o3 = 3 * RW_WIDTH
    sh = np.concatenate([sh[:, :o3 + 96], sh[:, o3 + 128:o3 + 224], sh[:, o3 + 256:]], 1)
    cv = tok(r["conv"])
    wp = r["wkv_p"].reshape(HEADS_RW, HD, HD).transpose(0, 2, 1)
    ws = r["wkv_s"].reshape(PAIRS, 2, HD, DB, HD).transpose(3, 0, 1, 4, 2).reshape(DB, HEADS_RW, HD, HD)
    c = np.ascontiguousarray
    return (c(y[:SEQ][None]), c(y[SEQ:].reshape(DB, DS, D_MODEL)),
            c(k[:SEQ].reshape(1, 1, pages, PAGE, KVH, HDIM)), c(v[:SEQ].reshape(1, 1, pages, PAGE, KVH, HDIM)),
            c(ki[:SEQ].reshape(1, 1, pages, PAGE, ID)), c(k[SEQ:].reshape(1, DB, DS, KVH, HDIM)),
            c(v[SEQ:].reshape(1, DB, DS, KVH, HDIM)), c(ki[SEQ:].reshape(1, DB, DS, ID)),
            c(wp[None, None]), c(ws[None]), c(sh[:1][None]), c(sh[1:][None]),
            c(cv[:2].reshape(1, 1, 2, D_FF)), c(cv[2:].reshape(1, DB, 2, D_FF)))
```
